# Optimizing a Trainium2 kernel written in Bass

```python
import jax
import jax.numpy as jnp
from jax import lax
import numpy as np
import jax, jax.numpy as jnp

D_MODEL = 1024
BATCH = 1
SEQ = 512
DEPTH = 1

HEAD_DIM = 64
MIX_WIDTH = D_MODEL
NSA_HEADS = MIX_WIDTH // 2 // HEAD_DIM
NSA_KV_HEADS = 2
SWA_HEADS = MIX_WIDTH // 2 // HEAD_DIM
SWA_KV_HEADS = 2
CMP_BLOCK = 32
CMP_STRIDE = 16
CMP_HIDDEN = 256
SEL_BLOCK = 64
SEL_TOPK = 16
SEL_Q_CHUNK = 64
NSA_WINDOW = 512
SWA_WINDOW = 128
BAND_BLOCK = 128
N_NSA_BRANCHES = 3
D_FF = 2816
NORM_EPS = 1e-6
NEG_INF = -1e30
FORCE_SCORE = 1e9
ATTN_SCALE = HEAD_DIM ** -0.5
PROJ_SPLITS = (NSA_HEADS * HEAD_DIM, 2 * N_NSA_BRANCHES * NSA_KV_HEADS * HEAD_DIM, N_NSA_BRANCHES * NSA_HEADS, SWA_HEADS * HEAD_DIM, 2 * SWA_KV_HEADS * HEAD_DIM)
PROJ_WIDTH = sum(PROJ_SPLITS)


def alibi_slopes(n_heads, n_groups):
    slopes = 2.0 ** (-8.0 * np.arange(1, n_heads + 1) / n_heads)
    return jnp.asarray(slopes.reshape(n_groups, n_heads // n_groups), jnp.float32)

def rmsnorm(x, g):
    xf = x.astype(jnp.float32)
    y = xf * lax.rsqrt(jnp.mean(xf * xf, axis=-1, keepdims=True) + NORM_EPS)
    return (y * g.astype(jnp.float32)).astype(x.dtype)

def swiglu(x, w_in, w_out):
    gate, up = jnp.split(x @ w_in, 2, axis=-1)
    return (jax.nn.silu(gate) * up) @ w_out

def banded_attention(q, k, v, slopes, window, sinks=None):
    B, T, G, R, D = q.shape
    nb = T // BAND_BLOCK
    n_prev = -(-(window - 1) // BAND_BLOCK)
    pad = n_prev * BAND_BLOCK
    kw_len = (n_prev + 1) * BAND_BLOCK
    kp = jnp.pad(k, ((0, 0), (pad, 0), (0, 0), (0, 0))).reshape(B, nb + n_prev, BAND_BLOCK, G, D)
    vp = jnp.pad(v, ((0, 0), (pad, 0), (0, 0), (0, 0))).reshape(B, nb + n_prev, BAND_BLOCK, G, D)
    kw = jnp.concatenate([kp[:, j:j + nb] for j in range(n_prev + 1)], axis=2)
    vw = jnp.concatenate([vp[:, j:j + nb] for j in range(n_prev + 1)], axis=2)
    qb = q.reshape(B, nb, BAND_BLOCK, G, R, D)
    s = jnp.einsum('bnqgrd,bnkgd->bngrqk', qb, kw) * ATTN_SCALE
    t_pos = np.arange(nb)[:, None] * BAND_BLOCK + np.arange(BAND_BLOCK)[None, :]
    s_pos = np.arange(nb)[:, None] * BAND_BLOCK - pad + np.arange(kw_len)[None, :]
    dist = t_pos[:, :, None] - s_pos[:, None, :]
    mask = jnp.asarray((dist >= 0) & (dist < window) & (s_pos[:, None, :] >= 0))
    bias = -slopes[None, :, :, None, None] * jnp.asarray(dist, jnp.float32)[:, None, None]
    s = jnp.where(mask[:, None, None], s + bias, NEG_INF)
    if sinks is not None:
        sink = jnp.broadcast_to(sinks[None, None, :, :, None, None], s.shape[:-1] + (1,))
        p = jax.nn.softmax(jnp.concatenate([s, sink], axis=-1), axis=-1)[..., :-1]
    else:
        p = jax.nn.softmax(s, axis=-1)
    o = jnp.einsum('bngrqk,bnkgd->bnqgrd', p, vw)
    return o.reshape(B, T, G, R, D)

def compress_blocks(kr, pos, w1, b1, w2):
    B, T, G, D = kr.shape
    nc = (T - CMP_BLOCK) // CMP_STRIDE + 1
    idx = np.arange(nc)[:, None] * CMP_STRIDE + np.arange(CMP_BLOCK)[None, :]
    blk = kr[:, idx] + pos[None, None, :, None, :]
    flat = blk.transpose(0, 1, 3, 2, 4).reshape(B, nc, G, CMP_BLOCK * D)
    return jax.nn.gelu(flat @ w1 + b1) @ w2

def selected_attention(q, k, v, sel_idx, slopes):
    B, T, G, R, D = q.shape
    ns = T // SEL_BLOCK
    n_sel = sel_idx.shape[-1]
    nq = T // SEL_Q_CHUNK
    kb = k.reshape(B, ns, SEL_BLOCK, G, D).transpose(0, 3, 1, 2, 4)
    vb = v.reshape(B, ns, SEL_BLOCK, G, D).transpose(0, 3, 1, 2, 4)
    qc = q.reshape(B, nq, SEL_Q_CHUNK, G, R, D).transpose(1, 0, 2, 3, 4, 5)
    ic = sel_idx.reshape(B, nq, SEL_Q_CHUNK, G, n_sel).transpose(1, 0, 2, 3, 4)
    tc = jnp.arange(T).reshape(nq, SEL_Q_CHUNK)
    b_ix = jnp.arange(B)[:, None, None, None]
    g_ix = jnp.arange(G)[None, None, :, None]

    def chunk(args):
        qx, ix, tx = args
        kg = kb[b_ix, g_ix, ix]
        vg = vb[b_ix, g_ix, ix]
        s = jnp.einsum('bcgrd,bcgkld->bcgrkl', qx, kg) * ATTN_SCALE
        spos = ix[..., None] * SEL_BLOCK + jnp.arange(SEL_BLOCK)
        dist = tx[None, :, None, None, None] - spos
        mask = (dist >= 0)[:, :, :, None]
        bias = -slopes[None, None, :, :, None, None] * dist.astype(jnp.float32)[:, :, :, None]
        s = jnp.where(mask, s + bias, NEG_INF)
        C = qx.shape[1]
        p = jax.nn.softmax(s.reshape(B, C, G, R, n_sel * SEL_BLOCK), axis=-1).reshape(s.shape)
        return jnp.einsum('bcgrkl,bcgkld->bcgrd', p, vg)

    o = lax.map(chunk, (qc, ic, tc))
    return o.transpose(1, 0, 2, 3, 4, 5).reshape(B, T, G, R, D)

def nsa_group(q, kc_raw, vc_raw, ks, vs, kw, vw, gate_logits, ck_pos, ck_w1, ck_b1, ck_w2, cv_pos, cv_w1, cv_b1, cv_w2, slopes):
    B, T, G, R, D = q.shape
    kc = compress_blocks(kc_raw, ck_pos, ck_w1, ck_b1, ck_w2).astype(jnp.float32)
    vc = compress_blocks(vc_raw, cv_pos, cv_w1, cv_b1, cv_w2).astype(jnp.float32)
    nc = kc.shape[1]
    blk_end = np.arange(nc) * CMP_STRIDE + CMP_BLOCK - 1
    dist_c = np.arange(T)[:, None] - blk_end[None, :]
    mask_c = jnp.asarray(dist_c >= 0)
    s = jnp.einsum('btgrd,bcgd->bgrtc', q, kc) * ATTN_SCALE
    s = jnp.where(mask_c, s - slopes[:, :, None, None] * jnp.asarray(dist_c, jnp.float32), NEG_INF)
    p_cmp = jnp.where(mask_c, jax.nn.softmax(s, axis=-1), 0.0)
    o_cmp = jnp.einsum('bgrtc,bcgd->btgrd', p_cmp, vc)
    ns = T // SEL_BLOCK
    c_start = np.arange(nc) * CMP_STRIDE
    s_start = np.arange(ns) * SEL_BLOCK
    overlap = np.clip(np.minimum(c_start[:, None] + CMP_BLOCK, s_start[None, :] + SEL_BLOCK) - np.maximum(c_start[:, None], s_start[None, :]), 0, None) / CMP_BLOCK
    p_slc = jnp.einsum('bgrtc,cs->btgs', p_cmp, jnp.asarray(overlap, jnp.float32))
    cur = np.arange(T) // SEL_BLOCK
    blk = np.arange(ns)
    valid = jnp.asarray(blk[None, :] <= cur[:, None])[None, :, None, :]
    forced = jnp.asarray((blk[None, :] == 0) | (blk[None, :] == cur[:, None]) | (blk[None, :] == cur[:, None] - 1))[None, :, None, :]
    score = jnp.where(forced, FORCE_SCORE, jnp.where(valid, p_slc, NEG_INF))
    _, sel_idx = lax.top_k(score, min(SEL_TOPK, ns))
    o_slc = selected_attention(q, ks, vs, sel_idx, slopes)
    o_win = banded_attention(q, kw, vw, slopes, NSA_WINDOW)
    g = jax.nn.sigmoid(gate_logits)
    return g[..., 0:1] * o_cmp + g[..., 1:2] * o_slc + g[..., 2:3] * o_win

def hybrid_mixer(xn, w_in, ck_pos, ck_w1, ck_b1, ck_w2, cv_pos, cv_w1, cv_b1, cv_w2, sinks, w_out):
    B, T, _ = xn.shape
    D = HEAD_DIM
    ga, ra = NSA_KV_HEADS, NSA_HEADS // NSA_KV_HEADS
    gb, rb = SWA_KV_HEADS, SWA_HEADS // SWA_KV_HEADS
    proj = (xn @ w_in).astype(jnp.float32)
    offsets = [int(o) for o in np.cumsum(PROJ_SPLITS)[:-1]]
    q_a, kv_a, gate_a, q_b, kv_b = jnp.split(proj, offsets, axis=-1)
    q_a = q_a.reshape(B, T, ga, ra, D)
    kc_raw, vc_raw, ks, vs, kw, vw = [t.reshape(B, T, ga, D) for t in jnp.split(kv_a, 2 * N_NSA_BRANCHES, axis=-1)]
    gate_a = gate_a.reshape(B, T, ga, ra, N_NSA_BRANCHES)
    o_a = nsa_group(q_a, kc_raw, vc_raw, ks, vs, kw, vw, gate_a, ck_pos, ck_w1, ck_b1, ck_w2, cv_pos, cv_w1, cv_b1, cv_w2, alibi_slopes(NSA_HEADS, NSA_KV_HEADS))
    q_b = q_b.reshape(B, T, gb, rb, D)
    k_b, v_b = [t.reshape(B, T, gb, D) for t in jnp.split(kv_b, 2, axis=-1)]
    o_b = banded_attention(q_b, k_b, v_b, alibi_slopes(SWA_HEADS, SWA_KV_HEADS), SWA_WINDOW, sinks.astype(jnp.float32).reshape(gb, rb))
    o = jnp.concatenate([o_a.reshape(B, T, NSA_HEADS * D), o_b.reshape(B, T, SWA_HEADS * D)], axis=-1)
    return o.astype(xn.dtype) @ w_out

def first_inputs(seed: int = 0) -> dict:
    key = jax.random.key(seed)
    ks = jax.random.split(key, 24)
    L = DEPTH

    def nrm(k, shape, fan_in):
        return jax.random.normal(k, shape, jnp.float32) * fan_in ** -0.5

    def gain(k, shape):
        return 1.0 + 0.1 * jax.random.normal(k, shape, jnp.float32)

    return {
        'x': jax.random.normal(ks[0], (BATCH, SEQ, D_MODEL), jnp.float32),
        'ffn1_norm': gain(ks[1], (L, D_MODEL)),
        'ffn1_w_in': nrm(ks[2], (L, D_MODEL, 2 * D_FF), D_MODEL),
        'ffn1_w_out': nrm(ks[3], (L, D_FF, D_MODEL), D_FF),
        'mix_norm': gain(ks[4], (L, D_MODEL)),
        'w_mix_in': nrm(ks[5], (L, D_MODEL, PROJ_WIDTH), D_MODEL),
        'cmp_k_pos': 0.5 * jax.random.normal(ks[6], (L, CMP_BLOCK, HEAD_DIM), jnp.float32),
        'cmp_k_w1': nrm(ks[7], (L, CMP_BLOCK * HEAD_DIM, CMP_HIDDEN), CMP_BLOCK * HEAD_DIM),
        'cmp_k_b1': 0.02 * jax.random.normal(ks[8], (L, CMP_HIDDEN), jnp.float32),
        'cmp_k_w2': nrm(ks[9], (L, CMP_HIDDEN, HEAD_DIM), CMP_HIDDEN),
        'cmp_v_pos': 0.5 * jax.random.normal(ks[10], (L, CMP_BLOCK, HEAD_DIM), jnp.float32),
        'cmp_v_w1': nrm(ks[11], (L, CMP_BLOCK * HEAD_DIM, CMP_HIDDEN), CMP_BLOCK * HEAD_DIM),
        'cmp_v_b1': 0.02 * jax.random.normal(ks[12], (L, CMP_HIDDEN), jnp.float32),
        'cmp_v_w2': nrm(ks[13], (L, CMP_HIDDEN, HEAD_DIM), CMP_HIDDEN),
        'swa_sinks': 0.5 * jax.random.normal(ks[14], (L, SWA_HEADS), jnp.float32),
        'w_mix_out': nrm(ks[15], (L, MIX_WIDTH, D_MODEL), MIX_WIDTH),
        'ffn2_norm': gain(ks[16], (L, D_MODEL)),
        'ffn2_w_in': nrm(ks[17], (L, D_MODEL, 2 * D_FF), D_MODEL),
        'ffn2_w_out': nrm(ks[18], (L, D_FF, D_MODEL), D_FF),
        'final_norm': gain(ks[19], (D_MODEL,)),
    }

def first_block(x, ffn1_norm, ffn1_w_in, ffn1_w_out, mix_norm, w_mix_in, cmp_k_pos, cmp_k_w1, cmp_k_b1, cmp_k_w2, cmp_v_pos, cmp_v_w1, cmp_v_b1, cmp_v_w2, swa_sinks, w_mix_out, ffn2_norm, ffn2_w_in, ffn2_w_out, final_norm):
    h = x
    for l in range(DEPTH):
        h = h + 0.5 * swiglu(rmsnorm(h, ffn1_norm[l]), ffn1_w_in[l], ffn1_w_out[l])
        h = h + hybrid_mixer(rmsnorm(h, mix_norm[l]), w_mix_in[l], cmp_k_pos[l], cmp_k_w1[l], cmp_k_b1[l], cmp_k_w2[l], cmp_v_pos[l], cmp_v_w1[l], cmp_v_b1[l], cmp_v_w2[l], swa_sinks[l], w_mix_out[l])
        h = h + 0.5 * swiglu(rmsnorm(h, ffn2_norm[l]), ffn2_w_in[l], ffn2_w_out[l])
    return rmsnorm(h, final_norm)


DEPTH_2 = 2

CHUNK = 64
LEFT_CHUNKS = 8
BAND_CHUNKS = LEFT_CHUNKS + 1
BAND = BAND_CHUNKS * CHUNK
MIX_WIDTH_2 = D_MODEL
RWKV_WIDTH = MIX_WIDTH_2 // 2
ATT_WIDTH = MIX_WIDTH_2 - RWKV_WIDTH
RWKV_HEADS = RWKV_WIDTH // HEAD_DIM
ATT_HEADS = ATT_WIDTH // HEAD_DIM
DECAY_LORA = 64
AAA_LORA = 64
GATE_LORA = 128
RWKV_COLS = 3 * RWKV_WIDTH + DECAY_LORA + AAA_LORA + GATE_LORA
IN_COLS = RWKV_COLS + 3 * ATT_WIDTH
MAX_REL = 2 * CHUNK
CONV_WIDTH = 31
D_FF_2 = 4 * D_MODEL
LN_EPS = 1e-5
GN_EPS = 64e-5


def rmsnorm_2(x, g):
    x32 = x.astype(jnp.float32)
    y = x32 * lax.rsqrt(jnp.mean(x32 * x32, axis=-1, keepdims=True) + NORM_EPS)
    return (y * g.astype(jnp.float32)).astype(x.dtype)

def token_shift(p):
    return jnp.pad(p, ((0, 0), (1, 0), (0, 0)))[:, :-1]

def rwkv7_scan(r, decay, k, v, kk, a):
    B, T, H, N = r.shape
    def step(S, inp):
        r_t, w_t, k_t, v_t, kk_t, a_t = inp
        sa = jnp.einsum('bhij,bhj->bhi', S, -kk_t)
        S = (S * w_t[:, :, None, :]
             + sa[..., None] * (kk_t * a_t)[:, :, None, :]
             + v_t[..., None] * k_t[:, :, None, :])
        y = jnp.einsum('bhij,bhj->bhi', S, r_t)
        return S, y
    xs = tuple(jnp.moveaxis(z.astype(jnp.float32), 1, 0) for z in (r, decay, k, v, kk, a))
    S0 = jnp.zeros((B, H, N, N), jnp.float32)
    _, ys = lax.scan(step, S0, xs)
    return jnp.moveaxis(ys, 0, 1)

def rwkv7_group(p, mu, w0, w2, a0, a2, g2, k_k, k_a, r_k, lnx_w, lnx_b):
    B, T, _ = p.shape
    p = p + (token_shift(p) - p) * mu
    split_at = [RWKV_WIDTH, 2 * RWKV_WIDTH, 3 * RWKV_WIDTH,
                3 * RWKV_WIDTH + DECAY_LORA, 3 * RWKV_WIDTH + DECAY_LORA + AAA_LORA]
    r, k, v, xw, xa, xg = jnp.split(p, split_at, axis=-1)
    w = -jax.nn.softplus(-(w0 + jnp.tanh(xw) @ w2)) - 0.5
    decay = jnp.exp(-jnp.exp(w.astype(jnp.float32)))
    a = jax.nn.sigmoid(a0 + xa @ a2)
    g = jax.nn.sigmoid(xg) @ g2
    heads = lambda z: z.reshape(B, T, RWKV_HEADS, HEAD_DIM)
    kk = heads(k * k_k).astype(jnp.float32)
    kk = kk / jnp.maximum(jnp.sqrt(jnp.sum(kk * kk, axis=-1, keepdims=True)), 1e-12)
    k = k * (1 + (a - 1) * k_a)
    rh, kh, vh, ah = heads(r), heads(k), heads(v), heads(a)
    y = rwkv7_scan(rh, heads(decay), kh, vh, kk, ah)
    mean = jnp.mean(y, axis=-1, keepdims=True)
    var = jnp.mean(jnp.square(y - mean), axis=-1, keepdims=True)
    y = (y - mean) * lax.rsqrt(var + GN_EPS)
    y = y * lnx_w.reshape(RWKV_HEADS, HEAD_DIM).astype(jnp.float32) + lnx_b.reshape(RWKV_HEADS, HEAD_DIM).astype(jnp.float32)
    bonus = jnp.sum((rh * kh * r_k.reshape(RWKV_HEADS, HEAD_DIM)).astype(jnp.float32), axis=-1, keepdims=True) * vh.astype(jnp.float32)
    y = (y + bonus).reshape(B, T, RWKV_WIDTH).astype(p.dtype)
    return y * g

def chunk_band_attention(q, k, v, rel_bias):
    B, T, _ = q.shape
    nc = T // CHUNK
    shp = (B, nc, CHUNK, ATT_HEADS, HEAD_DIM)
    qc, kc, vc = q.reshape(shp), k.reshape(shp), v.reshape(shp)
    pad = ((0, 0), (LEFT_CHUNKS, 0), (0, 0), (0, 0), (0, 0))
    band_idx = jnp.arange(nc)[:, None] + jnp.arange(BAND_CHUNKS)[None, :]
    kb = jnp.pad(kc, pad)[:, band_idx].reshape(B, nc, BAND, ATT_HEADS, HEAD_DIM)
    vb = jnp.pad(vc, pad)[:, band_idx].reshape(B, nc, BAND, ATT_HEADS, HEAD_DIM)
    valid = jnp.repeat(band_idx >= LEFT_CHUNKS, CHUNK, axis=1)
    rel = jnp.arange(CHUNK)[:, None] + LEFT_CHUNKS * CHUNK - jnp.arange(BAND)[None, :]
    bias = rel_bias[:, jnp.clip(rel, -MAX_REL, MAX_REL) + MAX_REL]
    s = jnp.einsum('bcqhd,bckhd->bhcqk', qc, kb).astype(jnp.float32) * (HEAD_DIM ** -0.5)
    s = s + bias[:, None].astype(jnp.float32)
    s = jnp.where(valid[:, None, :], s, -1e30)
    probs = jax.nn.softmax(s, axis=-1).astype(v.dtype)
    o = jnp.einsum('bhcqk,bckhd->bcqhd', probs, vb)
    return o.reshape(B, T, ATT_WIDTH)

def rwkv_attention_mixer(h, w_in, mu, w0, w2, a0, a2, g2, k_k, k_a, r_k, lnx_w, lnx_b, rel_bias, w_out):
    proj = h @ w_in
    p_rwkv, q, k, v = jnp.split(proj, [RWKV_COLS, RWKV_COLS + ATT_WIDTH, RWKV_COLS + 2 * ATT_WIDTH], axis=-1)
    y_rwkv = rwkv7_group(p_rwkv, mu, w0, w2, a0, a2, g2, k_k, k_a, r_k, lnx_w, lnx_b)
    y_att = chunk_band_attention(q, k, v, rel_bias)
    return jnp.concatenate([y_rwkv, y_att], axis=-1) @ w_out

def conformer_conv(h, pw1, pw1_b, dw, dw_b, ln_w, ln_b, pw2, pw2_b):
    u = jax.nn.glu(h @ pw1 + pw1_b, axis=-1)
    u = lax.conv_general_dilated(u, dw[:, None, :].astype(u.dtype), (1,), [(CONV_WIDTH - 1, 0)],
                                 dimension_numbers=('NWC', 'WIO', 'NWC'),
                                 feature_group_count=D_MODEL) + dw_b
    u32 = u.astype(jnp.float32)
    mean = jnp.mean(u32, axis=-1, keepdims=True)
    var = jnp.mean(jnp.square(u32 - mean), axis=-1, keepdims=True)
    u = ((u32 - mean) * lax.rsqrt(var + LN_EPS) * ln_w.astype(jnp.float32) + ln_b.astype(jnp.float32)).astype(h.dtype)
    return jax.nn.silu(u) @ pw2 + pw2_b

def sq_relu_mlp(h, up, down):
    return jnp.square(jax.nn.relu(h @ up)) @ down

def second_inputs(seed: int = 0) -> dict:
    key = jax.random.key(seed)
    ks = jax.random.split(key, 40)
    nrm = lambda i, shape, scale: jax.random.normal(ks[i], shape, jnp.float32) * scale
    gain = lambda i, n: 1.0 + 0.05 * jax.random.normal(ks[i], (n,), jnp.float32)
    return {
        "x": nrm(0, (BATCH, SEQ, D_MODEL), 1.0),
        "l0_norm_mix": gain(1, D_MODEL),
        "l0_w_in": nrm(2, (D_MODEL, IN_COLS), D_MODEL ** -0.5),
        "l0_shift_mu": jax.random.uniform(ks[3], (RWKV_COLS,), jnp.float32),
        "l0_w0": jax.random.uniform(ks[4], (RWKV_WIDTH,), jnp.float32, -6.0, 1.0),
        "l0_w2": nrm(5, (DECAY_LORA, RWKV_WIDTH), DECAY_LORA ** -0.5),
        "l0_a0": nrm(6, (RWKV_WIDTH,), 0.1),
        "l0_a2": nrm(7, (AAA_LORA, RWKV_WIDTH), AAA_LORA ** -0.5),
        "l0_g2": nrm(8, (GATE_LORA, RWKV_WIDTH), GATE_LORA ** -0.5),
        "l0_k_k": 0.85 + nrm(9, (RWKV_WIDTH,), 0.05),
        "l0_k_a": 1.0 + nrm(10, (RWKV_WIDTH,), 0.05),
        "l0_r_k": nrm(11, (RWKV_WIDTH,), 0.1),
        "l0_lnx_w": gain(12, RWKV_WIDTH),
        "l0_lnx_b": nrm(13, (RWKV_WIDTH,), 0.02),
        "l0_rel_bias": nrm(14, (ATT_HEADS, 2 * MAX_REL + 1), 0.5),
        "l0_w_out": nrm(15, (MIX_WIDTH_2, D_MODEL), MIX_WIDTH_2 ** -0.5),
        "l0_norm_ffn": gain(16, D_MODEL),
        "l0_ffn_up": nrm(17, (D_MODEL, D_FF_2), D_MODEL ** -0.5),
        "l0_ffn_down": nrm(18, (D_FF_2, D_MODEL), D_FF_2 ** -0.5),
        "l1_norm_mix": gain(19, D_MODEL),
        "l1_pw1": nrm(20, (D_MODEL, 2 * D_MODEL), D_MODEL ** -0.5),
        "l1_pw1_b": nrm(21, (2 * D_MODEL,), 0.02),
        "l1_dw": nrm(22, (CONV_WIDTH, D_MODEL), CONV_WIDTH ** -0.5),
        "l1_dw_b": nrm(23, (D_MODEL,), 0.02),
        "l1_ln_w": gain(24, D_MODEL),
        "l1_ln_b": nrm(25, (D_MODEL,), 0.02),
        "l1_pw2": nrm(26, (D_MODEL, D_MODEL), D_MODEL ** -0.5),
        "l1_pw2_b": nrm(27, (D_MODEL,), 0.02),
        "l1_norm_ffn": gain(28, D_MODEL),
        "l1_ffn_up": nrm(29, (D_MODEL, D_FF_2), D_MODEL ** -0.5),
        "l1_ffn_down": nrm(30, (D_FF_2, D_MODEL), D_FF_2 ** -0.5),
        "final_norm": gain(31, D_MODEL),
    }

def second_block(x, l0_norm_mix, l0_w_in, l0_shift_mu, l0_w0, l0_w2, l0_a0, l0_a2, l0_g2,
              l0_k_k, l0_k_a, l0_r_k, l0_lnx_w, l0_lnx_b, l0_rel_bias, l0_w_out,
              l0_norm_ffn, l0_ffn_up, l0_ffn_down,
              l1_norm_mix, l1_pw1, l1_pw1_b, l1_dw, l1_dw_b, l1_ln_w, l1_ln_b,
              l1_pw2, l1_pw2_b, l1_norm_ffn, l1_ffn_up, l1_ffn_down, final_norm):
    mix_norms = (l0_norm_mix, l1_norm_mix)
    mix_params = (
        (l0_w_in, l0_shift_mu, l0_w0, l0_w2, l0_a0, l0_a2, l0_g2, l0_k_k, l0_k_a,
         l0_r_k, l0_lnx_w, l0_lnx_b, l0_rel_bias, l0_w_out),
        (l1_pw1, l1_pw1_b, l1_dw, l1_dw_b, l1_ln_w, l1_ln_b, l1_pw2, l1_pw2_b),
    )
    ffn_params = ((l0_norm_ffn, l0_ffn_up, l0_ffn_down), (l1_norm_ffn, l1_ffn_up, l1_ffn_down))
    for layer in range(DEPTH_2):
        h = rmsnorm_2(x, mix_norms[layer])
        if layer % 2 == 0:
            x = x + rwkv_attention_mixer(h, *mix_params[layer])
        else:
            x = x + conformer_conv(h, *mix_params[layer])
        g_ffn, up, down = ffn_params[layer]
        x = x + sq_relu_mlp(rmsnorm_2(x, g_ffn), up, down)
    return rmsnorm_2(x, final_norm)


def setup_inputs(seed=0):
    out = dict(first_inputs(seed))
    for name, value in second_inputs(seed + 1).items():
        if name != "x":
            out[name + "_2"] = value
    return out


def reference(
    x, ffn1_norm, ffn1_w_in, ffn1_w_out, mix_norm, w_mix_in, cmp_k_pos, cmp_k_w1, cmp_k_b1,
    cmp_k_w2, cmp_v_pos, cmp_v_w1, cmp_v_b1, cmp_v_w2, swa_sinks, w_mix_out, ffn2_norm,
    ffn2_w_in, ffn2_w_out, final_norm, l0_norm_mix_2, l0_w_in_2, l0_shift_mu_2, l0_w0_2,
    l0_w2_2, l0_a0_2, l0_a2_2, l0_g2_2, l0_k_k_2, l0_k_a_2, l0_r_k_2, l0_lnx_w_2, l0_lnx_b_2,
    l0_rel_bias_2, l0_w_out_2, l0_norm_ffn_2, l0_ffn_up_2, l0_ffn_down_2, l1_norm_mix_2,
    l1_pw1_2, l1_pw1_b_2, l1_dw_2, l1_dw_b_2, l1_ln_w_2, l1_ln_b_2, l1_pw2_2, l1_pw2_b_2,
    l1_norm_ffn_2, l1_ffn_up_2, l1_ffn_down_2, final_norm_2,
):
    x = first_block(
        x, ffn1_norm, ffn1_w_in, ffn1_w_out, mix_norm, w_mix_in, cmp_k_pos, cmp_k_w1, cmp_k_b1,
        cmp_k_w2, cmp_v_pos, cmp_v_w1, cmp_v_b1, cmp_v_w2, swa_sinks, w_mix_out, ffn2_norm,
        ffn2_w_in, ffn2_w_out, final_norm,
    )
    return second_block(
        x, l0_norm_mix_2, l0_w_in_2, l0_shift_mu_2, l0_w0_2, l0_w2_2, l0_a0_2, l0_a2_2, l0_g2_2,
        l0_k_k_2, l0_k_a_2, l0_r_k_2, l0_lnx_w_2, l0_lnx_b_2, l0_rel_bias_2, l0_w_out_2,
        l0_norm_ffn_2, l0_ffn_up_2, l0_ffn_down_2, l1_norm_mix_2, l1_pw1_2, l1_pw1_b_2, l1_dw_2,
        l1_dw_b_2, l1_ln_w_2, l1_ln_b_2, l1_pw2_2, l1_pw2_b_2, l1_norm_ffn_2, l1_ffn_up_2,
        l1_ffn_down_2, final_norm_2,
    )


_drawn_inputs = setup_inputs


def setup_inputs(seed=0):
    import zlib

    import numpy as np

    out = dict(_drawn_inputs(seed))
    spreads = {}
    factors = {'cmp_k_pos': 3.849,
     'cmp_k_b1': 64.0,
     'cmp_v_b1': 8.0,
     'swa_sinks': 2.908,
     'l0_a0_2': 3.654,
     'l0_k_k_2': 11.519,
     'l0_lnx_b_2': 6.613,
     'l1_pw1_b_2': 7.057,
     'l1_dw_b_2': 3.859,
     'l1_ln_b_2': 7.562,
     'l1_pw2_b_2': 4.779}
    for name, (base, spread) in spreads.items():
        noise = np.random.default_rng([zlib.crc32(name.encode()), seed]).standard_normal(out[name].shape)
        drawn = base * np.exp(spread * noise) if base else spread * noise
        out[name] = jnp.asarray(drawn.astype(out[name].dtype))
    for name, factor in factors.items():
        out[name] = (out[name] * factor).astype(out[name].dtype)
    return out
```

```python
from contextlib import ExitStack

import numpy as np
import concourse.bass as bass
from concourse import mybir

F32 = mybir.dt.float32
F32R = mybir.dt.float32r
BF16 = mybir.dt.bfloat16
ALU = mybir.AluOpType
ACT = mybir.ActivationFunctionType
AX = mybir.AxisListType

P = 128
T = 512
D = 1024
KD = D // P
TT = T // P
HD = 64
KU = 8
RING = 4
F1 = 2816 // P
F1A = 16
F2 = 4096 // P
EPS = 1e-6
LN_EPS = 1e-5

START = RING


def stream_plan():
    at, base = 0, {}
    for name, n in (
        ("ffn1_upA", 2 * F1A), ("ffn1_downA", KD * 2), ("ffn1_upB", 2 * (F1 - F1A)), ("ffn1_downB", KD),
        ("mix_in", 25), ("mix_out", KD),
        ("ffn2_upA", 2 * F1A), ("ffn2_downA", KD * 2), ("ffn2_upB", 2 * (F1 - F1A)), ("ffn2_downB", KD),
        ("rwkv_in", 26), ("rwkv_out", KD),
        ("mlp0_upA", 16), ("mlp0_downA", KD * 2), ("mlp0_upB", 16), ("mlp0_downB", KD * 2),
        ("pw1", 16), ("pw2", KD),
        ("mlp1_upA", 16), ("mlp1_downA", KD * 2), ("mlp1_upB", 16), ("mlp1_downB", KD * 2),
    ):
        base[name] = at
        at += n
    base["end"] = at
    return base


BASE = stream_plan()
UNITS = BASE["end"]

VECTORS = (
    ("ffn1_norm", 8), ("mix_norm", 8), ("ffn2_norm", 8), ("final_norm", 8),
    ("l0_norm_mix_2", 8), ("l0_norm_ffn_2", 8), ("l1_norm_mix_2", 8), ("l1_norm_ffn_2", 8),
    ("final_norm_2", 8), ("l0_shift_mu_2", 14), ("l0_w0_2", 4), ("l0_a0_2", 4), ("l0_k_k_2", 4),
    ("l0_k_a_2", 4), ("l0_r_k_2", 4), ("l0_lnx_w_2", 4), ("l0_lnx_b_2", 4), ("l1_pw1_b_2", 16),
    ("l1_dw_b_2", 8), ("l1_ln_w_2", 8), ("l1_ln_b_2", 8), ("l1_pw2_b_2", 8),
    ("cmp_k_b1", 2), ("cmp_v_b1", 2), ("cmp_k_pos", 16), ("cmp_v_pos", 16),
)
COL = {}
for _name, _n in VECTORS:
    COL[_name] = sum(n for _, n in VECTORS[:len(COL)])
NVEC = sum(n for _, n in VECTORS)
SINKS = NVEC
CMP_W2 = SINKS + 8
NCOL = CMP_W2 + 2 * 2 * HD


class Parts:
    pass



def stream_load(sp, c):
    def load(u, slot):
        sp.dma_start(c.w_raw[:, slot], c.weights[u]).then_inc(c.s_raw[slot], 16)

    for u in range(RING):
        load(u, u)
    with sp.Fori(1, UNITS // RING) as i:
        for slot in range(RING):
            sp.wait_ge(c.s_lo, i * RING + (slot + 1 - RING))
            load(i * RING + slot, slot)
    for u in range(UNITS // RING * RING, UNITS):
        sp.wait_ge(c.s_lo, u + 1 - RING)
        load(u, u % RING)


def stream_high(act, c, u, slot, turn):
    act.wait_ge(c.s_raw[slot], turn * 16 + 16)
    act.wait_ge(c.s_pe, u + START + 1 - RING)
    act.activation(c.w_hi[:, slot], c.w_raw[:, slot], ACT.Copy).then_inc(c.s_hi, 1)


def stream_high_ahead(act, c, i, base, s):
    ahead = base + s + RING - 1
    stream_high(act, c, i * RING + ahead, ahead % RING, i + ahead // RING)


def stream_low(pool, c, first, end):
    def low(u, slot):
        pool.wait_ge(c.s_hi, u + 1)
        pool.tensor_tensor(c.w_lo[:, slot], c.w_raw[:, slot], c.w_hi[:, slot].bitcast(F32),
                           ALU.subtract).then_inc(c.s_lo, 1)

    turns = (end - first) // RING
    with pool.Fori(0, turns) as i:
        for s in range(RING):
            low(i * RING + (first + s), (first + s) % RING)
    for u in range(first + turns * RING, end):
        low(u, u % RING)


def split_products(pe, c, out, slot, rhs_hi, rhs_lo, kts, k0=0, start=True, stop=True, before=None, cols=P):
    for k in kts:
        if before is not None:
            before(k)
        hi, lo = c.w_hi[:, slot, k, 0:cols], c.w_lo[:, slot, k, 0:cols]
        first, last = start and k == kts[0], stop and k == kts[-1]
        pe.matmul(out, hi, rhs_hi(k0 + k), start=first, stop=False)
        pe.matmul(out, hi, rhs_lo(k0 + k), start=False, stop=False)
        mm = pe.matmul(out, lo, rhs_hi(k0 + k), start=False, stop=last)
    return mm



def input_pe(pe, c):
    pe.wait_ge(c.s_const, 1)
    pe.wait_ge(c.s_load, 16)
    for k in range(KD):
        for t in range(TT):
            mm = pe.transpose(c.ps[:, k, t * P:(t + 1) * P], c.stage[:, t, k * P:(k + 1) * P], c.ident[:])
        mm.then_inc(c.s_tin, 1) if k < KD - 1 else mm.then_inc(c.s_pe, START)


def input_dve(dve, c):
    for k in range(KD):
        dve.wait_ge(c.s_tin, k + 1) if k < KD - 1 else dve.wait_ge(c.s_pe, START)
        op = dve.tensor_copy(c.x[:, k], c.ps[:, k])
        op.then_inc(c.s_x, 1) if k < KD - 1 else op.then_inc(c.s_evac, START)
    dve.wait_ge(c.s_evac, START)
    dve.nop().then_inc(c.s_x, 1)
    dve.nop().then_inc(c.s_hid, START)


def input_act(act, c):
    for k in range(KD):
        act.wait_ge(c.s_x, k + 1)
        if k >= 2:
            act.wait_ge(c.s_ss, k - 1)
        act.activation(c.sq[:, k % 2], c.x[:, k], ACT.Square).then_inc(c.s_sq, 1)


def add_square(dve, c, j, k, n=None):
    dve.wait_ge(c.s_sq, j + 1 if n is None else n)
    if k == 0:
        dve.tensor_copy(c.ss[:], c.sq[:, 0]).then_inc(c.s_ss, 1)
    else:
        dve.wait_ge(c.s_ss, j if n is None else n - 1)
        dve.tensor_tensor(c.ss[:], c.ss[:], c.sq[:, k % 2], ALU.add).then_inc(c.s_ss, 1)



def norm_pe(pe, c, i):
    if i == 0:
        pe.wait_ge(c.s_const, 2)
        pe.wait_ge(c.s_evac, START)
    else:
        pe.wait_ge(c.s_root, i)
    pe.wait_ge(c.s_ss, KD * (i + 1))
    pe.matmul(c.ps[:, 4], c.ones[:], c.ss[:], start=True, stop=True).then_inc(c.s_msum, 1)


def norm_act_root(act, c, i):
    act.wait_ge(c.s_msum, i + 1)
    act.activation(c.root[:], c.ps[:, 4], ACT.Sqrt, bias=c.eps[:, 0:1], scale=1.0 / D).then_inc(c.s_root, 1)


def norm_act_high(act, c, i):
    for k in range(KD):
        act.wait_ge(c.s_y, KD * i + k + 1)
        act.activation(c.xn_hi[:, k], c.y[:, k % 3], ACT.Copy).then_inc(c.s_xhi, 1)


def norm_dve_scale(dve, c, i):
    dve.wait_ge(c.s_root, i + 1)
    dve.reciprocal(c.rstd[:], c.root[:]).then_inc(c.s_rstd, 1)
    dve.wait_ge(c.s_rstd, i + 1)


def norm_dve(dve, c, i, gain, xhi, xn):
    norm_dve_scale(dve, c, i)

    def low(k):
        dve.wait_ge(c.s_xhi, xhi + k + 1)
        dve.tensor_tensor(c.xn_lo[:, k], c.y[:, k % 3], c.xn_hi[:, k].bitcast(F32),
                          ALU.subtract).then_inc(c.s_xn, 1)

    for k in range(KD):
        if k >= 3:
            dve.wait_ge(c.s_xn, xn + k - 2)
        dve.scalar_tensor_tensor(out=c.y[:, k % 3], in0=c.x[:, k], scalar=c.par[:, COL[gain] + k:COL[gain] + k + 1],
                                 in1=c.rstd[:], op0=ALU.mult, op1=ALU.mult).then_inc(c.s_y, 1)
        if k >= 1:
            low(k - 1)
    low(KD - 1)



def up_pe(pe, c, base, units, xn_ready):
    with pe.Fori(0, units // RING) as i:
        for s in range(RING):
            u, slot = base + s, (base + s) % RING
            pe.wait_ge(c.s_lo, i * RING + (u + 1))
            pe.wait_ge(c.s_evac, i * RING + (u + START + 1 - RING))
            split_products(pe, c, c.ps[:, slot], slot, lambda k: c.xn_hi[:, k], lambda k: c.xn_lo[:, k],
                           range(KD), before=(lambda k: pe.wait_ge(c.s_xn, xn_ready + k + 1)) if s == 0 else None,
                           ).then_inc(c.s_pe, 1)


def glu_up_act(act, c, base, nf, hid_base):
    with act.Fori(0, nf // 2) as i:
        for s in range(RING):
            u, slot = base + s, (base + s) % RING
            stream_high_ahead(act, c, i, base, s)
            if s % 2 == 0:
                act.wait_ge(c.s_pe, i * RING + (u + START + 1))
                act.wait_ge(c.s_evac, i * RING + (u + START - 2))
                act.activation(c.gate[:, s // 2], c.ps[:, slot], ACT.Silu).then_inc(c.s_act, 1)


def glu_up_dve(dve, c, base, nf, hid_base, act_base, free_pe):
    dve.wait_ge(c.s_pe, free_pe + START)
    with dve.Fori(0, nf // 2) as i:
        for f in range(2):
            u = base + 2 * f + 1
            dve.wait_ge(c.s_pe, i * RING + (u + START + 1))
            dve.wait_ge(c.s_act, i * 2 + (act_base + f + 1))
            dve.wait_ge(c.s_hid, i * 2 + (hid_base + START + f - 1))
            dve.tensor_tensor(c.h[:, f], c.gate[:, f], c.ps[:, u % RING], ALU.mult).then_inc(c.s_evac, 2)
            dve.wait_ge(c.s_evac, i * RING + (u + START + 1))
            hidden_parts(dve, c, i, f, hid_base)


def hidden_parts(dve, c, i, f, hid_base):
    dve.tensor_copy(c.hid_hi[:, i * 2 + f], c.h[:, f]).then_inc(c.s_hhi, 1)
    dve.wait_ge(c.s_hhi, i * 2 + (hid_base + f + 1))
    dve.tensor_tensor(c.hid_lo[:, i * 2 + f], c.h[:, f], c.hid_hi[:, i * 2 + f].bitcast(F32),
                      ALU.subtract).then_inc(c.s_hid, 1)


def down_pe(pe, c, base, nk, hi, lo, ready):
    per = -(-nk // KU)
    with pe.Fori(0, KD * per // RING) as i:
        for s in range(RING):
            u, g = base + s, s % per
            bank = (u - g) % RING
            pe.wait_ge(c.s_lo, i * RING + (u + 1))
            if g == 0:
                pe.wait_ge(c.s_evac, i * RING + (u + START + 1 - RING))
            split_products(pe, c, c.ps[:, bank], u % RING, lambda k: hi[:, k], lambda k: lo[:, k],
                           range(min(KU, nk - g * KU)), k0=g * KU, start=g == 0, stop=g == per - 1,
                           before=(lambda k: ready(g * KU + k)) if s < per else None,
                           ).then_inc(c.s_pe, 1)


def down_act(act, c, base, nk, sq_base=None):
    per = -(-nk // KU)
    turns = KD * per // RING

    def turn(i, last):
        for s in range(RING):
            u = base + s
            if not last or i * RING + u + RING - 1 < UNITS:
                stream_high_ahead(act, c, i, base, s)
            if sq_base is not None and s % per == per - 1:
                n = s // per
                act.wait_ge(c.s_evac, i * RING + (u + START + 1))
                act.wait_ge(c.s_ss, i * (RING // per) + (sq_base + n - 1))
                act.activation(c.sq[:, n % 2], c.x[:, i * (RING // per) + n], ACT.Square).then_inc(c.s_sq, 1)

    ends = base + KD * per == UNITS
    with act.Fori(0, turns - ends) as i:
        turn(i, False)
    if ends:
        turn(turns - 1, True)


def down_dve(dve, c, base, nk, coef, sq_base=None, bias=None):
    per = -(-nk // KU)
    if bias is not None:
        for k in range(KD):
            dve.tensor_scalar(c.x[:, k], c.x[:, k], c.column(bias, k), None, ALU.add).then_inc(c.s_xb, 1)
        dve.wait_ge(c.s_xb, KD)
    if sq_base is not None:
        dve.memset(c.ss[:], 0.0).then_inc(c.s_zero, 1)
        dve.wait_ge(c.s_zero, sq_base // KD)
    with dve.Fori(0, KD * per // RING) as i:
        for s in range(per - 1, RING, per):
            u, n = base + s, s // per
            tile = i * (RING // per) + n
            dve.wait_ge(c.s_pe, i * RING + (u + START + 1))
            dve.scalar_tensor_tensor(out=c.x[:, tile], in0=c.ps[:, (u + 1 - per) % RING], scalar=coef,
                                     in1=c.x[:, tile], op0=ALU.mult, op1=ALU.add).then_inc(c.s_evac, per)
            if sq_base is not None:
                dve.wait_ge(c.s_sq, i * (RING // per) + (sq_base + n + 1))
                dve.wait_ge(c.s_ss, i * (RING // per) + (sq_base + n))
                dve.tensor_tensor(c.ss[:], c.ss[:], c.sq[:, n % 2], ALU.add).then_inc(c.s_ss, 1)



class Kind:

    def __init__(self, first, width, rows, turned, banks):
        self.first, self.width, self.rows, self.turned, self.banks = first, width, rows, turned, banks


class Pass:

    def __init__(self, kind, q, k_hi, k_lo, v_hi, v_lo, side, tile, bias, prepare_dve=None, start=-3e38,
                 table_used=None, sink=None, gate=None, row_mask=None, opens=False, closes=False, pair_done=False,
                 o_before=0):
        self.kind, self.side, self.tile = kind, side, tile
        self.q, self.k_hi, self.k_lo, self.v_hi, self.v_lo = q, k_hi, k_lo, v_hi, v_lo
        self.bias, self.prepare_dve, self.start = bias, prepare_dve, start
        self.table_used, self.sink, self.gate, self.row_mask = table_used, sink, gate, row_mask
        self.opens, self.closes, self.pair_done, self.o_before = opens, closes, pair_done, o_before


FULL = Kind(
    first=(0, 0, 0, 0), width=(128, 256, 384, 512), rows=P,
    turned=((0, 0, 0, 0, 4), (1, 1, 0, 1, 4), (3, 1, 384, 3, 4), (2, 2, 0, 2, 4)), banks=(512, 512, 256))
LOCAL = Kind(
    first=(0, 0, 1, 2), width=(128, 256, 256, 256), rows=P,
    turned=((0, 0, 0, 0, 2), (1, 0, 256, 1, 3), (2, 1, 0, 2, 4), (3, 1, 256, 3, 4)), banks=(512, 384))
BLOCKS = Kind(
    first=(0, 0, 0, 0), width=(32, 32, 32, 32), rows=32,
    turned=((0, 0, 0, 0, 4),), banks=(512,))
S_BANKS, T_BANK, O_BANK = (0, 1, 5), 2, 6
SCALE = HD ** -0.5


def at_column(kind, i):
    return sum(kind.width[:i])


def passes_before(passes):
    out = [0]
    for p in passes:
        out.append(out[-1] + len(p.kind.banks))
    return out


def attention_pe(pe, c, a, passes):
    n_banks = passes_before(passes)

    def scores(n, tiles):
        if n >= len(passes):
            return
        p = passes[n]
        for i in tiles:
            m = TT * n + i
            if m >= len(S_BANKS):
                pe.wait_ge(a.s_max, m - len(S_BANKS) + 1)
            width = p.kind.width[i] if p.kind is BLOCKS else max(p.kind.width[i], 256)
            out = c.ps[:, S_BANKS[m % 3], 0:width]
            keys = slice(p.kind.first[i] * P, p.kind.first[i] * P + width)
            q = p.q[:, i * P:i * P + P]
            pe.matmul(out, q, p.k_hi[:, keys], start=True, stop=False)
            pe.matmul(out, q, p.k_lo[:, keys], start=False, stop=True).then_inc(a.s_scores, 1)

    def turn(n):
        p = passes[n]
        for bank in range(len(p.kind.banks)):
            if n >= 1:
                pe.wait_ge(a.s_low, n_banks[n - 1] + min(bank + 1, len(passes[n - 1].kind.banks)))
            for key, b, col, q0, q1 in p.kind.turned:
                if b != bank:
                    continue
                for i in range(q0, q1):
                    pe.wait_ge(a.s_scaled, TT * n + i + 1)
                    at = at_column(p.kind, i) + (key - p.kind.first[i]) * P
                    mm = pe.transpose(c.ps[0:p.kind.rows, T_BANK + bank, col + (i - q0) * P:col + (i - q0) * P + P],
                                      a.p[:, n % 3, at:at + p.kind.rows], c.ident[:])
            mm.then_inc(a.s_turned, 1)

    def values(n):
        p = passes[n]
        out = c.ps[:, O_BANK + p.side]
        if p.opens and p.o_before > 0:
            pe.wait_ge(a.s_olow, p.o_before)
        first = p.opens
        for x, (key, b, col, q0, q1) in enumerate(p.kind.turned):
            pe.wait_ge(a.s_low, n_banks[n] + b + 1)
            w = slice(b * 512 + col, b * 512 + col + (q1 - q0) * P)
            rows = slice(0, p.kind.rows)
            for v, w_part in ((p.v_hi, a.pt_hi), (p.v_hi, a.pt_lo), (p.v_lo, a.pt_hi)):
                mm = pe.matmul(out[:, q0 * P:q1 * P], v(key), w_part[rows, n % 2, w], start=first,
                               stop=p.closes and x == len(p.kind.turned) - 1 and v is p.v_lo, skip_group_check=True)
                first = False
        mm.then_inc(a.s_values, 1)

    scores(0, range(TT))
    scores(1, range(TT))
    for n in range(-1, len(passes)):
        scores(n + 3, range(TT - 1))
        if n + 1 < len(passes):
            turn(n + 1)
        scores(n + 3, range(TT - 1, TT))
        if n >= 0:
            values(n)


def attention_act(act, c, a, passes):
    n_banks = passes_before(passes)

    def softmax(n):
        p = passes[n]
        act.wait_ge(a.s_negmax, n + 1)
        if p.table_used is not None:
            p.table_used(act)
        for i in range(TT):
            at = slice(at_column(p.kind, i), at_column(p.kind, i) + p.kind.width[i])
            act.activation(a.p[:, n % 3, at], a.p[:, n % 3, at], ACT.Exp, bias=a.negmax[:, n % 2, i:i + 1],
                           scale=SCALE, accum_out=a.sums[:, n % 2, i:i + 1]).then_inc(a.s_exp, 1)
        if p.sink is not None:
            act.activation(a.sink_exp[:, n % 2], a.negmax[:, n % 2], ACT.Exp, bias=p.sink, scale=1.0).then_inc(a.s_sinkexp, 1)

    def high(n):
        p = passes[n]
        for b, width in enumerate(p.kind.banks):
            act.wait_ge(a.s_turned, n_banks[n] + b + 1)
            if n >= 2 and b == 0:
                act.wait_ge(a.s_values, n - 1)
            act.activation(a.pt_hi[0:p.kind.rows, n % 2, b * 512:b * 512 + width],
                           c.ps[0:p.kind.rows, T_BANK + b, 0:width], ACT.Copy).then_inc(a.s_high, 1)

    def outputs(n):
        p = passes[n]
        if not p.pair_done:
            return
        act.wait_ge(a.s_values, n + 1)
        for side in range(2):
            rows = slice(side * HD, side * HD + HD)
            if a.o32 is not None:
                act.activation(a.o32[rows, p.tile], c.ps[rows, O_BANK + side], ACT.Copy).then_inc(a.s_olow, 1)
                continue
            act.activation(a.o_hi[rows, p.tile], c.ps[rows, O_BANK + side], ACT.Copy).then_inc(a.s_ohigh, 1)

    softmax(0)
    for n in range(-1, len(passes)):
        if n >= 0:
            high(n)
        if n + 2 < len(passes):
            softmax(n + 2)
        if n >= 1:
            outputs(n - 1)
    outputs(len(passes) - 1)


def attention_dve(dve, c, a, passes):
    n_banks = passes_before(passes)
    pairs = 0
    sinks = 0

    def maxima(n):
        p = passes[n]
        if p.prepare_dve is not None:
            p.prepare_dve(dve)
        if n >= 3:
            dve.wait_ge(a.s_turned, n_banks[n - 2])
        for i in range(TT):
            m = TT * n + i
            dve.wait_ge(a.s_scores, m + 1)
            at = slice(at_column(p.kind, i), at_column(p.kind, i) + p.kind.width[i])
            dve.tensor_tensor_reduce(out=a.p[:, n % 3, at], in0=c.ps[:, S_BANKS[m % 3], 0:p.kind.width[i]],
                                     in1=p.bias(i), scale=1.0, scalar=p.start, op0=ALU.add, op1=ALU.max,
                                     accum_out=a.maxima[:, n % 2, i:i + 1]).then_inc(a.s_max, 1)
        dve.wait_ge(a.s_max, TT * n + TT)
        dve.tensor_scalar(a.negmax[:, n % 2], a.maxima[:, n % 2], -SCALE, None, ALU.mult).then_inc(a.s_negmax, 1)

    def scale(n):
        nonlocal sinks
        p = passes[n]
        dve.wait_ge(a.s_exp, TT * n + TT)
        if p.sink is not None:
            sinks += 1
            dve.wait_ge(a.s_sinkexp, sinks)
            dve.tensor_tensor(a.sums[:, n % 2], a.sums[:, n % 2], a.sink_exp[:, n % 2], ALU.add).then_inc(a.s_sum, 1)
            dve.wait_ge(a.s_sum, sinks)
        dve.reciprocal(a.scale[:, n % 2], a.sums[:, n % 2]).then_inc(a.s_recip, 1)
        dve.wait_ge(a.s_recip, n + 1)
        gated = passes_gated[n]
        if p.gate is not None:
            dve.tensor_tensor(a.scale[:, n % 2], a.scale[:, n % 2], p.gate, ALU.mult).then_inc(a.s_gated, 1)
            dve.wait_ge(a.s_gated, gated)
        if p.row_mask is not None:
            dve.tensor_tensor(a.scale[:, n % 2, 0:1], a.scale[:, n % 2, 0:1], p.row_mask, ALU.mult).then_inc(a.s_rows, 1)
            dve.wait_ge(a.s_rows, passes_masked[n])
        for i in range(TT):
            at = slice(at_column(p.kind, i), at_column(p.kind, i) + p.kind.width[i])
            dve.tensor_scalar(a.p[:, n % 3, at], a.p[:, n % 3, at], a.scale[:, n % 2, i:i + 1], None,
                              ALU.mult).then_inc(a.s_scaled, 1)

    def low(n):
        p = passes[n]
        for b, width in enumerate(p.kind.banks):
            dve.wait_ge(a.s_high, n_banks[n] + b + 1)
            at = slice(b * 512, b * 512 + width)
            dve.tensor_tensor(a.pt_lo[0:p.kind.rows, n % 2, at], c.ps[0:p.kind.rows, T_BANK + b, 0:width],
                              a.pt_hi[0:p.kind.rows, n % 2, at].bitcast(F32), ALU.subtract).then_inc(a.s_low, 1)

    def outputs(n):
        nonlocal pairs
        p = passes[n]
        if not p.pair_done or a.o32 is not None:
            return
        for side in range(2):
            rows = slice(side * HD, side * HD + HD)
            dve.wait_ge(a.s_ohigh, 2 * pairs + side + 1)
            dve.tensor_tensor(a.o_lo[rows, p.tile], c.ps[rows, O_BANK + side], a.o_hi[rows, p.tile].bitcast(F32),
                              ALU.subtract).then_inc(a.s_olow, 1)
        pairs += 1

    passes_gated = [sum(q.gate is not None for q in passes[:n + 1]) for n in range(len(passes))]
    passes_masked = [sum(q.row_mask is not None for q in passes[:n + 1]) for n in range(len(passes))]
    maxima(0)
    for n in range(-1, len(passes)):
        if n + 2 < len(passes):
            maxima(n + 2)
        if n + 1 < len(passes):
            scale(n + 1)
        if n >= 0:
            low(n)
        if n >= 1:
            outputs(n - 1)
    outputs(len(passes) - 1)


def attention_buffers(c, sb, sem, tag, o_hi=None, o_lo=None, o32=None, pt=None):
    a = Parts()
    a.o_hi, a.o_lo, a.o32 = o_hi, o_lo, o32
    a.p = sb(tag + "p", [P, 3, 1280])
    if pt is None:
        a.pt_hi = sb(tag + "pt_hi", [P, 2, 1280], F32R)
        a.pt_lo = sb(tag + "pt_lo", [P, 2, 1280], F32R)
    else:
        a.pt_hi, a.pt_lo = pt
    a.maxima = sb(tag + "maxima", [P, 2, TT])
    a.negmax = sb(tag + "negmax", [P, 2, TT])
    a.sums = sb(tag + "sums", [P, 2, TT])
    a.scale = sb(tag + "scale", [P, 2, TT])
    a.sink_exp = sb(tag + "sink_exp", [P, 2, TT])
    attention_semaphores(a, sem, tag)
    return a


def attention_view(a, o32, sem, tag):
    b = Parts()
    b.o_hi, b.o_lo, b.o32 = a.o_hi, a.o_lo, o32
    b.p, b.pt_hi, b.pt_lo = a.p, a.pt_hi, a.pt_lo
    b.maxima, b.negmax, b.sums, b.scale, b.sink_exp = a.maxima, a.negmax, a.sums, a.scale, a.sink_exp
    attention_semaphores(b, sem, tag)
    return b


def attention_semaphores(a, sem, tag):
    a.s_scores = sem(tag + "s_scores")
    a.s_max = sem(tag + "s_max")
    a.s_negmax = sem(tag + "s_negmax")
    a.s_exp = sem(tag + "s_exp")
    a.s_sinkexp = sem(tag + "s_sinkexp")
    a.s_sum = sem(tag + "s_sum")
    a.s_recip = sem(tag + "s_recip")
    a.s_gated = sem(tag + "s_gated")
    a.s_rows = sem(tag + "s_rows")
    a.s_scaled = sem(tag + "s_scaled")
    a.s_turned = sem(tag + "s_turned")
    a.s_high = sem(tag + "s_high")
    a.s_low = sem(tag + "s_low")
    a.s_values = sem(tag + "s_values")
    a.s_ohigh = sem(tag + "s_ohigh")
    a.s_olow = sem(tag + "s_olow")
    a.s_bias = sem(tag + "s_bias")



NH = 8
SLOPES = [2.0 ** (-8.0 * (h + 1) / NH) for h in range(NH)]
CMP_L, CMP_STRIDE = 32, 16
NC = (T - CMP_L) // CMP_STRIDE + 1
FAR = 1e32
MIX_TILES = ("kc", "vc", "qa0", "qa1", "qa2", "qa3", "qb0", "qb1", "qb2", "qb3", "ks", "kw", "kb", "vs", "vw", "vb", "gate")
MIX_SPLIT = MIX_TILES[2:13]


def mixer_units():
    order = list(MIX_TILES[:7])
    compression = [(q, half) for q in range(4) for half in range(2)]
    for x, name in enumerate(MIX_TILES[7:]):
        order += compression[x:x + 1] + [name]
    return order


MIX_UNITS = mixer_units()


def mixer_constants(pool, c):
    def keep(ap, pattern, base, mult):
        pool.wait_ge(c.s_zeroed, c.zeroed)
        pool.affine_select(out=ap, in_=ap, compare_op=ALU.is_ge, fill=FAR, base=base, pattern=pattern,
                           channel_multiplier=mult).then_inc(c.s_zeroed, 1)
        c.zeroed += 1

    pool.iota(c.dist[:], [[-1, T]], base=T - P, channel_multiplier=1,
              allow_small_or_imprecise_dtypes=True).then_inc(c.s_zeroed, 1)
    pool.iota(c.dist_local[:], [[-1, 2 * P]], base=P, channel_multiplier=1,
              allow_small_or_imprecise_dtypes=True).then_inc(c.s_zeroed, 1)
    pool.iota(c.dist_cmp[:], [[P, TT], [-CMP_STRIDE, NC + 1]], base=1 - CMP_L, channel_multiplier=1,
              allow_small_or_imprecise_dtypes=True).then_inc(c.s_zeroed, 1)
    pool.memset(c.sees_block[:], 1.0).then_inc(c.s_zeroed, 1)
    c.zeroed += 4
    keep(c.dist[:], [[-1, T]], T - P, 1)
    keep(c.dist_local[:], [[-1, 2 * P]], P, 1)
    keep(c.dist_local[:], [[1, 2 * P]], -1, -1)
    keep(c.dist_cmp[:], [[P, TT], [-CMP_STRIDE, NC + 1]], 1 - CMP_L, 1)
    pool.wait_ge(c.s_zeroed, c.zeroed)
    pool.affine_select(out=c.sees_block[:], in_=c.sees_block[:], compare_op=ALU.is_ge, fill=0.0, base=1 - CMP_L,
                       pattern=[[0, 1]], channel_multiplier=1).then_inc(c.s_const, 1)


def stacked_high(act, ps, q, k, done):
    for side in range(2):
        src = ps[side * HD:side * HD + HD]
        if q is not None:
            act.activation(q[0:HD, side], src, ACT.Copy).then_inc(done, 1)
        else:
            for rows in (slice(0, HD), slice(HD, P)):
                act.activation(k[rows, side], src, ACT.Copy).then_inc(done, 1)


def stacked_low(dve, ps, q, k_hi, k_lo, high, before, evac):
    for side in range(2):
        src = ps[side * HD:side * HD + HD]
        if q is not None:
            dve.wait_ge(high, before + side + 1)
            op = dve.tensor_tensor(q[HD:P, side], src, q[0:HD, side].bitcast(F32), ALU.subtract)
        else:
            dve.wait_ge(high, before + 2 * side + 2)
            for rows in (slice(0, HD), slice(HD, P)):
                op = dve.tensor_tensor(k_lo[rows, side], src, k_hi[0:HD, side].bitcast(F32), ALU.subtract)
    op.then_inc(evac, 1)


def mixer_passes(c, a, m):
    passes = []

    def add(**kw):
        passes.append(Pass(**kw))

    order = [(tile, side) for tile in range(4) for side in range(2)]
    for x, (tile, side) in enumerate(order):
        h = tile + 4 * side
        both = dict(side=side, tile=tile, q=m.q[:, 2 * tile + side])
        gate = lambda b, h=h: m.gates[:, :, 3 * h + b]
        slot = x % 2

        def prepare(dve, h=h, slot=slot, x=x):
            dve.tensor_scalar(m.bias[slot][:], c.dist[:], -SLOPES[h] / SCALE, None, ALU.mult).then_inc(a.s_bias, 1)
            dve.tensor_scalar(m.bias_cmp[:, slot], c.dist_cmp[:], -SLOPES[h] / SCALE, None, ALU.mult).then_inc(a.s_bias, 1)
            dve.wait_ge(a.s_bias, 2 * x + 2)

        add(kind=BLOCKS, k_hi=m.kc_hi[:, side], k_lo=m.kc_lo[:, side], v_hi=lambda key: m.vc_hi[:], v_lo=lambda key: m.vc_lo[:],
            bias=lambda i, slot=slot: m.bias_cmp[:, slot, i], gate=gate(0), row_mask=c.sees_block[:, 0:1],
            prepare_dve=prepare, opens=True, o_before=2 * tile if tile else 0, **both)
        for b, (k, v) in ((1, (0, 0)), (2, (1, 1))):
            add(kind=FULL, k_hi=m.k_hi[:, 2 * k + side], k_lo=m.k_lo[:, 2 * k + side], v_hi=lambda key, v=v: m.v_hi[:, v, key],
                v_lo=lambda key, v=v: m.v_lo[:, v, key],
                bias=lambda i, slot=slot: m.bias[slot][:, (TT - 1 - i) * P:T], gate=gate(b),
                closes=b == 2, pair_done=b == 2 and side == 1, **both)
    for x, (tile, side) in enumerate(order):
        h = tile + 4 * side
        slot = x % 2

        def prepare(dve, h=h, slot=slot, x=x):
            dve.tensor_scalar(m.bias[slot][:, 0:2 * P], c.dist_local[:], -SLOPES[h] / SCALE, None,
                              ALU.mult).then_inc(a.s_bias, 1)
            dve.wait_ge(a.s_bias, 2 * NH + x + 1)

        add(kind=LOCAL, k_hi=m.k_hi[:, 4 + side], k_lo=m.k_lo[:, 4 + side], v_hi=lambda key: m.v_hi[:, 2, key],
            v_lo=lambda key: m.v_lo[:, 2, key], bias=lambda i, slot=slot: m.bias[slot][:, (P if i == 0 else 0):2 * P],
            prepare_dve=prepare, sink=c.sinks[:, h:h + 1], start=m.sink_start[:, h:h + 1], opens=True, closes=True,
            o_before=2 * (4 + tile), pair_done=side == 1, side=side, tile=4 + tile,
            q=m.q[:, 2 * (4 + tile) + side])
    return passes


def mixer_in_pe(pe, c, m, base, xn_ready):
    for j, name in enumerate(MIX_UNITS):
        u = base + j
        cols = 24 if name == "gate" else P
        pe.wait_ge(c.s_lo, u + 1)
        if name not in MIX_TILES:
            q, half = name
            pe.wait_ge(m.s_blk, q // 2 + 1)
            split_products(pe, c, c.ps[:, 4 + q, 0:64], u % RING, lambda k: m.blk_hi[:, q // 2, k],
                           lambda k: m.blk_lo[:, q // 2, k], range(KU), k0=half * KU, start=half == 0,
                           stop=half == 1).then_inc(c.s_pe, 1)
            continue
        pe.wait_ge(c.s_evac, u + START + 1 - RING)
        split_products(pe, c, c.ps[0:cols, u % RING], u % RING, lambda k: c.xn_hi[:, k], lambda k: c.xn_lo[:, k],
                       range(KD), cols=cols,
                       before=(lambda k: pe.wait_ge(c.s_xn, xn_ready + k + 1)) if j == 0 else None).then_inc(c.s_pe, 1)
    pe.wait_ge(c.s_evac, base + len(MIX_UNITS) + START)
    for v in range(3):
        for t in range(TT):
            mm = pe.transpose(c.ps[:, v, t * P:t * P + P], c.y[:, v, t * P:t * P + P], c.ident[:])
        mm.then_inc(m.s_vt, 1)
    pe.wait_ge(m.s_sig, 1)
    for t in range(TT):
        mm = pe.transpose(c.ps[:, 3, t * 24:t * 24 + 24], m.sig[0:24, t * P:t * P + P], c.ident[0:24, 0:24])
    mm.then_inc(m.s_vt, 1)
    pe.wait_ge(c.s_par, 16)
    pe.wait_ge(m.s_chid, 4)
    for g in range(2):
        for t in range(2):
            mm = pe.matmul(c.ps[g * HD:g * HD + HD, 4, 0:32], m.w2[:, 0, t], m.chid[:, t, g * 32:g * 32 + 32],
                           start=t == 0, stop=t == 1)
    mm.then_inc(m.s_vt, 1)
    for g in range(2):
        for t in range(2):
            mm = pe.matmul(c.ps[0:32, 5, g * HD:g * HD + HD], m.chid[:, 2 + t, g * 32:g * 32 + 32], m.w2[:, 1, t],
                           start=t == 0, stop=t == 1)
    mm.then_inc(m.s_vt, 1)
    pe.wait_ge(m.s_vlo, 5)
    pe.wait_ge(m.s_gates, 1)


def mixer_in_act(act, c, m, base):
    for j, name in enumerate(MIX_UNITS):
        u = base + j
        stream_high(act, c, u + RING - 1, (u + RING - 1) % RING, (u + RING - 1) // RING)
        act.wait_ge(c.s_pe, u + START + 1)
        if name not in MIX_TILES:
            q, half = name
            col = COL["cmp_k_b1" if q < 2 else "cmp_v_b1"] + q % 2
            if half == 1:
                act.activation(m.chid[:, q], c.ps[:, 4 + q, 0:64], ACT.Gelu_apprx_tanh,
                               bias=c.par[:, col:col + 1]).then_inc(m.s_chid, 1)
            continue
        if name in MIX_SPLIT:
            x = MIX_SPLIT.index(name)
            stacked_high(act, c.ps[:, u % RING], m.q[:, 2 * x:2 * x + 2] if x < 8 else None,
                         m.k_hi[:, 2 * x - 16:2 * x - 14] if x >= 8 else None, m.s_mhi)
        if j in (3, 4):
            act.wait_ge(m.s_blk32, j - 1)
            act.activation(m.blk_hi[:, j - 3], m.blk[:, j - 3], ACT.Copy).then_inc(m.s_blkhi, 1)
        if name == "gate":
            act.activation(m.sig[0:24], c.ps[0:24, u % RING], ACT.Sigmoid).then_inc(m.s_sig, 1)
    for v in range(3):
        act.wait_ge(m.s_vt, v + 1)
        act.activation(m.v_hi[:, v], c.ps[:, v].rearrange("p (t n) -> p t n", n=P), ACT.Copy).then_inc(m.s_vhi, 1)
    act.wait_ge(m.s_vt, 5)
    stacked_high(act, c.ps[:, 4, 0:32], None, m.kc_hi, m.s_kchi)
    act.wait_ge(m.s_vt, 6)
    act.activation(m.vc_hi[:], c.ps[0:32, 5, 0:P], ACT.Copy).then_inc(m.s_vhi, 1)


def mixer_in_dve(dve, c, m, base):
    dve.wait_ge(c.s_pe, base + START)
    dve.memset(m.blk[:], 0.0).then_inc(m.s_blk32, 1)
    dve.tensor_scalar(m.sink_start[:], c.sinks, 1.0 / SCALE, None, ALU.mult).then_inc(m.s_gates0, 1)
    dve.wait_ge(m.s_blk32, 1)
    blocks = m.blk[:].rearrange("p a k (g b) -> p a k g b", g=2)
    for j, name in enumerate(MIX_UNITS):
        u = base + j
        dve.wait_ge(c.s_pe, u + START + 1)
        if name not in MIX_TILES:
            dve.wait_ge(c.s_evac, u + START)
            dve.nop().then_inc(c.s_evac, 1)
            continue
        if name in ("kc", "vc"):
            pos = COL["cmp_k_pos" if j == 0 else "cmp_v_pos"]
            for g in range(2):
                for odd in range(2):
                    rows = slice(odd * HD, odd * HD + HD)
                    src = c.ps[g * HD:g * HD + HD, u % RING].rearrange("p (b k o) -> p k b o", k=8, o=2)
                    for part in range(2):
                        tokens = src[:, :, part:part + NC, odd]
                        dve.tensor_tensor(blocks[rows, j, part * 8:part * 8 + 8, g, 0:NC], tokens,
                                          c.par[rows, pos + part * 8:pos + part * 8 + 8].unsqueeze(2)
                                          .broadcast_to([HD, 8, NC]), ALU.add).then_inc(m.s_blk8, 1)
            dve.wait_ge(m.s_blk8, 8 * (j + 1))
            dve.nop().then_inc(c.s_evac, 1)
            dve.nop().then_inc(m.s_blk32, 1)
        elif name in MIX_SPLIT:
            x = MIX_SPLIT.index(name)
            before = 2 * x if x < 8 else 16 + 4 * (x - 8)
            if x < 8:
                stacked_low(dve, c.ps[:, u % RING], m.q[:, 2 * x:2 * x + 2], None, None, m.s_mhi, before, c.s_evac)
            else:
                k = slice(2 * x - 16, 2 * x - 14)
                stacked_low(dve, c.ps[:, u % RING], None, m.k_hi[:, k], m.k_lo[:, k], m.s_mhi, before, c.s_evac)
        elif name == "gate":
            dve.wait_ge(m.s_sig, 1)
            dve.nop().then_inc(c.s_evac, 1)
        else:
            dve.tensor_copy(c.y[:, MIX_TILES.index(name) - 13], c.ps[:, u % RING]).then_inc(c.s_evac, 1)
        if j in (4, 5):
            dve.wait_ge(m.s_blkhi, j - 3)
            dve.tensor_tensor(m.blk_lo[:, j - 4], m.blk[:, j - 4], m.blk_hi[:, j - 4].bitcast(F32),
                              ALU.subtract).then_inc(m.s_blk, 1)
    for v in range(3):
        dve.wait_ge(m.s_vhi, v + 1)
        dve.tensor_tensor(m.v_lo[:, v], c.ps[:, v].rearrange("p (t n) -> p t n", n=P), m.v_hi[:, v].bitcast(F32),
                          ALU.subtract).then_inc(m.s_vlo, 1)
    dve.wait_ge(m.s_vt, 4)
    dve.tensor_copy(m.gates[:], c.ps[:, 3, 0:96].rearrange("p (t n) -> p t n", n=24)).then_inc(m.s_gates, 1)
    stacked_low(dve, c.ps[:, 4, 0:32], None, m.kc_hi, m.kc_lo, m.s_kchi, 0, m.s_vlo)
    dve.wait_ge(m.s_vhi, 4)
    dve.tensor_tensor(m.vc_lo[:], c.ps[0:32, 5, 0:P], m.vc_hi[:].bitcast(F32), ALU.subtract).then_inc(m.s_vlo, 1)
    dve.wait_ge(m.s_gates0, 1)
    dve.wait_ge(m.s_gates, 1)

def mixer_tensors(c, sb, sem):
    m = Parts()
    m.v_hi = sb("v_hi", [P, 3, TT, P], F32R)
    m.v_lo = sb("v_lo", [P, 3, TT, P], F32R)
    m.q = sb("q_parts", [P, 16, T], F32R)
    m.k_hi = sb("k_hi", [P, 6, T], F32R)
    m.k_lo = sb("k_lo", [P, 6, T], F32R)
    m.kc_hi = sb("kc_hi", [P, 2, 32], F32R)
    m.kc_lo = sb("kc_lo", [P, 2, 32], F32R)
    m.vc_hi = sb("vc_hi", [32, P], F32R)
    m.vc_lo = sb("vc_lo", [32, P], F32R)
    m.bias = (c.rstd, c.root)
    m.bias_cmp = sb("bias_cmp", [P, 2, TT, 32])
    m.gates = sb("gates", [P, TT, 24])
    m.sink_start = sb("sink_start", [P, NH])
    m.s_blk = sem("m" + "s_blk")
    m.s_blk32 = sem("m" + "s_blk32")
    m.s_blk8 = sem("m" + "s_blk8")
    m.s_blkhi = sem("m" + "s_blkhi")
    m.s_vt = sem("m" + "s_vt")
    m.s_sig = sem("m" + "s_sig")
    m.s_chid = sem("m" + "s_chid")
    m.s_vlo = sem("m" + "s_vlo")
    m.s_kchi = sem("ms_kchi")
    m.s_vhi = sem("m" + "s_vhi")
    m.s_gates = sem("m" + "s_gates")
    m.s_gates0 = sem("m" + "s_gates0")
    m.s_mhi = sem("m" + "s_mhi")
    return m



ATT_TILES = ("q", "q", "k", "k", "v", "v")
MAX_REL = 128


def att_tensors(c, sb, sem):
    m = Parts()
    m.q = sb("aq", [P, 4, T], F32R)
    m.k_hi = sb("ak_hi", [P, 4, T], F32R)
    m.k_lo = sb("ak_lo", [P, 4, T], F32R)
    m.v_hi = sb("av_hi", [P, 2, TT, P], F32R)
    m.v_lo = sb("av_lo", [P, 2, TT, P], F32R)
    m.bias = sb("abias", [P, 2, T])
    m.s_mhi = sem("t" + "s_mhi")
    m.s_vt = sem("t" + "s_vt")
    m.s_vhi = sem("t" + "s_vhi")
    m.s_vlo = sem("t" + "s_vlo")
    m.s_loaded = sem("t" + "s_loaded")
    m.s_biased = sem("t" + "s_biased")
    m.s_ohi = sem("t" + "s_ohi")
    m.s_table = [sem("t_table0"), sem("t_table1")]
    return m


def att_passes(c, a, m, half):
    passes = []
    for x in range(4):
        tile, side = x // 2, x % 2
        h = 4 * half + x
        slot = x % 2

        def prepare(dve, x=x, slot=slot, n=4 * half + x):
            dve.wait_ge(m.s_table[slot], 16 * (n // 2 + 1))
            dve.tensor_scalar(m.bias[:, slot], m.bias[:, slot], 1.0 / SCALE, None, ALU.mult).then_inc(m.s_biased, 1)
            dve.wait_ge(m.s_biased, 2 * n + 1)
            dve.memset(m.bias[0:HD, slot, T - HD:T], -1e31).then_inc(m.s_biased, 1)
            dve.wait_ge(m.s_biased, 2 * n + 2)

        passes.append(Pass(
            kind=FULL, k_hi=m.k_hi[:, x], k_lo=m.k_lo[:, x], q=m.q[:, x],
            v_hi=lambda key, tile=tile: m.v_hi[:, tile, key], v_lo=lambda key, tile=tile: m.v_lo[:, tile, key],
            bias=lambda i, slot=slot: m.bias[:, slot, (TT - 1 - i) * P:T], gate=None, row_mask=None, sink=None,
            start=-3e38, opens=True, closes=True, pair_done=side == 1, side=side, tile=tile,
            o_before=2 * tile, prepare_dve=prepare,
            table_used=lambda act, n=h: att_table_load(act, c, m, n + 2)))
    return passes


def att_in_pe(pe, c, m, half, xn_ready):
    base = BASE["rwkv_in"] + 6 * half
    for j in range(6):
        u = base + j
        pe.wait_ge(c.s_lo, u + 1)
        pe.wait_ge(c.s_evac, u + START + 1 - RING)
        split_products(pe, c, c.ps[:, u % RING], u % RING, lambda k: c.xn_hi[:, k], lambda k: c.xn_lo[:, k], range(KD),
                       before=(lambda k: pe.wait_ge(c.s_xn, xn_ready + k + 1)) if j == 0 else None).then_inc(c.s_pe, 1)
    pe.wait_ge(c.s_evac, base + 6 + START)
    for v in range(2):
        for t in range(TT):
            mm = pe.transpose(c.ps[:, v, t * P:t * P + P], c.y[:, v, t * P:t * P + P], c.ident[:])
        mm.then_inc(m.s_vt, 1)
    pe.wait_ge(m.s_vlo, 2 * half + 2)


def att_table_load(act, c, m, n):
    if n < NH:
        act.dma_start(m.bias[:, n % 2], c.table[n]).then_inc(m.s_table[n % 2], 16)


def att_in_act(act, c, m, half):
    base = BASE["rwkv_in"] + 6 * half
    if half == 0:
        act.wait_ge(c.s_pe, base + START)
        act.wait_ge(c.s_ss, KD * 5)
        att_table_load(act, c, m, 0)
        att_table_load(act, c, m, 1)
    for j in range(6):
        u = base + j
        stream_high(act, c, u + RING - 1, (u + RING - 1) % RING, (u + RING - 1) // RING)
        if j < 4:
            act.wait_ge(c.s_pe, u + START + 1)
            x = slice(2 * (j % 2), 2 * (j % 2) + 2)
            stacked_high(act, c.ps[:, u % RING], m.q[:, x] if j < 2 else None, m.k_hi[:, x] if j >= 2 else None, m.s_mhi)
    for v in range(2):
        act.wait_ge(m.s_vt, 2 * half + v + 1)
        act.activation(m.v_hi[:, v], c.ps[:, v].rearrange("p (t n) -> p t n", n=P), ACT.Copy).then_inc(m.s_vhi, 1)


def att_in_dve(dve, c, m, half):
    base = BASE["rwkv_in"] + 6 * half
    for j in range(6):
        u = base + j
        dve.wait_ge(c.s_pe, u + START + 1)
        if j < 4:
            x = slice(2 * (j % 2), 2 * (j % 2) + 2)
            before = 12 * half + (2 * j if j < 2 else 4 * j - 4)
            if j < 2:
                stacked_low(dve, c.ps[:, u % RING], m.q[:, x], None, None, m.s_mhi, before, c.s_evac)
            else:
                stacked_low(dve, c.ps[:, u % RING], None, m.k_hi[:, x], m.k_lo[:, x], m.s_mhi, before, c.s_evac)
        else:
            dve.tensor_copy(c.y[:, j - 4], c.ps[:, u % RING]).then_inc(c.s_evac, 1)
    for v in range(2):
        dve.wait_ge(m.s_vhi, 2 * half + v + 1)
        dve.tensor_tensor(m.v_lo[:, v], c.ps[:, v].rearrange("p (t n) -> p t n", n=P), m.v_hi[:, v].bitcast(F32),
                          ALU.subtract).then_inc(m.s_vlo, 1)



CH = 64
NCH = T // CH
PAIRS = 4
LEVELS = (2, 4, 8, 16, 32)
EXP_HALF = float(np.exp(-0.5))
GN_EPS = 64e-5


def rwkv_steps():
    heads = range(2)
    pe = ["lora_w", "lora_a", "kknorm"]
    for s in heads:
        pe += [f"prod{s}{b}" for b in range(TT)] + [f"lab{s}"]
    pe += ["turnA", "turnB", "turnK", "turnV"]
    for lv in range(len(LEVELS)):
        pe += [f"w{lv}{s}" for s in heads] + [f"de{lv}{s}" for s in heads]
    pe += ["lv", "u", "z", "ru", "yl", "g0", "g1", "h0", "h1"]
    pe += [f"s{ch}" for ch in range(2, NCH)] + ["y0", "y1", "mean", "var", "bonus", "lora_g"]
    act = ["raw0", "raw1", "raw2", "sigw", "siga", "sq", "root", "eP", "ePi", "ePp", "ePe", "tA", "tB", "tK", "tV",
           "lv", "u", "z", "yl", "h0", "h1", "ysq", "yroot"]
    dve = []
    for x in "rkv":
        dve += [f"d{x}", f"{x}"]
    dve += ["ld", "L", "kk0", "rootmax", "lp", "le", "rec", "kk", "ka", "kfin", "A", "R", "b0", "B", "Bp", "K", "Kp", "rk"]
    for s in heads:
        dve += [f"mm{s}{b}" for b in range(TT)] + [f"dm{s}", f"D{s}", f"em{s}", f"E{s}"]
    for lv in range(len(LEVELS)):
        dve += [f"W{lv}{s}" for s in heads]
        dve += [x for s in heads for x in ((f"D{lv}{s}", f"E{lv}{s}") if lv < len(LEVELS) - 1 else (f"E{lv}{s}",))]
    dve += ["ru", "gd", "g0", "g1", "S1"] + [f"S{ch}{s}" for ch in range(2, NCH) for s in heads]
    dve += ["y0", "y1", "yc", "yrec", "yn", "ylnb", "bon", "ysum", "out"]
    return pe, act, dve


PE_STEPS, ACT_STEPS, DVE_STEPS = rwkv_steps()
for _engine in (PE_STEPS, ACT_STEPS, DVE_STEPS):
    assert len(set(_engine)) == len(_engine)


def rwkv_tensors(c, sb, sem):
    w = Parts()
    w.raw = sb("raw", [P, 3, 1 + T])
    w.lora_in = sb("lora_in", [P, 2, T])
    w.lora_w = sb("lora_w", [P, 2, T])
    w.r, w.k, w.v = (sb("rk" + x, [P, T]) for x in "rkv")
    w.eP = sb("eP", [P, T])
    w.L = sb("L", [P, T])
    w.AR = sb("AR", [P, TT, 2, P])
    w.BK = sb("BK", [P, 2, T])
    w.BKp = sb("BKp", [P, 2, T])
    w.tok = sb("tok", [P, 4, TT, P])
    w.M = sb("M", [P, 2, TT, 4, P])
    w.DE = sb("DE", [P, 2, 2, TT, P])
    w.S = sb("S", [P, NCH, HD])
    w.y32 = sb("y32", [P, PAIRS, T])
    w.scan_keep = sb("scan_keep", [P, NCH, CH], BF16)
    w.ld = c.ss
    w.kk = c.rstd
    w.a = c.root
    w.tmp, w.tmp2, w.rk = c.y[:, 0], c.y[:, 1], c.y[:, 2]
    w.ePi, w.ePp, w.ePe = w.raw[:, 0, 1:], w.raw[:, 1, 1:], w.raw[:, 2, 1:]
    w.W = w.BK[:].rearrange("p s (b n) -> p s b n", n=P)
    w.LV = w.tmp.rearrange("p (b n) -> p b n", n=P)
    w.U = w.kk[:].rearrange("p (b n) -> p b n", n=P)
    w.Z = w.a[:].rearrange("p (b n) -> p b n", n=P)
    w.YL, w.RU = w.ld, w.L
    w.G = w.BKp[:, 0].rearrange("p (c n) -> p c n", n=HD)
    w.H = w.BKp[:, 1].rearrange("p (c n) -> p c n", n=HD)
    w.s_wpe = sem("s_wpe")
    w.s_wact = sem("s_wact")
    w.s_wdve = sem("s_wdve")
    w.s_wshift = sem("s_wshift")
    w.s_wlora = sem("s_wlora")
    w.s_whi = sem("s_whi")
    w.s_wlo = sem("s_wlo")
    w.s_wload = sem("s_wload")
    return w


def step_counter(w, engine_name, steps):
    pos = {name: i for i, name in enumerate(steps)}
    sem = {"pe": w.s_wpe, "act": w.s_wact, "dve": w.s_wdve}[engine_name]
    issued = [0]

    def done(name, ins):
        assert steps[issued[0] % len(steps)] == name, (name, steps[issued[0] % len(steps)])
        issued[0] += 1
        ins.then_inc(sem, 1)

    def wait(eng, j, name):
        eng.wait_ge(sem, j * len(steps) + pos[name] + 1)

    return done, wait


def rwkv_waits(w):
    return {e: step_counter(w, e, steps) for e, steps in (("pe", PE_STEPS), ("act", ACT_STEPS), ("dve", DVE_STEPS))}


def rwkv_units_pe(pe, c, base, n):
    for j in range(n):
        u = base + j
        pe.wait_ge(c.s_lo, u + 1)
        pe.wait_ge(c.s_evac, u + START + 1 - RING)
        split_products(pe, c, c.ps[:, u % RING], u % RING, lambda k: c.xn_hi[:, k], lambda k: c.xn_lo[:, k],
                       range(KD)).then_inc(c.s_pe, 1)


def rwkv_pe(pe, c, w, base):
    ways = rwkv_waits(w)
    done, _ = ways["pe"]
    A = lambda j, name: ways["act"][1](pe, j, name)
    V = lambda j, name: ways["dve"][1](pe, j, name)
    ps = c.ps
    rwkv_units_pe(pe, c, base, 2)
    rwkv_units_pe(pe, c, base + 2, 3)
    pe.wait_ge(w.s_wload, 32)
    pe.wait_ge(w.s_wlora, 3)
    for j in range(PAIRS):
        if j + 1 < PAIRS:
            rwkv_units_pe(pe, c, base + 2 + 3 * (j + 1), 3)
        cols = slice(j * P, j * P + P)
        if j >= 1:
            V(j - 1, "out")
        done("lora_w", pe.matmul(ps[:, 4], w.lora_w[0:HD, 0, cols], w.lora_in[0:HD, 0], start=True, stop=True))
        done("lora_a", pe.matmul(ps[:, 5], w.lora_w[HD:P, 0, cols], w.lora_in[HD:P, 0], start=True, stop=True))
        A(j, "sq")
        done("kknorm", pe.matmul(ps[:, 6], c.ones_head[:], w.tmp2, start=True, stop=True))
        for s in range(2):
            rows = slice(s * HD, s * HD + HD)
            if s == 0:
                V(j, "Kp")
                A(j, "root")
            for b in range(TT):
                bank = 4 + b % 2
                if b >= 2 or s:
                    V(j, f"mm{s}{b - 2}" if b >= 2 else f"mm0{b + 2}")
                blk = slice(b * P, b * P + P)
                pe.matmul(ps[:, bank, 0:2 * P], w.BK[rows, 0, blk], w.AR[rows, b], start=True, stop=True)
                done(f"prod{s}{b}", pe.matmul(ps[:, bank, 2 * P:4 * P], w.BK[rows, 1, blk], w.AR[rows, b],
                                              start=True, stop=True))
            for b in range(TT):
                mm = pe.matmul(ps[:, 6 + s, b * P:b * P + P], w.AR[rows, b, 0], w.BK[rows, 0, b * P:b * P + P],
                               start=True, stop=True)
            done(f"lab{s}", mm)
        sources = (lambda b: w.AR[:, b, 0], lambda b: w.BKp[:, 0, b * P:b * P + P], lambda b: w.BKp[:, 1, b * P:b * P + P],
                   lambda b: w.v[:, b * P:b * P + P])
        for x, name in enumerate(("turnA", "turnB", "turnK", "turnV")):
            if x == 0:
                V(j, "mm12")
            elif x == 1:
                V(j, "mm13")
            elif x == 2:
                A(j, "tA")
            else:
                A(j, "tB")
            for b in range(TT):
                mm = pe.transpose(ps[:, 4 + x % 2, b * P:b * P + P], sources[x](b), c.ident[:])
            done(name, mm)
        for lv in range(len(LEVELS)):
            for s in range(2):
                V(j, f"E{s}" if lv == 0 else f"E{lv - 1}{s}")
                if lv == 0:
                    A(j, ("tK", "tV")[s])
                for b in range(TT):
                    mm = pe.matmul(ps[:, 4 + s, b * P:b * P + P], w.M[:, s, b, 0], w.DE[:, s, 0, b], start=True, stop=True)
                done(f"w{lv}{s}", mm)
            for s in range(2):
                V(j, f"W{lv}{s}")
                if s == 1:
                    V(j, f"E{lv}0")
                last = lv == len(LEVELS) - 1
                if not last:
                    for b in range(TT):
                        pe.matmul(ps[:, 6, b * P:b * P + P], w.DE[:, s, 1, b], w.W[:, s, b], start=True, stop=True)
                for b in range(TT):
                    mm = pe.matmul(ps[:, 7, b * P:b * P + P], w.W[:, s, b], w.DE[:, s, 1, b], start=True, stop=True)
                done(f"de{lv}{s}", mm)
        for s in range(2):
            for b in range(TT):
                at = slice(b * P + s * HD, b * P + s * HD + HD)
                mm = pe.matmul(ps[:, 4, at], w.M[:, s, b, 2], w.tok[:, 3, b, s * HD:s * HD + HD], start=True, stop=True)
        done("lv", mm)
        V(j, f"E{len(LEVELS) - 1}1")
        for bank, name in ((5, "u"), (6, "z")):
            if name == "z":
                A(j, "lv")
            for s in range(2):
                for b in range(TT):
                    at = slice(b * P + s * HD, b * P + s * HD + HD)
                    rhs = w.tok[:, 0, b, s * HD:s * HD + HD] if name == "u" else w.LV[:, b, s * HD:s * HD + HD]
                    mm = pe.matmul(ps[:, bank, at], w.DE[:, s, 1, b], rhs, start=True, stop=True)
            done(name, mm)
        A(j, "u")
        for s in range(2):
            for b in range(TT):
                mm = pe.matmul(ps[s * HD:s * HD + HD, 7, b * P:b * P + P], w.U[:, b, s * HD:s * HD + HD],
                               w.M[:, s, b, 1], start=True, stop=True)
        done("ru", mm)
        A(j, "z")
        for s in range(2):
            for b in range(TT):
                pe.matmul(ps[s * HD:s * HD + HD, 4, b * P:b * P + P], w.Z[:, b, s * HD:s * HD + HD],
                          w.M[:, s, b, 1], start=True, stop=False)
                mm = pe.matmul(ps[s * HD:s * HD + HD, 4, b * P:b * P + P], w.tok[:, 3, b, s * HD:s * HD + HD],
                               w.M[:, s, b, 3], start=False, stop=True)
        done("yl", mm)
        for half in range(2):
            rows = slice(half * HD, half * HD + HD)
            for s in range(2):
                f = slice(s * HD, s * HD + HD)
                for b in range(TT):
                    mm = pe.matmul(ps[f, 5 + half, b * HD:b * HD + HD], w.U[rows, b, f], w.tok[rows, 1, b, f],
                                   start=True, stop=True)
            done(f"g{half}", mm)
        for half in range(2):
            rows = slice(half * HD, half * HD + HD)
            if half == 0:
                V(j, "ru")
            else:
                A(j, "yl")
            for s in range(2):
                f = slice(s * HD, s * HD + HD)
                for b in range(TT):
                    out = ps[f, (7, 4)[half], b * HD:b * HD + HD]
                    pe.matmul(out, w.tok[rows, 1, b, f], w.Z[rows, b, f], start=True, stop=False)
                    mm = pe.matmul(out, w.tok[rows, 2, b, f], w.tok[rows, 3, b, f], start=False, stop=True)
            done(f"h{half}", mm)
        V(j, "g1")
        A(j, "h1")
        for ch in range(2, NCH):
            V(j, "S1" if ch == 2 else f"S{ch - 1}1")
            for s in range(2):
                f = slice(s * HD, s * HD + HD)
                mm = pe.matmul(ps[f, 5 + s, (ch % 2) * HD:(ch % 2) * HD + HD], w.G[f, ch - 1], w.S[f, ch - 1],
                               start=True, stop=True)
            done(f"s{ch}", mm)
        V(j, f"S{NCH - 1}1")
        for s in range(2):
            f = slice(s * HD, s * HD + HD)
            for ch in range(1, NCH):
                mm = pe.matmul(ps[f, (7, 4)[s], ch * CH:ch * CH + CH], w.S[f, ch], w.RU[f, ch * CH:ch * CH + CH],
                               start=True, stop=True)
            done(f"y{s}", mm)
        V(j, "y1")
        done("mean", pe.matmul(ps[:, 5], c.ones_head[:], w.YL[:], start=True, stop=True))
        A(j, "ysq")
        done("var", pe.matmul(ps[:, 6], c.ones_head[:], w.tmp2, start=True, stop=True))
        V(j, "rk")
        done("bonus", pe.matmul(ps[:, 7], c.ones_head[:], w.rk, start=True, stop=True))
        done("lora_g", pe.matmul(ps[:, 4], w.lora_w[:, 1, cols], w.lora_in[:, 1], start=True, stop=True))


def rwkv_act(act, c, w, base):
    ways = rwkv_waits(w)
    done, own = ways["act"]
    E = lambda j, name: ways["pe"][1](act, j, name)
    V = lambda j, name: ways["dve"][1](act, j, name)
    ps = c.ps

    def high(u):
        stream_high(act, c, u + RING - 1, (u + RING - 1) % RING, (u + RING - 1) // RING)

    act.wait_ge(c.s_pe, base + START + 1)
    act.dma_start(w.lora_w[:, 0], c.lora[0:P]).then_inc(w.s_wload, 16)
    act.dma_start(w.lora_w[:, 1], c.lora[P:2 * P]).then_inc(w.s_wload, 16)
    act.wait_ge(w.s_wshift, 1)
    for x in range(2):
        high(base + x)
        act.wait_ge(c.s_pe, base + x + START + 1)
        act.activation(w.raw[:, x, 1:], ps[:, (base + x) % RING], ACT.Copy).then_inc(w.s_whi, 1)
    act.wait_ge(w.s_wshift, 6)
    act.activation(w.lora_in[0:HD, 0], c.y[0:HD, 0], ACT.Tanh).then_inc(w.s_wlora, 1)
    act.activation(w.lora_in[HD:P, 0], c.y[HD:P, 0], ACT.Copy).then_inc(w.s_wlora, 1)
    act.activation(w.lora_in[:, 1], c.y[:, 1], ACT.Sigmoid).then_inc(w.s_wlora, 1)
    act.wait_ge(w.s_wlora, 3)
    for j in range(PAIRS):
        for x in range(3):
            u = base + 2 + 3 * j + x
            high(u)
            act.wait_ge(c.s_pe, u + START + 1)
            done(f"raw{x}", act.activation(w.raw[:, x, 1:], ps[:, u % RING], ACT.Copy))
        E(j, "lora_w")
        done("sigw", act.activation(w.ld[:], ps[:, 4], ACT.Sigmoid, bias=c.column("l0_w0_2", j)))
        E(j, "lora_a")
        done("siga", act.activation(w.a[:], ps[:, 5], ACT.Sigmoid, bias=c.column("l0_a0_2", j)))
        V(j, "kk0")
        done("sq", act.activation(w.tmp2, w.kk[:], ACT.Square))
        E(j, "kknorm")
        done("root", act.activation(w.tmp, ps[:, 6], ACT.Sqrt))
        V(j, "L")
        done("eP", act.activation(w.eP[:], w.L[:], ACT.Exp))
        V(j, "v")
        done("ePi", act.activation(w.ePi, w.L[:], ACT.Exp, scale=-1.0))
        V(j, "lp")
        done("ePp", act.activation(w.ePp, w.ePp, ACT.Exp))
        V(j, "le")
        done("ePe", act.activation(w.ePe, w.ePe, ACT.Exp))
        for x, name in enumerate(("A", "B", "K", "V")):
            E(j, "turn" + name)
            done("t" + name, act.activation(w.tok[:, x], ps[:, 4 + x % 2].rearrange("p (b n) -> p b n", n=P), ACT.Copy))
        E(j, "lv")
        done("lv", act.activation(w.LV, ps[:, 4].rearrange("p (b n) -> p b n", n=P), ACT.Copy))
        E(j, "u")
        done("u", act.activation(w.U, ps[:, 5].rearrange("p (b n) -> p b n", n=P), ACT.Copy))
        E(j, "z")
        done("z", act.activation(w.Z, ps[:, 6].rearrange("p (b n) -> p b n", n=P), ACT.Copy))
        E(j, "yl")
        done("yl", act.activation(w.YL[:], ps[:, 4], ACT.Copy))
        for half in range(2):
            E(j, f"h{half}")
            done(f"h{half}", act.activation(w.H[:, half:NCH:2], ps[:, (7, 4)[half], 0:TT * HD].rearrange("p (b n) -> p b n", n=HD),
                                            ACT.Copy))
        V(j, "yc")
        done("ysq", act.activation(w.tmp2, w.tmp, ACT.Square))
        E(j, "var")
        done("yroot", act.activation(w.kk[:], ps[:, 6], ACT.Sqrt, bias=c.gn_eps[:, 0:1], scale=1.0 / HD))
    V(PAIRS - 1, "out")
    act.wait_ge(c.s_pe, base + 14 + START)
    for k in range(KD):
        src = w.y32[:, k] if k < 4 else c.o32[:, k - 4]
        act.activation(c.xn_hi[:, k], src, ACT.Copy).then_inc(w.s_whi, 1)


def rwkv_dve(dve, c, w, base):
    ways = rwkv_waits(w)
    done, _ = ways["dve"]
    own = lambda j, name: ways["dve"][1](dve, j, name)
    E = lambda j, name: ways["pe"][1](dve, j, name)
    A = lambda j, name: ways["act"][1](dve, j, name)
    ps = c.ps
    blocks = lambda ap: ap.rearrange("p (b n) -> p b n", n=P)
    over = lambda mask: mask.unsqueeze(1).broadcast_to([P, TT, P])

    dve.wait_ge(c.s_pe, base + START + 1)
    for x in range(3):
        dve.memset(w.raw[:, x, 0:1], 0.0).then_inc(w.s_wlo, 1)
    dve.memset(w.scan_keep[:], 1.0).then_inc(w.s_wlo, 1)
    dve.wait_ge(w.s_wlo, 4)
    dve.memset(w.scan_keep[:, :, 0:1], 0.0).then_inc(w.s_wshift, 1)
    dve.tensor_scalar(c.omka[:], c.par[:, COL["l0_k_a_2"]:COL["l0_k_a_2"] + 4], -1.0, 1.0, ALU.mult,
                      ALU.add).then_inc(w.s_wshift, 1)
    for x in range(2):
        dve.wait_ge(w.s_whi, x + 1)
        dve.tensor_tensor(c.y[:, x], w.raw[:, x, 0:T], w.raw[:, x, 1:], ALU.subtract).then_inc(w.s_wshift, 1)
        dve.wait_ge(w.s_wshift, 3 + 2 * x)
        dve.scalar_tensor_tensor(out=c.y[:, x], in0=c.y[:, x], scalar=c.column("l0_shift_mu_2", 12 + x),
                                 in1=w.raw[:, x, 1:], op0=ALU.mult, op1=ALU.add).then_inc(w.s_wshift, 1)
        dve.nop().then_inc(c.s_evac, 1)
    dve.wait_ge(w.s_wlora, 3)
    for j in range(PAIRS):
        for x, (name, dst) in enumerate((("r", w.r), ("k", w.k), ("v", w.v))):
            A(j, f"raw{x}")
            dve.nop().then_inc(c.s_evac, 1)
            done("d" + name, dve.tensor_tensor(dst[:], w.raw[:, x, 0:T], w.raw[:, x, 1:], ALU.subtract))
            own(j, "d" + name)
            done(name, dve.scalar_tensor_tensor(out=dst[:], in0=dst[:], scalar=c.column("l0_shift_mu_2", 4 * x + j),
                                                in1=w.raw[:, x, 1:], op0=ALU.mult, op1=ALU.add))
        A(j, "sigw")
        done("ld", dve.tensor_scalar(w.ld[:], w.ld[:], -EXP_HALF, None, ALU.mult))
        own(j, "ld")
        done("L", dve.tensor_tensor_scan(w.L[:], w.scan_keep[:].rearrange("p c n -> p (c n)"), w.ld[:], 0.0, ALU.mult, ALU.add))
        A(j, "raw2")
        done("kk0", dve.tensor_scalar(w.kk[:], w.k[:], c.column("l0_k_k_2", j), None, ALU.mult))
        A(j, "root")
        done("rootmax", dve.tensor_scalar(w.tmp, w.tmp, 1e-12, None, ALU.max))
        own(j, "L")
        done("lp", dve.tensor_tensor(w.ePp, w.L[:], w.ld[:], ALU.subtract))
        lw = w.L[:].rearrange("p (c n) -> p c n", n=CH)
        done("le", dve.tensor_tensor(w.ePe.rearrange("p (c n) -> p c n", n=CH),
                                     lw[:, :, CH - 1:CH].broadcast_to([P, NCH, CH]), lw, ALU.subtract))
        own(j, "rootmax")
        done("rec", dve.reciprocal(w.tmp, w.tmp))
        own(j, "rec")
        done("kk", dve.tensor_tensor(w.kk[:], w.kk[:], w.tmp, ALU.mult))
        A(j, "siga")
        done("ka", dve.tensor_scalar(w.tmp2, w.a[:], c.column("l0_k_a_2", j), c.omka[:, j:j + 1], ALU.mult, ALU.add))
        own(j, "ka")
        done("kfin", dve.tensor_tensor(w.k[:], w.k[:], w.tmp2, ALU.mult))
        A(j, "ePe")
        own(j, "kfin")
        done("A", dve.scalar_tensor_tensor(out=w.AR[:, :, 0], in0=blocks(w.kk[:]), scalar=-1.0, in1=blocks(w.ePp),
                                           op0=ALU.mult, op1=ALU.mult))
        done("R", dve.tensor_tensor(w.AR[:, :, 1], blocks(w.r[:]), blocks(w.eP[:]), ALU.mult))
        done("b0", dve.tensor_tensor(w.tmp, w.kk[:], w.a[:], ALU.mult))
        own(j, "b0")
        done("B", dve.tensor_tensor(w.BK[:, 0], w.tmp, w.ePi, ALU.mult))
        done("Bp", dve.tensor_tensor(w.BKp[:, 0], w.tmp, w.ePe, ALU.mult))
        done("K", dve.tensor_tensor(w.BK[:, 1], w.k[:], w.ePi, ALU.mult))
        done("Kp", dve.tensor_tensor(w.BKp[:, 1], w.k[:], w.ePe, ALU.mult))
        done("rk", dve.scalar_tensor_tensor(out=w.rk, in0=w.r[:], scalar=c.column("l0_r_k_2", j), in1=w.k[:],
                                            op0=ALU.mult, op1=ALU.mult))
        for s in range(2):
            D, Et = w.DE[:, s, 0], w.DE[:, s, 1]
            for b in range(TT):
                E(j, f"prod{s}{b}")
                done(f"mm{s}{b}", dve.tensor_tensor(w.M[:, s, b], ps[:, 4 + b % 2].rearrange("p (x n) -> p x n", n=P),
                                                    c.mask4[:], ALU.mult))
            E(j, f"lab{s}")
            done(f"dm{s}", dve.tensor_tensor(D, blocks(ps[:, 6 + s]), over(c.level[:, 0]), ALU.mult))
            own(j, f"dm{s}")
            done(f"D{s}", dve.tensor_tensor(D, D, over(c.ident[:]), ALU.add))
            done(f"em{s}", dve.tensor_tensor(Et, w.M[:, s, :, 0], over(c.level[:, 6]), ALU.mult))
            own(j, f"em{s}")
            done(f"E{s}", dve.tensor_tensor(Et, Et, over(c.ident[:]), ALU.add))
        for lv in range(len(LEVELS)):
            for s in range(2):
                E(j, f"w{lv}{s}")
                if lv == 0:
                    E(j, "lab1")
                done(f"W{lv}{s}", dve.tensor_tensor(w.W[:, s], blocks(ps[:, 4 + s]), over(c.level[:, lv + 1]), ALU.mult))
            for s in range(2):
                E(j, f"de{lv}{s}")
                if lv < len(LEVELS) - 1:
                    done(f"D{lv}{s}", dve.tensor_tensor(w.DE[:, s, 0], w.DE[:, s, 0], blocks(ps[:, 6]), ALU.add))
                done(f"E{lv}{s}", dve.tensor_tensor(w.DE[:, s, 1], w.DE[:, s, 1], blocks(ps[:, 7]), ALU.add))
        E(j, "ru")
        done("ru", dve.tensor_tensor(w.RU[:].rearrange("p (b n) -> p b n", n=P), blocks(ps[:, 7]), w.AR[:, :, 1], ALU.add))
        A(j, "tB")
        A(j, "tK")
        p_end = w.eP[:].rearrange("p (c n) -> p c n", n=CH)[:, :, CH - 1:CH].broadcast_to([P, NCH, HD])
        done("gd", dve.tensor_tensor(w.G, c.ident_head[:].unsqueeze(1).broadcast_to([P, NCH, HD]), p_end, ALU.mult))
        own(j, "gd")
        for half in range(2):
            E(j, f"g{half}")
            g = w.G[:, half:NCH:2]
            done(f"g{half}", dve.tensor_tensor(g, g, ps[:, 5 + half, 0:TT * HD].rearrange("p (b n) -> p b n", n=HD), ALU.add))
        A(j, "h1")
        done("S1", dve.tensor_copy(w.S[:, 1], w.H[:, 0]))
        for ch in range(2, NCH):
            E(j, f"s{ch}")
            for s in range(2):
                f = slice(s * HD, s * HD + HD)
                done(f"S{ch}{s}", dve.tensor_tensor(w.S[f, ch], w.H[f, ch - 1], ps[f, 5 + s, (ch % 2) * HD:(ch % 2) * HD + HD],
                                                    ALU.add))
        for s in range(2):
            f = slice(s * HD, s * HD + HD)
            E(j, f"y{s}")
            done(f"y{s}", dve.tensor_tensor(w.YL[f, CH:], w.YL[f, CH:], ps[f, (7, 4)[s], CH:], ALU.add))
        E(j, "mean")
        done("yc", dve.scalar_tensor_tensor(out=w.tmp, in0=ps[:, 5], scalar=-1.0 / HD, in1=w.YL[:], op0=ALU.mult, op1=ALU.add))
        A(j, "yroot")
        done("yrec", dve.reciprocal(w.kk[:], w.kk[:]))
        own(j, "yrec")
        done("yn", dve.tensor_tensor(w.tmp, w.tmp, w.kk[:], ALU.mult))
        own(j, "yn")
        done("ylnb", dve.tensor_scalar(w.tmp, w.tmp, c.column("l0_lnx_w_2", j), c.column("l0_lnx_b_2", j), ALU.mult, ALU.add))
        E(j, "bonus")
        done("bon", dve.tensor_tensor(w.a[:], w.v[:], ps[:, 7], ALU.mult))
        own(j, "bon")
        done("ysum", dve.tensor_tensor(w.a[:], w.a[:], w.tmp, ALU.add))
        E(j, "lora_g")
        own(j, "ysum")
        done("out", dve.tensor_tensor(w.y32[:, j], w.a[:], ps[:, 4], ALU.mult))
    for k in range(KD):
        src = w.y32[:, k] if k < 4 else c.o32[:, k - 4]
        dve.wait_ge(w.s_whi, 2 + k + 1)
        dve.tensor_tensor(c.xn_lo[:, k], src, c.xn_hi[:, k].bitcast(F32), ALU.subtract).then_inc(c.s_xn, 1)


def rwkv_constants(pool, c):
    def select(ap, pattern, base, mult, op=ALU.is_ge, fill=0.0):
        pool.wait_ge(c.s_zeroed, c.zeroed)
        pool.affine_select(out=ap, in_=ap, compare_op=op, fill=fill, base=base, pattern=pattern,
                           channel_multiplier=mult).then_inc(c.s_zeroed, 1)
        c.zeroed += 1

    for ap, value in ((c.level, 1.0), (c.mask4, 1.0), (c.ones_head, 1.0), (c.ident_head, 0.0), (c.gn_eps, GN_EPS),
                      (c.ln_eps, LN_EPS)):
        pool.memset(ap[:], value).then_inc(c.s_zeroed, 1)
        c.zeroed += 1
    for x, m in enumerate((1,) + LEVELS):
        n = P // (2 * m)
        ap = c.level[:, x].rearrange("p (q h r) -> p q h r", h=2, r=m)
        select(ap, [[-2 * m, n], [0, 2], [0, m]], -m, 1)
        select(ap, [[2 * m, n], [0, 2], [0, m]], 2 * m - 1, -1)
        select(ap, [[0, n], [-1, 2], [0, m]], 0, 0)
    ap = c.level[:, 6].rearrange("p (q h) -> p q h", h=2)
    select(ap, [[-2, P // 2], [0, 2]], 0, 1, op=ALU.is_equal)
    select(ap, [[0, P // 2], [1, 2]], -1, 0)
    for x in range(4):
        ap = c.mask4[:, x].rearrange("p (c n) -> p c n", n=CH)
        select(ap, [[CH, 2], [1, CH]], -1 if x % 2 == 0 else 0, -1)
        select(ap, [[-CH, 2], [0, CH]], 0, 1)
    ap = c.ones_head[:].rearrange("p (h n) -> p h n", n=HD)
    select(ap, [[-HD, 2], [0, HD]], 0, 1)
    select(ap, [[HD, 2], [0, HD]], HD - 1, -1)
    for h in range(2):
        select(c.ident_head[:], [[-1, HD]], -HD * h, 1, op=ALU.not_equal, fill=1.0)
    pool.wait_ge(c.s_zeroed, c.zeroed)
    pool.nop().then_inc(c.s_const2, 1)



def mlp_up_act(act, c, base, nf):
    with act.Fori(0, nf // RING) as i:
        for s in range(RING):
            u, slot = base + s, (base + s) % RING
            stream_high_ahead(act, c, i, base, s)
            act.wait_ge(c.s_pe, i * RING + (u + START + 1))
            act.wait_ge(c.s_evac, i * RING + (u + START - 1))
            act.activation(c.gate[:, s % 2], c.ps[:, slot], ACT.Relu).then_inc(c.s_act, 1)


def mlp_up_dve(dve, c, base, nf, hid_base, act_base):
    dve.wait_ge(c.s_pe, base + START)
    with dve.Fori(0, nf // RING) as i:
        for s in range(RING):
            u = base + s
            dve.wait_ge(c.s_pe, i * RING + (u + START + 1))
            dve.wait_ge(c.s_act, i * RING + (act_base + s + 1))
            dve.wait_ge(c.s_hid, i * RING + (hid_base + START + s - 1))
            dve.tensor_tensor(c.h[:, s % 2], c.gate[:, s % 2], c.ps[:, u % RING], ALU.mult).then_inc(c.s_evac, 1)
            dve.wait_ge(c.s_evac, i * RING + (u + START + 1))
            dve.tensor_copy(c.hid_hi[:, i * RING + s], c.h[:, s % 2]).then_inc(c.s_hhi, 1)
            dve.wait_ge(c.s_hhi, i * RING + (hid_base + s + 1))
            dve.tensor_tensor(c.hid_lo[:, i * RING + s], c.h[:, s % 2], c.hid_hi[:, i * RING + s].bitcast(F32),
                              ALU.subtract).then_inc(c.s_hid, 1)



TAPS = 31


def conv_tensors(c, sb, sem):
    v = Parts()
    v.u = sb("cu", [P, 2, TAPS - 1 + T])
    v.gate = sb("cgate", [P, 2, T])
    v.acc = sb("cacc", [P, 2, T])
    v.out = sb("cout", [P, KD, T])
    v.sum = sb("csum", [P, T])
    v.mean = sb("cmean", [P, T])
    v.taps = sb("ctaps", [P, KD, TAPS])
    v.s_vgate = sem("s_vgate")
    v.s_vu = sem("s_vu")
    v.s_vtap = sem("s_vtap")
    v.s_vout = sem("s_vout")
    v.s_vsq = sem("s_vsq")
    v.s_vsum = sem("s_vsum")
    v.s_vstat = sem("s_vstat")
    v.s_vroot = sem("s_vroot")
    v.s_vn = sem("s_vn")
    v.s_vsilu = sem("s_vsilu")
    v.s_vload = sem("s_vload")
    v.s_vmean = sem("s_vmean")
    return v


def conv_pe(pe, c, v, base, xn_ready):
    for j in range(16):
        u = base + j
        pe.wait_ge(c.s_lo, u + 1)
        pe.wait_ge(c.s_evac, u + START + 1 - RING)
        split_products(pe, c, c.ps[:, u % RING], u % RING, lambda k: c.xn_hi[:, k], lambda k: c.xn_lo[:, k], range(KD),
                       before=(lambda k: pe.wait_ge(c.s_xn, xn_ready + k + 1)) if j == 0 else None).then_inc(c.s_pe, 1)
    pe.wait_ge(v.s_vsum, 2 * KD)
    pe.matmul(c.ps[:, 5], c.ones[:], v.sum[:], start=True, stop=True)
    pe.matmul(c.ps[:, 6], c.ones[:], c.ss[:], start=True, stop=True).then_inc(v.s_vstat, 1)


def conv_act(act, c, v, base):
    act.wait_ge(c.s_pe, base + START)
    act.wait_ge(c.s_ss, KD * 7)
    act.dma_start(v.taps[:], c.dw).then_inc(v.s_vload, 16)

    def square(n):
        act.wait_ge(v.s_vout, n + 1)
        if n >= 2:
            act.wait_ge(v.s_vsum, 2 * (n - 1))
        act.activation(c.sq[:, n % 2], v.out[:, n], ACT.Square).then_inc(v.s_vsq, 1)

    for n in range(KD):
        for x in range(2):
            u = base + 2 * n + x
            stream_high(act, c, u + RING - 1, (u + RING - 1) % RING, (u + RING - 1) // RING)
        if n >= 1:
            square(n - 1)
        act.wait_ge(c.s_pe, u + START + 1)
        if n >= 2:
            act.wait_ge(v.s_vu, n - 1)
        act.activation(v.gate[:, n % 2], c.ps[:, u % RING], ACT.Sigmoid,
                       bias=c.column("l1_pw1_b_2", KD + n)).then_inc(v.s_vgate, 1)
    square(KD - 1)
    act.wait_ge(v.s_vmean, 3)
    act.activation(c.root[:], c.rstd[:], ACT.Sqrt, bias=c.ln_eps[:, 0:1]).then_inc(v.s_vroot, 1)
    for k in range(KD):
        act.wait_ge(v.s_vn, k + 1)
        act.activation(v.out[:, k], v.out[:, k], ACT.Silu, bias=c.column("l1_ln_b_2", k),
                       scale=c.column("l1_ln_w_2", k)).then_inc(v.s_vsilu, 1)
        act.wait_ge(v.s_vsilu, k + 1)
        act.activation(c.xn_hi[:, k], v.out[:, k], ACT.Copy).then_inc(c.s_xhi, 1)


def conv_dve(dve, c, v, base, xhi_base):
    dve.wait_ge(c.s_pe, base + START)
    for b in range(2):
        dve.memset(v.u[:, b, 0:TAPS - 1], 0.0).then_inc(v.s_vload, 16)
    dve.wait_ge(v.s_vload, 48)
    taps = 0
    for n in range(KD):
        u = base + 2 * n
        dve.wait_ge(c.s_pe, u + START + 2)
        dve.wait_ge(v.s_vgate, n + 1)
        dve.scalar_tensor_tensor(out=v.u[:, n % 2, TAPS - 1:], in0=c.ps[:, u % RING], scalar=c.column("l1_pw1_b_2", n),
                                 in1=v.gate[:, n % 2], op0=ALU.add, op1=ALU.mult).then_inc(v.s_vu, 1)
        dve.wait_ge(v.s_vu, n + 1)
        dve.nop().then_inc(c.s_evac, 2)
        for t in range(TAPS):
            acc = v.acc[:, t % 2]
            src, w = v.u[:, n % 2, t:t + T], v.taps[:, n, t:t + 1]
            if t >= 2:
                dve.wait_ge(v.s_vtap, taps - 1)
                dve.scalar_tensor_tensor(out=acc, in0=src, scalar=w, in1=acc, op0=ALU.mult,
                                         op1=ALU.add).then_inc(v.s_vtap, 1)
            elif t == 0:
                dve.tensor_scalar(acc, src, w, c.column("l1_dw_b_2", n), ALU.mult, ALU.add).then_inc(v.s_vtap, 1)
            else:
                dve.tensor_scalar(acc, src, w, None, ALU.mult).then_inc(v.s_vtap, 1)
            taps += 1
        dve.wait_ge(v.s_vtap, taps)
        dve.tensor_tensor(v.out[:, n], v.acc[:, 0], v.acc[:, 1], ALU.add).then_inc(v.s_vout, 1)
        dve.wait_ge(v.s_vout, n + 1)
        if n == 0:
            dve.tensor_copy(v.sum[:], v.out[:, 0]).then_inc(v.s_vsum, 1)
        else:
            dve.tensor_tensor(v.sum[:], v.sum[:], v.out[:, n], ALU.add).then_inc(v.s_vsum, 1)
            conv_square(dve, c, v, n - 1)
    conv_square(dve, c, v, KD - 1)
    dve.wait_ge(v.s_vstat, 1)
    dve.tensor_scalar(v.mean[:], c.ps[:, 5], 1.0 / D, None, ALU.mult).then_inc(v.s_vmean, 1)
    dve.wait_ge(v.s_vmean, 1)
    dve.tensor_tensor(v.sum[:], v.mean[:], v.mean[:], ALU.mult).then_inc(v.s_vmean, 1)
    dve.wait_ge(v.s_vmean, 2)
    dve.scalar_tensor_tensor(out=c.rstd[:], in0=c.ps[:, 6], scalar=1.0 / D, in1=v.sum[:], op0=ALU.mult,
                             op1=ALU.subtract).then_inc(v.s_vmean, 1)
    dve.wait_ge(v.s_vroot, 1)
    dve.reciprocal(c.rstd[:], c.root[:]).then_inc(v.s_vmean, 1)
    dve.wait_ge(v.s_vmean, 4)

    def low(k):
        dve.wait_ge(c.s_xhi, xhi_base + k + 1)
        dve.tensor_tensor(c.xn_lo[:, k], v.out[:, k], c.xn_hi[:, k].bitcast(F32), ALU.subtract).then_inc(c.s_xn, 1)

    for k in range(KD):
        dve.tensor_tensor(v.out[:, k], v.out[:, k], v.mean[:], ALU.subtract).then_inc(v.s_vmean, 1)
        dve.wait_ge(v.s_vmean, 5 + k)
        dve.tensor_tensor(v.out[:, k], v.out[:, k], c.rstd[:], ALU.mult).then_inc(v.s_vn, 1)
        if k >= 1:
            low(k - 1)
    low(KD - 1)


def conv_square(dve, c, v, n):
    dve.wait_ge(v.s_vsq, n + 1)
    dve.wait_ge(v.s_vsum, 2 * n + 1 + (n < KD - 1))
    if n == 0:
        dve.tensor_copy(c.ss[:], c.sq[:, 0]).then_inc(v.s_vsum, 1)
    else:
        dve.tensor_tensor(c.ss[:], c.ss[:], c.sq[:, n % 2], ALU.add).then_inc(v.s_vsum, 1)



def renorm_act(act, c, i):
    norm_act_root(act, c, i)
    for k in range(KD):
        act.wait_ge(c.s_y, KD * i + k + 1)
        act.wait_ge(c.s_ss, KD * (i + 1) + k - 1)
        act.activation(c.sq[:, k % 2], c.x[:, k], ACT.Square).then_inc(c.s_sq, 1)


def renorm_dve(dve, c, i, gain):
    norm_dve_scale(dve, c, i)
    dve.memset(c.ss[:], 0.0).then_inc(c.s_zero, 1)
    dve.wait_ge(c.s_zero, i + 1)
    for k in range(KD):
        dve.scalar_tensor_tensor(out=c.x[:, k], in0=c.x[:, k], scalar=c.column(gain, k), in1=c.rstd[:],
                                 op0=ALU.mult, op1=ALU.mult).then_inc(c.s_y, 1)
    for k in range(KD):
        dve.wait_ge(c.s_sq, KD * (i + 1) + k + 1)
        dve.wait_ge(c.s_ss, KD * (i + 1) + k)
        dve.tensor_tensor(c.ss[:], c.ss[:], c.sq[:, k % 2], ALU.add).then_inc(c.s_ss, 1)



def output_dve(dve, c, i, gain):
    norm_dve_scale(dve, c, i)
    for k in range(KD):
        dve.scalar_tensor_tensor(out=c.x[:, k], in0=c.x[:, k], scalar=c.par[:, COL[gain] + k:COL[gain] + k + 1],
                                 in1=c.rstd[:], op0=ALU.mult, op1=ALU.mult).then_inc(c.s_y, 1)
    for t in range(TT):
        for half in range(2):
            dve.wait_ge(c.s_tout, 2 * t + half + 1)
            dve.tensor_copy(c.stage[:, t, half * 512:half * 512 + 512], c.ps[:, 2 * (t % 2) + half]).then_inc(c.s_out, 1)


def output_pe(pe, c, i):
    for t in range(TT):
        for k in range(KD):
            if t == 0:
                pe.wait_ge(c.s_y, KD * i + k + 1)
            if t >= 2 and k % 4 == 0:
                pe.wait_ge(c.s_out, 2 * (t - 2) + k // 4 + 1)
            mm = pe.transpose(c.ps[:, 2 * (t % 2) + k // 4, k % 4 * P:k % 4 * P + P], c.x[:, k, t * P:t * P + P],
                              c.ident[:])
            if k % 4 == 3:
                mm.then_inc(c.s_tout, 1)


def output_sp(sp, c):
    for t in range(TT):
        sp.wait_ge(c.s_out, 2 * t + 2)
        sp.dma_start(c.out[t], c.stage[:, t]).then_inc(c.s_stored, 16)
    sp.wait_ge(c.s_stored, 16 * TT)


def constants_pool(pool, c):
    pool.memset(c.ident[:], 0.0).then_inc(c.s_zeroed, 1)
    c.zeroed += 1
    pool.wait_ge(c.s_zeroed, 1)
    pool.affine_select(out=c.ident[:], in_=c.ident[:], compare_op=ALU.not_equal, fill=1.0, base=0,
                       pattern=[[-1, P]], channel_multiplier=1).then_inc(c.s_const, 1)
    pool.memset(c.eps[:], EPS).then_inc(c.s_zeroed, 1)
    c.zeroed += 1
    pool.memset(c.ones[:], 1.0).then_inc(c.s_const, 1)


def program(nc, x, weights, params, lora, table, dw, out):
    ctx = ExitStack()
    with ctx:
        def sb(name, shape, dt=F32, scope=ctx):
            return scope.enter_context(nc.sbuf_tensor("sb_" + name, shape, dt))

        def sem(name):
            return ctx.enter_context(nc.semaphore(name))

        c = Parts()
        c.weights, c.lora, c.table, c.dw = weights, lora, table, dw
        c.out = out.rearrange("a (t p) d -> (a t) p d", p=P)
        c.ps = ctx.enter_context(nc.psum_tensor("ps", [P, 8, 512], F32))
        c.x = sb("x", [P, KD, T])
        c.xn_hi = sb("xn_hi", [P, KD, T], F32R)
        c.xn_lo = sb("xn_lo", [P, KD, T], F32R)
        c.w_raw = sb("w_raw", [P, RING, KU, P])
        c.w_hi = sb("w_hi", [P, RING, KU, P], F32R)
        c.w_lo = sb("w_lo", [P, RING, KU, P], F32R)
        c.ident = sb("ident", [P, P])
        c.ones = sb("ones", [P, P])
        c.eps = sb("eps", [P, 1])
        c.par = sb("par", [P, NCOL])
        c.sinks = c.par[:, SINKS:CMP_W2]
        c.dist = sb("dist", [P, T])
        c.dist_local = sb("dist_local", [P, 2 * P])
        c.dist_cmp = sb("dist_cmp", [P, TT, 32])
        c.sees_block = sb("sees_block", [P, 1])
        c.level = sb("level", [P, 7, P], BF16)
        c.mask4 = sb("mask4", [P, 4, P], BF16)
        c.ones_head = sb("ones_head", [P, P])
        c.ident_head = sb("ident_head", [P, HD])
        c.gn_eps = sb("gn_eps", [P, 1])
        c.ln_eps = sb("ln_eps", [P, 1])
        c.omka = sb("omka", [P, 4])
        c.zeroed = 0
        c.ss = sb("ss", [P, T])
        c.rstd = sb("rstd", [P, T])
        c.root = sb("root", [P, T])
        c.y = sb("y", [P, 3, T])
        c.sq = c.y
        with ExitStack() as region:
            c.stage = sb("stage", [P, TT, D], scope=region)
        with ExitStack() as region:
            c.hid_hi = sb("hid_hi", [P, F1A, T], F32R, region)
            c.hid_lo = sb("hid_lo", [P, F1A, T], F32R, region)
            c.gate = sb("gate", [P, 2, T], scope=region)
            c.h = sb("h", [P, 2, T], scope=region)
        with ExitStack() as region:
            with ExitStack() as sub:
                blk = sb("blk", [P, 2, 16, HD], scope=sub)
            m = mixer_tensors(c, lambda name, shape, dt=F32: sb(name, shape, dt, region), sem)
            m.blk = blk
            with ExitStack() as inner:
                m.blk_hi = sb("blk_hi", [P, 2, 16, HD], F32R, inner)
                m.blk_lo = sb("blk_lo", [P, 2, 16, HD], F32R, inner)
                m.sig = sb("sig", [P, T], scope=inner)
            m.chid = c.ss[:, 0:4 * HD].rearrange("p (q n) -> p q n", n=HD)
            flat = lambda ap: ap[:, 0:5].rearrange("p (a k) n -> p a (k n)", a=1)[:, 0].rearrange("p (a n) -> p a n", a=2)
            a = attention_buffers(c, lambda name, shape, dt=F32: sb(name, shape, dt, region), sem, "a_",
                                  m.q[:, 0:16:2], m.q[:, 1:16:2], pt=(flat(c.xn_hi), flat(c.xn_lo)))
        m.w2 = c.par[:, CMP_W2:NCOL].rearrange("p (a t n) -> p a t n", a=2, t=2)
        c.column = lambda name, j: c.par[:, COL[name] + j:COL[name] + j + 1]
        with ExitStack() as region:
            rsb = lambda name, shape, dt=F32: sb(name, shape, dt, region)
            c.o32 = rsb("o32", [P, 4, T])
            with ExitStack() as inner:
                isb = lambda name, shape, dt=F32: sb(name, shape, dt, inner)
                t = att_tensors(c, isb, sem)
                ta = attention_buffers(c, isb, sem, "t0_", o32=c.o32)
                tb = attention_view(ta, c.o32[:, 2:4], sem, "t1_")
            w = rwkv_tensors(c, rsb, sem)
        with ExitStack() as region:
            v = conv_tensors(c, lambda name, shape, dt=F32: sb(name, shape, dt, region), sem)
        c.s_raw = [sem(f"s_raw{i}") for i in range(RING)]
        c.s_hi = sem("s_hi")
        c.s_lo = sem("s_lo")
        c.s_pe = sem("s_pe")
        c.s_evac = sem("s_evac")
        c.s_const = sem("s_const")
        c.s_zeroed = sem("s_zeroed")
        c.s_load = sem("s_load")
        c.s_tin = sem("s_tin")
        c.s_x = sem("s_x")
        c.s_sq = sem("s_sq")
        c.s_ss = sem("s_ss")
        c.s_zero = sem("s_zero")
        c.s_msum = sem("s_msum")
        c.s_root = sem("s_root")
        c.s_rstd = sem("s_rstd")
        c.s_y = sem("s_y")
        c.s_xhi = sem("s_xhi")
        c.s_xn = sem("s_xn")
        c.s_act = sem("s_act")
        c.s_hhi = sem("s_hhi")
        c.s_hid = sem("s_hid")
        c.s_tout = sem("s_tout")
        c.s_out = sem("s_out")
        c.s_stored = sem("s_stored")
        c.s_par = sem("s_par")
        c.s_const2 = sem("s_const2")
        c.s_xb = sem("s_xb")
        block = ctx.enter_context(nc.Block())
        B = BASE

        @block.sync
        def _(sp):
            sp.dma_start(c.stage[:], x.rearrange("a (t p) d -> p (a t) d", p=P)).then_inc(c.s_load, 16)
            sp.dma_start(c.par[:], params).then_inc(c.s_par, 16)
            stream_load(sp, c)
            output_sp(sp, c)

        passes = mixer_passes(c, a, m)

        def hid_ready(pe, base):
            return lambda k: pe.wait_ge(c.s_hid, base + START + k + 1)

        @block.gpsimd
        def _(pool):
            constants_pool(pool, c)
            mixer_constants(pool, c)
            split = min(UNITS, B.get("mix_out", 0) + RING - 1)
            stream_low(pool, c, 0, split)
            rwkv_constants(pool, c)
            stream_low(pool, c, split, UNITS)

        last = 8

        @block.scalar
        def _(act):
            for u in range(RING - 1):
                act.wait_ge(c.s_raw[u], 16)
                act.activation(c.w_hi[:, u], c.w_raw[:, u], ACT.Copy).then_inc(c.s_hi, 1)

            def ffn(name, f, i, nxt):
                norm_act_root(act, c, i)
                norm_act_high(act, c, i)
                glu_up_act(act, c, B[name + "_upA"], F1A, f)
                down_act(act, c, B[name + "_downA"], F1A)
                glu_up_act(act, c, B[name + "_upB"], F1 - F1A, f + F1A)
                down_act(act, c, B[name + "_downB"], F1 - F1A, KD * nxt)

            def mlp(name, i, nxt):
                norm_act_root(act, c, i)
                norm_act_high(act, c, i)
                mlp_up_act(act, c, B[name + "_upA"], F1A)
                down_act(act, c, B[name + "_downA"], F1A)
                mlp_up_act(act, c, B[name + "_upB"], F1A)
                down_act(act, c, B[name + "_downB"], F1A, KD * nxt)

            input_act(act, c)
            ffn("ffn1", 0, 0, 1)
            norm_act_root(act, c, 1)
            norm_act_high(act, c, 1)
            mixer_in_act(act, c, m, B["mix_in"])
            attention_act(act, c, a, passes)
            down_act(act, c, B["mix_out"], KD, 2 * KD)
            ffn("ffn2", F1, 2, 3)
            renorm_act(act, c, 3)
            norm_act_root(act, c, 4)
            norm_act_high(act, c, 4)
            for half, x in ((0, ta), (1, tb)):
                att_in_act(act, c, t, half)
                attention_act(act, c, x, att_passes(c, x, t, half))
            rwkv_act(act, c, w, B["rwkv_in"] + 12)
            down_act(act, c, B["rwkv_out"], KD, 5 * KD)
            mlp("mlp0", 5, 6)
            norm_act_root(act, c, 6)
            norm_act_high(act, c, 6)
            conv_act(act, c, v, B["pw1"])
            down_act(act, c, B["pw2"], KD, 7 * KD)
            mlp("mlp1", 7, 8)
            norm_act_root(act, c, last)

        @block.tensor
        def _(pe):
            def hid_ready(base):
                return lambda k: pe.wait_ge(c.s_hid, base + START + k + 1)

            def ffn(name, f, i, xn):
                norm_pe(pe, c, i)
                up_pe(pe, c, B[name + "_upA"], 2 * F1A, xn)
                down_pe(pe, c, B[name + "_downA"], F1A, c.hid_hi, c.hid_lo, hid_ready(f))
                up_pe(pe, c, B[name + "_upB"], 2 * (F1 - F1A), xn)
                down_pe(pe, c, B[name + "_downB"], F1 - F1A, c.hid_hi, c.hid_lo, hid_ready(f + F1A))

            def mlp(name, f, i, xn):
                norm_pe(pe, c, i)
                up_pe(pe, c, B[name + "_upA"], F1A, xn)
                down_pe(pe, c, B[name + "_downA"], F1A, c.hid_hi, c.hid_lo, hid_ready(f))
                up_pe(pe, c, B[name + "_upB"], F1A, xn)
                down_pe(pe, c, B[name + "_downB"], F1A, c.hid_hi, c.hid_lo, hid_ready(f + F1A))

            input_pe(pe, c)
            ffn("ffn1", 0, 0, 0)
            norm_pe(pe, c, 1)
            mixer_in_pe(pe, c, m, B["mix_in"], KD)
            attention_pe(pe, c, a, passes)
            down_pe(pe, c, B["mix_out"], KD, a.o_hi, a.o_lo, lambda k: pe.wait_ge(a.s_olow, 2 * k + 2))
            ffn("ffn2", F1, 2, 2 * KD)
            norm_pe(pe, c, 3)
            norm_pe(pe, c, 4)
            for half, x in ((0, ta), (1, tb)):
                att_in_pe(pe, c, t, half, 3 * KD)
                attention_pe(pe, c, x, att_passes(c, x, t, half))
            pe.wait_ge(c.s_const2, 1)
            rwkv_pe(pe, c, w, B["rwkv_in"] + 12)
            down_pe(pe, c, B["rwkv_out"], KD, c.xn_hi, c.xn_lo, lambda k: pe.wait_ge(c.s_xn, 4 * KD + k + 1))
            mlp("mlp0", 2 * F1, 5, 5 * KD)
            norm_pe(pe, c, 6)
            conv_pe(pe, c, v, B["pw1"], 6 * KD)
            down_pe(pe, c, B["pw2"], KD, c.xn_hi, c.xn_lo, lambda k: pe.wait_ge(c.s_xn, 7 * KD + k + 1))
            mlp("mlp1", 2 * F1 + F2, 7, 8 * KD)
            norm_pe(pe, c, last)
            output_pe(pe, c, last)

        @block.vector
        def _(dve):
            def ffn(name, f, i, gain, xhi, nxt):
                norm_dve(dve, c, i, gain, xhi, xhi)
                glu_up_dve(dve, c, B[name + "_upA"], F1A, f, f, B[name + "_upA"])
                down_dve(dve, c, B[name + "_downA"], F1A, 0.5)
                glu_up_dve(dve, c, B[name + "_upB"], F1 - F1A, f + F1A, f + F1A, B[name + "_upB"])
                down_dve(dve, c, B[name + "_downB"], F1 - F1A, 0.5, KD * nxt)

            def mlp(name, f, i, gain, xhi, xn, nxt):
                norm_dve(dve, c, i, gain, xhi, xn)
                mlp_up_dve(dve, c, B[name + "_upA"], F1A, f, f)
                down_dve(dve, c, B[name + "_downA"], F1A, 1.0)
                mlp_up_dve(dve, c, B[name + "_upB"], F1A, f + F1A, f + F1A)
                down_dve(dve, c, B[name + "_downB"], F1A, 1.0, KD * nxt)

            input_dve(dve, c)
            for k in range(KD):
                add_square(dve, c, k, k)
            dve.wait_ge(c.s_par, 16)
            ffn("ffn1", 0, 0, "ffn1_norm", 0, 1)
            norm_dve(dve, c, 1, "mix_norm", KD, KD)
            mixer_in_dve(dve, c, m, B["mix_in"])
            attention_dve(dve, c, a, passes)
            down_dve(dve, c, B["mix_out"], KD, 1.0, 2 * KD)
            ffn("ffn2", F1, 2, "ffn2_norm", 2 * KD, 3)
            renorm_dve(dve, c, 3, "final_norm")
            norm_dve(dve, c, 4, "l0_norm_mix_2", 3 * KD, 3 * KD)
            for half, x in ((0, ta), (1, tb)):
                att_in_dve(dve, c, t, half)
                attention_dve(dve, c, x, att_passes(c, x, t, half))
            dve.wait_ge(c.s_const2, 1)
            rwkv_dve(dve, c, w, B["rwkv_in"] + 12)
            down_dve(dve, c, B["rwkv_out"], KD, 1.0, 5 * KD)
            mlp("mlp0", 2 * F1, 5, "l0_norm_ffn_2", 4 * KD, 5 * KD, 6)
            norm_dve(dve, c, 6, "l1_norm_mix_2", 5 * KD, 6 * KD)
            conv_dve(dve, c, v, B["pw1"], 6 * KD)
            down_dve(dve, c, B["pw2"], KD, 1.0, 7 * KD, bias="l1_pw2_b_2")
            mlp("mlp1", 2 * F1 + F2, 7, "l1_norm_ffn_2", 7 * KD, 8 * KD, 8)
            output_dve(dve, c, last, "final_norm_2")



def weight_units(a):
    units = np.zeros((UNITS, P, KU, P), np.float32)
    at = [0]

    def put(block):
        rows, cols = block.shape
        kt = rows // P
        units[at[0], :, 0:kt, 0:cols] = block.reshape(kt, P, cols).transpose(1, 0, 2)
        at[0] += 1

    def ffn(up, gated, down):
        tiles = down.shape[0] // P
        for lo in range(0, tiles, F1A):
            hi = min(tiles, lo + F1A)
            for f in range(lo, hi):
                put(up[:, f * P:f * P + P])
                if gated:
                    put(up[:, (tiles + f) * P:(tiles + f) * P + P])
            for n in range(KD):
                for k in range(lo, hi, KU):
                    put(down[k * P:min(k + KU, hi) * P, n * P:n * P + P])

    ffn(a["ffn1_w_in"][0], True, a["ffn1_w_out"][0])
    w = a["w_mix_in"][0]
    pair = lambda off, j: np.concatenate([w[:, off + HD * h:off + HD * h + HD] for h in (j, j + 4)], 1)
    kv = lambda i: w[:, 512 + i * P:512 + i * P + P]
    tiles = {"kc": kv(0), "vc": kv(1), "ks": kv(2), "kw": kv(4), "kb": w[:, 1816:1816 + P],
             "vs": kv(3), "vw": kv(5), "vb": w[:, 1944:1944 + P], "gate": w[:, 1280:1304]}
    for j in range(4):
        tiles[f"qa{j}"], tiles[f"qb{j}"] = pair(0, j), pair(1304, j)
    for unit in MIX_UNITS:
        if unit in tiles:
            put(tiles[unit])
        else:
            q, half = unit
            hidden = a["cmp_k_w1" if q < 2 else "cmp_v_w1"][0]
            put(hidden[half * D:half * D + D, q % 2 * P:q % 2 * P + P])
    rows = np.concatenate([np.arange(HD) + off + HD * h for off in (0, 512) for j in range(4) for h in (j, j + 4)])
    for n in range(KD):
        put(a["w_mix_out"][0][rows, n * P:n * P + P])
    ffn(a["ffn2_w_in"][0], True, a["ffn2_w_out"][0])
    w = a["l0_w_in_2"]
    tile = lambda t: put(w[:, t * P:t * P + P])
    for half in range(2):
        for off in (14, 18, 22):
            tile(off + 2 * half), tile(off + 2 * half + 1)
    tile(12), tile(13)
    for j in range(PAIRS):
        tile(j), tile(4 + j), tile(8 + j)
    for n in range(KD):
        put(a["l0_w_out_2"][:, n * P:n * P + P])
    ffn(a["l0_ffn_up_2"], False, a["l0_ffn_down_2"])
    for n in range(KD):
        for off in (0, D):
            put(a["l1_pw1_2"][:, off + n * P:off + n * P + P])
    for n in range(KD):
        put(a["l1_pw2_2"][:, n * P:n * P + P])
    ffn(a["l1_ffn_up_2"], False, a["l1_ffn_down_2"])
    assert at[0] == UNITS
    return units.reshape(UNITS, P, KU, P)


def parameter_columns(a):
    columns = [a[name].reshape(n, P).T for name, n in VECTORS]
    columns.append(np.broadcast_to(a["swa_sinks"].reshape(1, 8), (P, 8)))
    columns += [a[name][0].reshape(2, P, HD).transpose(1, 0, 2).reshape(P, 2 * HD) for name in ("cmp_k_w2", "cmp_v_w2")]
    return np.concatenate(columns, 1)


def bias_rows(table):
    distance = T - P + np.arange(P)[:, None] - np.arange(T)[None, :]
    return np.ascontiguousarray(table[:, np.minimum(distance, MAX_REL) + MAX_REL])


def kernel(**inputs):
    import concourse.bacc as bacc
    from concourse.bass_utils import run_bass_kernel_spmd

    a = {name: np.ascontiguousarray(v) for name, v in inputs.items()}
    arrays = {"x": a["x"], "weights": weight_units(a), "params": np.ascontiguousarray(parameter_columns(a)),
              "lora": np.concatenate([a["l0_w2_2"], a["l0_a2_2"], a["l0_g2_2"]], 0),
              "table": bias_rows(a["l0_rel_bias_2"]),
              "dw": np.ascontiguousarray(a["l1_dw_2"].reshape(TAPS, KD, P).transpose(2, 1, 0))}
    nc = bacc.Bacc("TRN2", target_bir_lowering=False, num_devices=1)
    args = [nc.dram_tensor(n, v.shape, mybir.dt.from_np(v.dtype), kind="ExternalInput").ap() for n, v in arrays.items()]
    out = nc.dram_tensor("out", (1, T, D), F32, kind="ExternalOutput").ap()
    program(nc, *args, out)
    r = run_bass_kernel_spmd(nc, [arrays], core_ids=[0])
    return r.results[0]["out"]
```

```python
from contextlib import ExitStack

import numpy as np
import concourse.bass as bass
from concourse import mybir

F32 = mybir.dt.float32
F32R = mybir.dt.float32r
BF16 = mybir.dt.bfloat16
ALU = mybir.AluOpType
ACT = mybir.ActivationFunctionType

P = 128
T = 512
D = 1024
KD = D // P
TT = T // P
HD = 64
KU = 8
RING = 4
F1 = 2816 // P
F1A = 16
F2 = 4096 // P
EPS = 1e-6
LN_EPS = 1e-5

START = RING


def stream_plan():
    at, base = 0, {}
    for name, n in (
        ("ffn1_upA", 2 * F1A), ("ffn1_downA", KD * 2), ("ffn1_upB", 2 * (F1 - F1A)), ("ffn1_downB", KD),
        ("mix_in", 25), ("mix_out", KD),
        ("ffn2_upA", 2 * F1A), ("ffn2_downA", KD * 2), ("ffn2_upB", 2 * (F1 - F1A)), ("ffn2_downB", KD),
        ("rwkv_in", 26), ("rwkv_out", KD),
        ("mlp0_upA", 16), ("mlp0_downA", KD * 2), ("mlp0_upB", 16), ("mlp0_downB", KD * 2),
        ("pw1", 28), ("pw2", KD),
        ("mlp1_upA", 16), ("mlp1_downA", KD * 2), ("mlp1_upB", 16), ("mlp1_downB", KD * 2),
    ):
        base[name] = at
        at += n
    base["end"] = at
    return base


BASE = stream_plan()
UNITS = BASE["end"]

VECTORS = (
    ("ffn1_norm", 8), ("mix_norm", 8), ("ffn2_norm", 8), ("final_norm", 8),
    ("l0_norm_mix_2", 8), ("l0_norm_ffn_2", 8), ("l1_norm_mix_2", 8), ("l1_norm_ffn_2", 8),
    ("final_norm_2", 8), ("l0_shift_mu_2", 14), ("l0_w0_2", 4), ("l0_a0_2", 4), ("l0_k_k_2", 4),
    ("l0_k_a_2", 4), ("l0_r_k_2", 4), ("l0_lnx_w_2", 4), ("l0_lnx_b_2", 4), ("l1_pw1_b_2", 16),
    ("l1_dw_b_2", 8), ("l1_ln_w_2", 8), ("l1_ln_b_2", 8), ("l1_pw2_b_2", 8),
    ("cmp_k_b1", 2), ("cmp_v_b1", 2), ("cmp_k_pos", 16), ("cmp_v_pos", 16),
)
COL = {}
for _name, _n in VECTORS:
    COL[_name] = sum(n for _, n in VECTORS[:len(COL)])
NVEC = sum(n for _, n in VECTORS)
SINKS = NVEC
CMP_W2 = SINKS + 8
NCOL = CMP_W2 + 2 * 2 * HD


class Parts:
    pass



def stream_load(sp, c):
    def load(u, slot):
        sp.dma_start(c.w_raw[:, slot], c.weights[u]).then_inc(c.s_raw[slot], 16)

    for u in range(RING):
        load(u, u)
    with sp.Fori(1, UNITS // RING) as i:
        for slot in range(RING):
            sp.wait_ge(c.s_lo, i * RING + (slot + 1 - RING))
            load(i * RING + slot, slot)
    for u in range(UNITS // RING * RING, UNITS):
        sp.wait_ge(c.s_lo, u + 1 - RING)
        load(u, u % RING)


def stream_high(act, c, u, slot, turn):
    act.wait_ge(c.s_raw[slot], turn * 16 + 16)
    act.wait_ge(c.s_pe, u + START + 1 - RING)
    act.activation(c.w_hi[:, slot], c.w_raw[:, slot], ACT.Copy).then_inc(c.s_hi, 1)


def stream_high_ahead(act, c, i, base, s):
    ahead = base + s + RING - 1
    stream_high(act, c, i * RING + ahead, ahead % RING, i + ahead // RING)


def stream_low(pool, c, first, end):
    def low(u, slot):
        pool.wait_ge(c.s_hi, u + 1)
        pool.tensor_tensor(c.w_lo[:, slot], c.w_raw[:, slot], c.w_hi[:, slot].bitcast(F32),
                           ALU.subtract).then_inc(c.s_lo, 1)

    turns = (end - first) // RING
    if turns > 0:
        with pool.Fori(0, turns) as i:
            for s in range(RING):
                low(i * RING + (first + s), (first + s) % RING)
    for u in range(first + turns * RING, end):
        low(u, u % RING)


def split_products(pe, c, out, slot, rhs_hi, rhs_lo, kts, k0=0, start=True, stop=True, before=None, cols=P):
    for k in kts:
        if before is not None:
            before(k)
        hi, lo = c.w_hi[:, slot, k, 0:cols], c.w_lo[:, slot, k, 0:cols]
        first, last = start and k == kts[0], stop and k == kts[-1]
        pe.matmul(out, hi, rhs_hi(k0 + k), start=first, stop=False)
        pe.matmul(out, hi, rhs_lo(k0 + k), start=False, stop=False)
        mm = pe.matmul(out, lo, rhs_hi(k0 + k), start=False, stop=last)
    return mm


def first_two_units(pe, c, u, rhs_hi, rhs_lo, before):
    pe.wait_ge(c.s_lo, u + 2)
    pe.wait_ge(c.s_evac, u + START + 2 - RING)
    for k in range(KU):
        before(k)
        for x in range(2):
            mm = split_products(pe, c, c.ps[:, (u + x) % RING], (u + x) % RING, rhs_hi, rhs_lo, range(k, k + 1),
                                start=k == 0, stop=k == KU - 1)
            if k == KU - 1:
                mm.then_inc(c.s_pe, 1)



def input_pe(pe, c):
    pe.wait_ge(c.s_const, 1)
    for t in range(TT):
        pe.wait_ge(c.s_load[t], 16)
        for k in range(KD):
            mm = pe.transpose(c.ps[:, k, t * P:(t + 1) * P], c.stage[:, t, k * P:(k + 1) * P], c.ident[:])
            if t == TT - 1:
                mm.then_inc(c.s_tin, 1) if k < KD - 1 else mm.then_inc(c.s_pe, START)


def input_dve(dve, c):
    for k in range(KD):
        dve.wait_ge(c.s_tin, k + 1) if k < KD - 1 else dve.wait_ge(c.s_pe, START)
        op = dve.tensor_copy(c.x[:, k], c.ps[:, k])
        op.then_inc(c.s_x, 1) if k < KD - 1 else op.then_inc(c.s_evac, START)
    dve.wait_ge(c.s_evac, START)
    dve.nop().then_inc(c.s_x, 1)
    dve.nop().then_inc(c.s_hid, START)
    dve.nop().then_inc(c.s_ss, KD)


def input_act(act, c):
    for t in range(TT):
        act.wait_ge(c.s_load[t], 16)
        if t >= 1:
            act.wait_ge(c.s_sum_t, t)
        act.activation(c.y[:, 0:2].rearrange("p a n -> p (a n)"), c.stage[:, t], ACT.Square,
                       accum_out=c.sum_t[:, t:t + 1]).then_inc(c.s_sum_t, 1)
    act.nop().then_inc(c.s_sq, KD)



def norm_pe(pe, c, i):
    if i == 0:
        pe.wait_ge(c.s_evac, START)
    else:
        pe.wait_ge(c.s_const, 2)
        pe.wait_ge(c.s_root, i)
        pe.wait_ge(c.s_ss, KD * (i + 1))
        for t in range(TT):
            mm = pe.matmul(c.ps[:, 4, t:t + 1], c.ss[:, t * P:t * P + P], c.ones[:, 0:1], start=True, stop=True)
        mm.then_inc(c.s_msum, 1)
    pe.wait_ge(c.s_rstd, i + 1)
    if i >= 1:
        pe.wait_ge(c.s_y, KD * i)
    token_values_pe(pe, c, 5, c.rstd_t).then_inc(c.s_spread, 1)


def token_values_pe(pe, c, bank, values):
    for t in range(TT):
        mm = pe.matmul(c.ps[:, bank, t * P:t * P + P], values[:, t:t + 1].broadcast_to([P, P]), c.ident[:],
                       start=True, stop=True)
    return mm


def norm_act_root(act, c, i):
    if i == 0:
        act.wait_ge(c.s_zeroed, 2)
        act.wait_ge(c.s_sum_t, TT)
    else:
        act.wait_ge(c.s_msum, i)
    act.activation(c.root_t[:], c.sum_t[:] if i == 0 else c.ps[:, 4, 0:TT], ACT.Sqrt, bias=c.eps[:, 0:1], scale=1.0 / D).then_inc(c.s_root, 1)


def norm_act_high(act, c, i):
    for k in range(KD):
        act.wait_ge(c.s_y, KD * i + k + 1)
        act.activation(c.xn_hi[:, k], c.y[:, k % 3], ACT.Copy).then_inc(c.s_xhi, 1)


def norm_dve_scale(dve, c, i):
    dve.wait_ge(c.s_root, i + 1)
    dve.reciprocal(c.rstd_t[:], c.root_t[:]).then_inc(c.s_rstd, 1)
    dve.wait_ge(c.s_spread, i + 1)


def norm_dve(dve, c, i, gain, xhi, xn):
    norm_dve_scale(dve, c, i)

    def low(k):
        dve.wait_ge(c.s_xhi, xhi + k + 1)
        dve.tensor_tensor(c.xn_lo[:, k], c.y[:, k % 3], c.xn_hi[:, k].bitcast(F32),
                          ALU.subtract).then_inc(c.s_xn, 1)

    for k in range(KD):
        if k >= 3:
            dve.wait_ge(c.s_xn, xn + k - 2)
        dve.scalar_tensor_tensor(out=c.y[:, k % 3], in0=c.x[:, k], scalar=c.par[:, COL[gain] + k:COL[gain] + k + 1],
                                 in1=c.ps[:, 5], op0=ALU.mult, op1=ALU.mult).then_inc(c.s_y, 1)
        if k >= 1:
            low(k - 1)
    low(KD - 1)



def up_pe(pe, c, base, units, xn_ready, first):
    hi, lo = (lambda k: c.xn_hi[:, k]), (lambda k: c.xn_lo[:, k])

    def turn(i, slots):
        for s in slots:
            u, slot = base + s, (base + s) % RING
            pe.wait_ge(c.s_lo, i * RING + (u + 1))
            pe.wait_ge(c.s_evac, i * RING + (u + START + 1 - RING))
            split_products(pe, c, c.ps[:, slot], slot, hi, lo, range(KD)).then_inc(c.s_pe, 1)

    if first:
        first_two_units(pe, c, base, hi, lo, lambda k: pe.wait_ge(c.s_xn, xn_ready + k + 1))
        turn(0, range(2, RING))
    with pe.Fori(1 if first else 0, units // RING) as i:
        turn(i, range(RING))


def glu_up_act(act, c, base, nf, hid_base):
    with act.Fori(0, nf // 2) as i:
        for s in range(RING):
            u, slot = base + s, (base + s) % RING
            stream_high_ahead(act, c, i, base, s)
            if s % 2 == 0:
                act.wait_ge(c.s_pe, i * RING + (u + START + 1))
                act.wait_ge(c.s_evac, i * RING + (u + START - 2))
                act.activation(c.gate[:, s // 2], c.ps[:, slot], ACT.Silu).then_inc(c.s_act, 1)


def glu_up_dve(dve, c, base, nf, hid_base, act_base, free_pe):
    dve.wait_ge(c.s_pe, free_pe + START)
    with dve.Fori(0, nf // 2) as i:
        for f in range(2):
            u = base + 2 * f + 1
            dve.wait_ge(c.s_pe, i * RING + (u + START + 1))
            dve.wait_ge(c.s_act, i * 2 + (act_base + f + 1))
            dve.wait_ge(c.s_hid, i * 2 + (hid_base + START + f - 1))
            dve.tensor_tensor(c.h[:, f], c.gate[:, f], c.ps[:, u % RING], ALU.mult).then_inc(c.s_evac, 2)
            dve.wait_ge(c.s_evac, i * RING + (u + START + 1))
            hidden_parts(dve, c, i, f, hid_base)


def hidden_parts(dve, c, i, f, hid_base):
    dve.tensor_copy(c.hid_hi[:, i * 2 + f], c.h[:, f]).then_inc(c.s_hhi, 1)
    dve.wait_ge(c.s_hhi, i * 2 + (hid_base + f + 1))
    dve.tensor_tensor(c.hid_lo[:, i * 2 + f], c.h[:, f], c.hid_hi[:, i * 2 + f].bitcast(F32),
                      ALU.subtract).then_inc(c.s_hid, 1)


def down_pe(pe, c, base, nk, hi, lo, ready, together=False):
    per = -(-nk // KU)

    def turn(i, slots, ready):
        for s in slots:
            u, g = base + s, s % per
            bank = (u - g) % RING
            pe.wait_ge(c.s_lo, i * RING + (u + 1))
            if g == 0:
                pe.wait_ge(c.s_evac, i * RING + (u + START + 1 - RING))
            split_products(pe, c, c.ps[:, bank], u % RING, lambda k: hi[:, k], lambda k: lo[:, k],
                           range(min(KU, nk - g * KU)), k0=g * KU, start=g == 0, stop=g == per - 1,
                           before=(lambda k: ready(g * KU + k)) if ready is not None and s < per else None,
                           ).then_inc(c.s_pe, 1)

    if together:
        first_two_units(pe, c, base, lambda k: hi[:, k], lambda k: lo[:, k], ready)
        turn(0, range(2, RING), None)
    with pe.Fori(1 if together else 0, KD * per // RING) as i:
        turn(i, range(RING), None if together else ready)


def down_act(act, c, base, nk, sq_base=None):
    per = -(-nk // KU)
    turns = KD * per // RING

    def turn(i, last):
        for s in range(RING):
            u = base + s
            if not last or i * RING + u + RING - 1 < UNITS:
                stream_high_ahead(act, c, i, base, s)
            if sq_base is not None and s % per == per - 1:
                n = s // per
                act.wait_ge(c.s_evac, i * RING + (u + START + 1))
                act.wait_ge(c.s_ss, i * (RING // per) + (sq_base + n - 1))
                act.activation(c.sq[:, n % 2], c.x[:, i * (RING // per) + n], ACT.Square).then_inc(c.s_sq, 1)

    ends = base + KD * per == UNITS
    with act.Fori(0, turns - ends) as i:
        turn(i, False)
    if ends:
        turn(turns - 1, True)


def down_dve(dve, c, base, nk, coef, sq_base=None, bias=None):
    per = -(-nk // KU)
    if bias is not None:
        for k in range(KD):
            dve.tensor_scalar(c.x[:, k], c.x[:, k], c.column(bias, k), None, ALU.add).then_inc(c.s_xb, 1)
        dve.wait_ge(c.s_xb, KD)
    if sq_base is not None:
        dve.memset(c.ss[:], 0.0).then_inc(c.s_zero, 1)
        dve.wait_ge(c.s_zero, sq_base // KD)
    with dve.Fori(0, KD * per // RING) as i:
        for s in range(per - 1, RING, per):
            u, n = base + s, s // per
            tile = i * (RING // per) + n
            dve.wait_ge(c.s_pe, i * RING + (u + START + 1))
            dve.scalar_tensor_tensor(out=c.x[:, tile], in0=c.ps[:, (u + 1 - per) % RING], scalar=coef,
                                     in1=c.x[:, tile], op0=ALU.mult, op1=ALU.add).then_inc(c.s_evac, per)
            if sq_base is not None:
                dve.wait_ge(c.s_sq, i * (RING // per) + (sq_base + n + 1))
                dve.wait_ge(c.s_ss, i * (RING // per) + (sq_base + n))
                dve.tensor_tensor(c.ss[:], c.ss[:], c.sq[:, n % 2], ALU.add).then_inc(c.s_ss, 1)



class Kind:

    def __init__(self, first, width, rows, turned, banks):
        self.first, self.width, self.rows, self.turned, self.banks = first, width, rows, turned, banks


class Pass:

    def __init__(self, kind, q, k_hi, k_lo, v_hi, v_lo, side, tile, bias, prepare_dve=None, start=-3e38,
                 table_used=None, sink=None, gate=None, row_mask=None, opens=False, closes=False, pair_done=False,
                 o_before=0):
        self.kind, self.side, self.tile = kind, side, tile
        self.q, self.k_hi, self.k_lo, self.v_hi, self.v_lo = q, k_hi, k_lo, v_hi, v_lo
        self.bias, self.prepare_dve, self.start = bias, prepare_dve, start
        self.table_used, self.sink, self.gate, self.row_mask = table_used, sink, gate, row_mask
        self.opens, self.closes, self.pair_done, self.o_before = opens, closes, pair_done, o_before


FULL = Kind(
    first=(0, 0, 0, 0), width=(128, 256, 384, 512), rows=P,
    turned=((0, 0, 0, 0, 4), (1, 1, 0, 1, 4), (3, 1, 384, 3, 4), (2, 2, 0, 2, 4)), banks=(512, 512, 256))
LOCAL = Kind(
    first=(0, 0, 1, 2), width=(128, 256, 256, 256), rows=P,
    turned=((0, 0, 0, 0, 2), (1, 0, 256, 1, 3), (2, 1, 0, 2, 4), (3, 1, 256, 3, 4)), banks=(512, 384))
BLOCKS = Kind(
    first=(0, 0, 0, 0), width=(32, 32, 32, 32), rows=32,
    turned=((0, 0, 0, 0, 4),), banks=(512,))
S_BANKS, T_BANK, O_BANK = (0, 1, 5), 2, 6
SCALE = HD ** -0.5


def score_tile(c, i, width):
    at = 256 if i == 1 else 0
    return c.ps[:, S_BANKS[max(i, 1) - 1], at:at + width]


def at_column(kind, i):
    return sum(kind.width[:i])


def passes_before(passes):
    out = [0]
    for p in passes:
        out.append(out[-1] + len(p.kind.banks))
    return out


def attention_pe(pe, c, a, passes):
    n_banks = passes_before(passes)

    def scores(n):
        if n >= len(passes):
            return
        p = passes[n]
        for i in range(TT):
            if n >= 1:
                pe.wait_ge(a.s_max, TT * (n - 1) + max(i, 1) + 1)
            width = p.kind.width[i] if p.kind is BLOCKS else max(p.kind.width[i], 256)
            out = score_tile(c, i, width)
            keys = slice(p.kind.first[i] * P, p.kind.first[i] * P + width)
            q = p.q[:, i * P:i * P + P]
            pe.matmul(out, q, p.k_hi[:, keys], start=True, stop=False)
            pe.matmul(out, q, p.k_lo[:, keys], start=False, stop=True).then_inc(a.s_scores, 1)

    def turn(n):
        p = passes[n]
        for bank in range(len(p.kind.banks)):
            if n >= 1:
                pe.wait_ge(a.s_low, n_banks[n - 1] + min(bank + 1, len(passes[n - 1].kind.banks)))
            for key, b, col, q0, q1 in p.kind.turned:
                if b != bank:
                    continue
                for i in range(q0, q1):
                    pe.wait_ge(a.s_scaled, TT * n + i + 1)
                    at = at_column(p.kind, i) + (key - p.kind.first[i]) * P
                    mm = pe.matmul(c.ps[0:p.kind.rows, T_BANK + bank, col + (i - q0) * P:col + (i - q0) * P + P],
                                   a.p[:, n % 3, at:at + p.kind.rows], a.diagonal[:, n % 2, i], start=True, stop=True)
            mm.then_inc(a.s_turned, 1)

    def values(n):
        p = passes[n]
        out = c.ps[:, O_BANK + p.side]
        if p.opens and p.o_before > 0:
            pe.wait_ge(a.s_olow, p.o_before)
        first = p.opens
        for x, (key, b, col, q0, q1) in enumerate(p.kind.turned):
            pe.wait_ge(a.s_low, n_banks[n] + b + 1)
            w = slice(b * 512 + col, b * 512 + col + (q1 - q0) * P)
            rows = slice(0, p.kind.rows)
            for v, w_part in ((p.v_hi, a.pt_hi), (p.v_hi, a.pt_lo), (p.v_lo, a.pt_hi)):
                mm = pe.matmul(out[:, q0 * P:q1 * P], v(key), w_part[rows, n % 2, w], start=first,
                               stop=p.closes and x == len(p.kind.turned) - 1 and v is p.v_lo, skip_group_check=True)
                first = False
        mm.then_inc(a.s_values, 1)

    scores(0)
    scores(1)
    for n in range(-1, len(passes)):
        scores(n + 3)
        if n + 1 < len(passes):
            turn(n + 1)
        if n >= 0:
            values(n)


def attention_act(act, c, a, passes):
    n_banks = passes_before(passes)

    def softmax(n):
        p = passes[n]
        act.wait_ge(a.s_negmax, n + 1)
        if p.table_used is not None:
            p.table_used(act)
        for i in range(TT):
            at = slice(at_column(p.kind, i), at_column(p.kind, i) + p.kind.width[i])
            act.activation(a.p[:, n % 3, at], a.p[:, n % 3, at], ACT.Exp, bias=a.negmax[:, n % 2, i:i + 1],
                           scale=SCALE, accum_out=a.sums[:, n % 2, i:i + 1]).then_inc(a.s_exp, 1)
        if p.sink is not None:
            act.activation(a.sink_exp[:, n % 2], a.negmax[:, n % 2], ACT.Exp, bias=p.sink, scale=1.0).then_inc(a.s_sinkexp, 1)

    def high(n):
        p = passes[n]
        for b, width in enumerate(p.kind.banks):
            act.wait_ge(a.s_turned, n_banks[n] + b + 1)
            if n >= 2 and b == 0:
                act.wait_ge(a.s_values, n - 1)
            act.activation(a.pt_hi[0:p.kind.rows, n % 2, b * 512:b * 512 + width],
                           c.ps[0:p.kind.rows, T_BANK + b, 0:width], ACT.Copy).then_inc(a.s_high, 1)

    def outputs(n):
        p = passes[n]
        if not p.pair_done:
            return
        act.wait_ge(a.s_values, n + 1)
        for side in range(2):
            rows = slice(side * HD, side * HD + HD)
            if a.o32 is not None:
                act.activation(a.o32[rows, p.tile], c.ps[rows, O_BANK + side], ACT.Copy).then_inc(a.s_olow, 1)
                continue
            act.activation(a.o_hi[rows, p.tile], c.ps[rows, O_BANK + side], ACT.Copy).then_inc(a.s_ohigh, 1)

    softmax(0)
    for n in range(-1, len(passes)):
        if n >= 0:
            high(n)
        if n + 2 < len(passes):
            softmax(n + 2)
        if n >= 1:
            outputs(n - 1)
    outputs(len(passes) - 1)


def attention_dve(dve, c, a, passes):
    n_banks = passes_before(passes)
    pairs = 0
    sinks = 0

    def maxima(n):
        p = passes[n]
        if p.prepare_dve is not None:
            p.prepare_dve(dve)
        if n >= 3:
            dve.wait_ge(a.s_turned, n_banks[n - 2])
        for i in range(TT):
            dve.wait_ge(a.s_scores, TT * n + max(i, 1) + 1)
            at = slice(at_column(p.kind, i), at_column(p.kind, i) + p.kind.width[i])
            dve.tensor_tensor_reduce(out=a.p[:, n % 3, at], in0=score_tile(c, i, p.kind.width[i]),
                                     in1=p.bias(i), scale=1.0, scalar=p.start, op0=ALU.add, op1=ALU.max,
                                     accum_out=a.maxima[:, n % 2, i:i + 1]).then_inc(a.s_max, 1)
        dve.wait_ge(a.s_max, TT * n + TT)
        dve.tensor_scalar(a.negmax[:, n % 2], a.maxima[:, n % 2], -SCALE, None, ALU.mult).then_inc(a.s_negmax, 1)

    def scale(n):
        nonlocal sinks
        p = passes[n]
        dve.wait_ge(a.s_exp, TT * n + TT)
        if p.sink is not None:
            sinks += 1
            dve.wait_ge(a.s_sinkexp, sinks)
            dve.tensor_tensor(a.sums[:, n % 2], a.sums[:, n % 2], a.sink_exp[:, n % 2], ALU.add).then_inc(a.s_sum, 1)
            dve.wait_ge(a.s_sum, sinks)
        dve.reciprocal(a.scale[:, n % 2], a.sums[:, n % 2]).then_inc(a.s_recip, 1)
        dve.wait_ge(a.s_recip, n + 1)
        gated = passes_gated[n]
        if p.gate is not None:
            dve.tensor_tensor(a.scale[:, n % 2], a.scale[:, n % 2], p.gate, ALU.mult).then_inc(a.s_gated, 1)
            dve.wait_ge(a.s_gated, gated)
        if p.row_mask is not None:
            dve.tensor_tensor(a.scale[:, n % 2, 0:1], a.scale[:, n % 2, 0:1], p.row_mask, ALU.mult).then_inc(a.s_rows, 1)
            dve.wait_ge(a.s_rows, passes_masked[n])
        for i in range(TT):
            dve.tensor_scalar(a.diagonal[:, n % 2, i], c.ident[:], a.scale[:, n % 2, i:i + 1], None,
                              ALU.mult).then_inc(a.s_scaled, 1)

    def low(n):
        p = passes[n]
        for b, width in enumerate(p.kind.banks):
            dve.wait_ge(a.s_high, n_banks[n] + b + 1)
            at = slice(b * 512, b * 512 + width)
            dve.tensor_tensor(a.pt_lo[0:p.kind.rows, n % 2, at], c.ps[0:p.kind.rows, T_BANK + b, 0:width],
                              a.pt_hi[0:p.kind.rows, n % 2, at].bitcast(F32), ALU.subtract).then_inc(a.s_low, 1)

    def outputs(n):
        nonlocal pairs
        p = passes[n]
        if not p.pair_done or a.o32 is not None:
            return
        for side in range(2):
            rows = slice(side * HD, side * HD + HD)
            dve.wait_ge(a.s_ohigh, 2 * pairs + side + 1)
            dve.tensor_tensor(a.o_lo[rows, p.tile], c.ps[rows, O_BANK + side], a.o_hi[rows, p.tile].bitcast(F32),
                              ALU.subtract).then_inc(a.s_olow, 1)
        pairs += 1

    passes_gated = [sum(q.gate is not None for q in passes[:n + 1]) for n in range(len(passes))]
    passes_masked = [sum(q.row_mask is not None for q in passes[:n + 1]) for n in range(len(passes))]
    maxima(0)
    for n in range(-1, len(passes)):
        if n + 2 < len(passes):
            maxima(n + 2)
        if n >= 0:
            low(n)
        if n + 1 < len(passes):
            scale(n + 1)
        if n >= 1:
            outputs(n - 1)
    outputs(len(passes) - 1)


def attention_buffers(c, sb, sem, tag, o_hi=None, o_lo=None, o32=None, pt=None):
    a = Parts()
    a.o_hi, a.o_lo, a.o32 = o_hi, o_lo, o32
    a.p = sb(tag + "p", [P, 3, 1280])
    a.diagonal = c.y[:, 0:2].rearrange("p a (t n) -> p a t n", n=P)
    if pt is None:
        a.pt_hi = sb(tag + "pt_hi", [P, 2, 1280], F32R)
        a.pt_lo = sb(tag + "pt_lo", [P, 2, 1280], F32R)
    else:
        a.pt_hi, a.pt_lo = pt
    a.maxima = sb(tag + "maxima", [P, 2, TT])
    a.negmax = sb(tag + "negmax", [P, 2, TT])
    a.sums = sb(tag + "sums", [P, 2, TT])
    a.scale = sb(tag + "scale", [P, 2, TT])
    a.sink_exp = sb(tag + "sink_exp", [P, 2, TT])
    attention_semaphores(a, sem, tag)
    return a


def attention_view(a, o32, sem, tag):
    b = Parts()
    b.o_hi, b.o_lo, b.o32 = a.o_hi, a.o_lo, o32
    b.p, b.diagonal, b.pt_hi, b.pt_lo = a.p, a.diagonal, a.pt_hi, a.pt_lo
    b.maxima, b.negmax, b.sums, b.scale, b.sink_exp = a.maxima, a.negmax, a.sums, a.scale, a.sink_exp
    attention_semaphores(b, sem, tag)
    return b


def attention_semaphores(a, sem, tag):
    a.s_scores = sem(tag + "s_scores")
    a.s_max = sem(tag + "s_max")
    a.s_negmax = sem(tag + "s_negmax")
    a.s_exp = sem(tag + "s_exp")
    a.s_sinkexp = sem(tag + "s_sinkexp")
    a.s_sum = sem(tag + "s_sum")
    a.s_recip = sem(tag + "s_recip")
    a.s_gated = sem(tag + "s_gated")
    a.s_rows = sem(tag + "s_rows")
    a.s_scaled = sem(tag + "s_scaled")
    a.s_turned = sem(tag + "s_turned")
    a.s_high = sem(tag + "s_high")
    a.s_low = sem(tag + "s_low")
    a.s_values = sem(tag + "s_values")
    a.s_ohigh = sem(tag + "s_ohigh")
    a.s_olow = sem(tag + "s_olow")
    a.s_bias = sem(tag + "s_bias")



NH = 8
SLOPES = [2.0 ** (-8.0 * (h + 1) / NH) for h in range(NH)]
CMP_L, CMP_STRIDE = 32, 16
NC = (T - CMP_L) // CMP_STRIDE + 1
FAR = 1e32
MIX_TILES = ("kc", "vc", "qa0", "qa1", "qa2", "qa3", "qb0", "qb1", "qb2", "qb3", "ks", "kw", "kb", "vs", "vw", "vb", "gate")
MIX_SPLIT = MIX_TILES[2:13]


def mixer_units():
    order = list(MIX_TILES[:7])
    compression = [(q, half) for q in range(4) for half in range(2)]
    for x, name in enumerate(MIX_TILES[7:]):
        order += compression[x:x + 1] + [name]
    return order


MIX_UNITS = mixer_units()


def mixer_constants(pool, c):
    def keep(ap, pattern, base, mult):
        pool.wait_ge(c.s_zeroed, c.zeroed)
        pool.affine_select(out=ap, in_=ap, compare_op=ALU.is_ge, fill=FAR, base=base, pattern=pattern,
                           channel_multiplier=mult).then_inc(c.s_zeroed, 1)
        c.zeroed += 1

    pool.iota(c.dist[:], [[-1, T]], base=T - P, channel_multiplier=1,
              allow_small_or_imprecise_dtypes=True).then_inc(c.s_zeroed, 1)
    pool.iota(c.dist_local[:], [[-1, 2 * P]], base=P, channel_multiplier=1,
              allow_small_or_imprecise_dtypes=True).then_inc(c.s_zeroed, 1)
    pool.iota(c.dist_cmp[:], [[P, TT], [-CMP_STRIDE, NC + 1]], base=1 - CMP_L, channel_multiplier=1,
              allow_small_or_imprecise_dtypes=True).then_inc(c.s_zeroed, 1)
    pool.memset(c.sees_block[:], 1.0).then_inc(c.s_zeroed, 1)
    c.zeroed += 4
    keep(c.dist[:], [[-1, T]], T - P, 1)
    keep(c.dist_local[:], [[-1, 2 * P]], P, 1)
    keep(c.dist_local[:], [[1, 2 * P]], -1, -1)
    keep(c.dist_cmp[:], [[P, TT], [-CMP_STRIDE, NC + 1]], 1 - CMP_L, 1)
    pool.wait_ge(c.s_zeroed, c.zeroed)
    pool.affine_select(out=c.sees_block[:], in_=c.sees_block[:], compare_op=ALU.is_ge, fill=0.0, base=1 - CMP_L,
                       pattern=[[0, 1]], channel_multiplier=1).then_inc(c.s_const, 1)


def stacked_high(act, ps, q, k, done):
    for side in range(2):
        src = ps[side * HD:side * HD + HD]
        if q is not None:
            act.activation(q[0:HD, side], src, ACT.Copy).then_inc(done, 1)
        else:
            for rows in (slice(0, HD), slice(HD, P)):
                act.activation(k[rows, side], src, ACT.Copy).then_inc(done, 1)


def stacked_low(dve, ps, q, k_hi, k_lo, high, before, evac):
    for side in range(2):
        src = ps[side * HD:side * HD + HD]
        if q is not None:
            dve.wait_ge(high, before + side + 1)
            op = dve.tensor_tensor(q[HD:P, side], src, q[0:HD, side].bitcast(F32), ALU.subtract)
        else:
            dve.wait_ge(high, before + 2 * side + 2)
            for rows in (slice(0, HD), slice(HD, P)):
                op = dve.tensor_tensor(k_lo[rows, side], src, k_hi[0:HD, side].bitcast(F32), ALU.subtract)
    op.then_inc(evac, 1)


def mixer_passes(c, a, m):
    passes = []

    def add(**kw):
        passes.append(Pass(**kw))

    order = [(tile, side) for tile in range(4) for side in range(2)]
    for x, (tile, side) in enumerate(order):
        h = tile + 4 * side
        both = dict(side=side, tile=tile, q=m.q[:, 2 * tile + side])
        gate = lambda b, h=h: m.gates[:, :, 3 * h + b]
        slot = x % 2

        def prepare(dve, h=h, slot=slot, x=x):
            dve.tensor_scalar(m.bias[slot][:], c.dist[:], -SLOPES[h] / SCALE, None, ALU.mult).then_inc(a.s_bias, 1)
            dve.tensor_scalar(m.bias_cmp[:, slot], c.dist_cmp[:], -SLOPES[h] / SCALE, None, ALU.mult).then_inc(a.s_bias, 1)
            dve.wait_ge(a.s_bias, 2 * x + 2)

        add(kind=BLOCKS, k_hi=m.kc_hi[:, side], k_lo=m.kc_lo[:, side], v_hi=lambda key: m.vc_hi[:], v_lo=lambda key: m.vc_lo[:],
            bias=lambda i, slot=slot: m.bias_cmp[:, slot, i], gate=gate(0), row_mask=c.sees_block[:, 0:1],
            prepare_dve=prepare, opens=True, o_before=2 * tile if tile else 0, **both)
        for b, (k, v) in ((1, (0, 0)), (2, (1, 1))):
            add(kind=FULL, k_hi=m.k_hi[:, 2 * k + side], k_lo=m.k_lo[:, 2 * k + side], v_hi=lambda key, v=v: m.v_hi[:, v, key],
                v_lo=lambda key, v=v: m.v_lo[:, v, key],
                bias=lambda i, slot=slot: m.bias[slot][:, (TT - 1 - i) * P:T], gate=gate(b),
                closes=b == 2, pair_done=b == 2 and side == 1, **both)
    for x, (tile, side) in enumerate(order):
        h = tile + 4 * side
        slot = x % 2

        def prepare(dve, h=h, slot=slot, x=x):
            dve.tensor_scalar(m.bias[slot][:, 0:2 * P], c.dist_local[:], -SLOPES[h] / SCALE, None,
                              ALU.mult).then_inc(a.s_bias, 1)
            dve.wait_ge(a.s_bias, 2 * NH + x + 1)

        add(kind=LOCAL, k_hi=m.k_hi[:, 4 + side], k_lo=m.k_lo[:, 4 + side], v_hi=lambda key: m.v_hi[:, 2, key],
            v_lo=lambda key: m.v_lo[:, 2, key], bias=lambda i, slot=slot: m.bias[slot][:, (P if i == 0 else 0):2 * P],
            prepare_dve=prepare, sink=c.sinks[:, h:h + 1], start=m.sink_start[:, h:h + 1], opens=True, closes=True,
            o_before=2 * (4 + tile), pair_done=side == 1, side=side, tile=4 + tile,
            q=m.q[:, 2 * (4 + tile) + side])
    return passes


def mixer_in_pe(pe, c, m, base, xn_ready):
    first_two_units(pe, c, base, lambda k: c.xn_hi[:, k], lambda k: c.xn_lo[:, k],
                    lambda k: pe.wait_ge(c.s_xn, xn_ready + k + 1))
    for j, name in enumerate(MIX_UNITS):
        if j < 2:
            continue
        u = base + j
        cols = 24 if name == "gate" else P
        pe.wait_ge(c.s_lo, u + 1)
        if name not in MIX_TILES:
            q, half = name
            pe.wait_ge(m.s_blk, q // 2 + 1)
            split_products(pe, c, c.ps[:, 4 + q, 0:64], u % RING, lambda k: m.blk_hi[:, q // 2, k],
                           lambda k: m.blk_lo[:, q // 2, k], range(KU), k0=half * KU, start=half == 0,
                           stop=half == 1).then_inc(c.s_pe, 1)
            continue
        pe.wait_ge(c.s_evac, u + START + 1 - RING)
        split_products(pe, c, c.ps[0:cols, u % RING], u % RING, lambda k: c.xn_hi[:, k], lambda k: c.xn_lo[:, k],
                       range(KD), cols=cols).then_inc(c.s_pe, 1)
    pe.wait_ge(c.s_evac, base + len(MIX_UNITS) + START)
    for v in range(3):
        for t in range(TT):
            mm = pe.transpose(c.ps[:, v, t * P:t * P + P], c.y[:, v, t * P:t * P + P], c.ident[:])
        mm.then_inc(m.s_vt, 1)
    pe.wait_ge(m.s_sig, 1)
    for t in range(TT):
        mm = pe.transpose(c.ps[:, 3, t * 24:t * 24 + 24], m.sig[0:24, t * P:t * P + P], c.ident[0:24, 0:24])
    mm.then_inc(m.s_vt, 1)
    pe.wait_ge(c.s_par, 16)
    pe.wait_ge(m.s_chid, 4)
    for g in range(2):
        for t in range(2):
            mm = pe.matmul(c.ps[g * HD:g * HD + HD, 4, 0:32], m.w2[:, 0, t], m.chid[:, t, g * 32:g * 32 + 32],
                           start=t == 0, stop=t == 1)
    mm.then_inc(m.s_vt, 1)
    for g in range(2):
        for t in range(2):
            mm = pe.matmul(c.ps[0:32, 5, g * HD:g * HD + HD], m.chid[:, 2 + t, g * 32:g * 32 + 32], m.w2[:, 1, t],
                           start=t == 0, stop=t == 1)
    mm.then_inc(m.s_vt, 1)
    pe.wait_ge(m.s_vlo, 5)
    pe.wait_ge(m.s_gates, 1)


def mixer_in_act(act, c, m, base):
    for j, name in enumerate(MIX_UNITS):
        u = base + j
        stream_high(act, c, u + RING - 1, (u + RING - 1) % RING, (u + RING - 1) // RING)
        act.wait_ge(c.s_pe, u + START + 1)
        if name not in MIX_TILES:
            q, half = name
            col = COL["cmp_k_b1" if q < 2 else "cmp_v_b1"] + q % 2
            if half == 1:
                act.activation(m.chid[:, q], c.ps[:, 4 + q, 0:64], ACT.Gelu_apprx_tanh,
                               bias=c.par[:, col:col + 1]).then_inc(m.s_chid, 1)
            continue
        if name in MIX_SPLIT:
            x = MIX_SPLIT.index(name)
            stacked_high(act, c.ps[:, u % RING], m.q[:, 2 * x:2 * x + 2] if x < 8 else None,
                         m.k_hi[:, 2 * x - 16:2 * x - 14] if x >= 8 else None, m.s_mhi)
        if j in (3, 4):
            act.wait_ge(m.s_blk32, j - 1)
            act.activation(m.blk_hi[:, j - 3], m.blk[:, j - 3], ACT.Copy).then_inc(m.s_blkhi, 1)
        if name == "gate":
            act.activation(m.sig[0:24], c.ps[0:24, u % RING], ACT.Sigmoid).then_inc(m.s_sig, 1)
    for v in range(3):
        act.wait_ge(m.s_vt, v + 1)
        act.activation(m.v_hi[:, v], c.ps[:, v].rearrange("p (t n) -> p t n", n=P), ACT.Copy).then_inc(m.s_vhi, 1)
    act.wait_ge(m.s_vt, 5)
    stacked_high(act, c.ps[:, 4, 0:32], None, m.kc_hi, m.s_kchi)
    act.wait_ge(m.s_vt, 6)
    act.activation(m.vc_hi[:], c.ps[0:32, 5, 0:P], ACT.Copy).then_inc(m.s_vhi, 1)


def mixer_in_dve(dve, c, m, base):
    dve.wait_ge(c.s_pe, base + START)
    dve.memset(m.blk[:], 0.0).then_inc(m.s_blk32, 1)
    dve.tensor_scalar(m.sink_start[:], c.sinks, 1.0 / SCALE, None, ALU.mult).then_inc(m.s_gates0, 1)
    dve.wait_ge(m.s_blk32, 1)
    blocks = m.blk[:].rearrange("p a k (g b) -> p a k g b", g=2)
    for j, name in enumerate(MIX_UNITS):
        u = base + j
        dve.wait_ge(c.s_pe, u + START + 1)
        if name not in MIX_TILES:
            dve.wait_ge(c.s_evac, u + START)
            dve.nop().then_inc(c.s_evac, 1)
            continue
        if name in ("kc", "vc"):
            pos = COL["cmp_k_pos" if j == 0 else "cmp_v_pos"]
            for g in range(2):
                for odd in range(2):
                    rows = slice(odd * HD, odd * HD + HD)
                    src = c.ps[g * HD:g * HD + HD, u % RING].rearrange("p (b k o) -> p k b o", k=8, o=2)
                    for part in range(2):
                        tokens = src[:, :, part:part + NC, odd]
                        dve.tensor_tensor(blocks[rows, j, part * 8:part * 8 + 8, g, 0:NC], tokens,
                                          c.par[rows, pos + part * 8:pos + part * 8 + 8].unsqueeze(2)
                                          .broadcast_to([HD, 8, NC]), ALU.add).then_inc(m.s_blk8, 1)
            dve.wait_ge(m.s_blk8, 8 * (j + 1))
            dve.nop().then_inc(c.s_evac, 1)
            dve.nop().then_inc(m.s_blk32, 1)
        elif name in MIX_SPLIT:
            x = MIX_SPLIT.index(name)
            before = 2 * x if x < 8 else 16 + 4 * (x - 8)
            if x < 8:
                stacked_low(dve, c.ps[:, u % RING], m.q[:, 2 * x:2 * x + 2], None, None, m.s_mhi, before, c.s_evac)
            else:
                k = slice(2 * x - 16, 2 * x - 14)
                stacked_low(dve, c.ps[:, u % RING], None, m.k_hi[:, k], m.k_lo[:, k], m.s_mhi, before, c.s_evac)
        elif name == "gate":
            dve.wait_ge(m.s_sig, 1)
            dve.nop().then_inc(c.s_evac, 1)
        else:
            dve.tensor_copy(c.y[:, MIX_TILES.index(name) - 13], c.ps[:, u % RING]).then_inc(c.s_evac, 1)
        if j in (4, 5):
            dve.wait_ge(m.s_blkhi, j - 3)
            dve.tensor_tensor(m.blk_lo[:, j - 4], m.blk[:, j - 4], m.blk_hi[:, j - 4].bitcast(F32),
                              ALU.subtract).then_inc(m.s_blk, 1)
    for v in range(3):
        dve.wait_ge(m.s_vhi, v + 1)
        dve.tensor_tensor(m.v_lo[:, v], c.ps[:, v].rearrange("p (t n) -> p t n", n=P), m.v_hi[:, v].bitcast(F32),
                          ALU.subtract).then_inc(m.s_vlo, 1)
    dve.wait_ge(m.s_vt, 4)
    dve.tensor_copy(m.gates[:], c.ps[:, 3, 0:96].rearrange("p (t n) -> p t n", n=24)).then_inc(m.s_gates, 1)
    stacked_low(dve, c.ps[:, 4, 0:32], None, m.kc_hi, m.kc_lo, m.s_kchi, 0, m.s_vlo)
    dve.wait_ge(m.s_vhi, 4)
    dve.tensor_tensor(m.vc_lo[:], c.ps[0:32, 5, 0:P], m.vc_hi[:].bitcast(F32), ALU.subtract).then_inc(m.s_vlo, 1)
    dve.wait_ge(m.s_gates0, 1)
    dve.wait_ge(m.s_gates, 1)

def mixer_tensors(c, sb, sem):
    m = Parts()
    m.v_hi = sb("v_hi", [P, 3, TT, P], F32R)
    m.v_lo = sb("v_lo", [P, 3, TT, P], F32R)
    m.q = sb("q_parts", [P, 16, T], F32R)
    m.k_hi = sb("k_hi", [P, 6, T], F32R)
    m.k_lo = sb("k_lo", [P, 6, T], F32R)
    m.kc_hi = sb("kc_hi", [P, 2, 32], F32R)
    m.kc_lo = sb("kc_lo", [P, 2, 32], F32R)
    m.vc_hi = sb("vc_hi", [32, P], F32R)
    m.vc_lo = sb("vc_lo", [32, P], F32R)
    m.bias = (c.rstd, c.root)
    m.bias_cmp = sb("bias_cmp", [P, 2, TT, 32])
    m.gates = sb("gates", [P, TT, 24])
    m.sink_start = sb("sink_start", [P, NH])
    m.s_blk = sem("m" + "s_blk")
    m.s_blk32 = sem("m" + "s_blk32")
    m.s_blk8 = sem("m" + "s_blk8")
    m.s_blkhi = sem("m" + "s_blkhi")
    m.s_vt = sem("m" + "s_vt")
    m.s_sig = sem("m" + "s_sig")
    m.s_chid = sem("m" + "s_chid")
    m.s_vlo = sem("m" + "s_vlo")
    m.s_kchi = sem("ms_kchi")
    m.s_vhi = sem("m" + "s_vhi")
    m.s_gates = sem("m" + "s_gates")
    m.s_gates0 = sem("m" + "s_gates0")
    m.s_mhi = sem("m" + "s_mhi")
    return m



MAX_REL = 128


def att_tensors(c, sb, sem):
    m = Parts()
    m.q = sb("aq", [P, 4, T], F32R)
    m.k_hi = sb("ak_hi", [P, 4, T], F32R)
    m.k_lo = sb("ak_lo", [P, 4, T], F32R)
    m.v_hi = sb("av_hi", [P, 2, TT, P], F32R)
    m.v_lo = sb("av_lo", [P, 2, TT, P], F32R)
    m.bias = sb("abias", [P, 2, T])
    m.s_mhi = sem("t" + "s_mhi")
    m.s_vt = sem("t" + "s_vt")
    m.s_vhi = sem("t" + "s_vhi")
    m.s_vlo = sem("t" + "s_vlo")
    m.s_biased = sem("t" + "s_biased")
    m.s_table = [sem("t_table0"), sem("t_table1")]
    return m


def att_passes(c, a, m, half):
    passes = []
    for x in range(4):
        tile, side = x // 2, x % 2
        h = 4 * half + x
        slot = x % 2

        def prepare(dve, x=x, slot=slot, n=4 * half + x):
            dve.wait_ge(m.s_table[slot], 16 * (n // 2 + 1))
            dve.tensor_scalar(m.bias[:, slot], m.bias[:, slot], 1.0 / SCALE, None, ALU.mult).then_inc(m.s_biased, 1)
            dve.wait_ge(m.s_biased, 2 * n + 1)
            dve.memset(m.bias[0:HD, slot, T - HD:T], -1e31).then_inc(m.s_biased, 1)
            dve.wait_ge(m.s_biased, 2 * n + 2)

        passes.append(Pass(
            kind=FULL, k_hi=m.k_hi[:, x], k_lo=m.k_lo[:, x], q=m.q[:, x],
            v_hi=lambda key, tile=tile: m.v_hi[:, tile, key], v_lo=lambda key, tile=tile: m.v_lo[:, tile, key],
            bias=lambda i, slot=slot: m.bias[:, slot, (TT - 1 - i) * P:T], gate=None, row_mask=None, sink=None,
            start=-3e38, opens=True, closes=True, pair_done=side == 1, side=side, tile=tile,
            o_before=2 * tile, prepare_dve=prepare,
            table_used=lambda act, n=h: att_table_load(act, c, m, n + 2)))
    return passes


def att_in_pe(pe, c, m, half, xn_ready):
    base = BASE["rwkv_in"] + 6 * half
    first_two_units(pe, c, base, lambda k: c.xn_hi[:, k], lambda k: c.xn_lo[:, k],
                    lambda k: pe.wait_ge(c.s_xn, xn_ready + k + 1))
    rwkv_units_pe(pe, c, base + 2, 4)
    pe.wait_ge(c.s_evac, base + 6 + START)
    for v in range(2):
        for t in range(TT):
            mm = pe.transpose(c.ps[:, v, t * P:t * P + P], c.y[:, v, t * P:t * P + P], c.ident[:])
        mm.then_inc(m.s_vt, 1)
    pe.wait_ge(m.s_vlo, 2 * half + 2)


def att_table_load(act, c, m, n):
    if n < NH:
        act.dma_start(m.bias[:, n % 2], c.table[n]).then_inc(m.s_table[n % 2], 16)


def att_in_act(act, c, m, half):
    base = BASE["rwkv_in"] + 6 * half
    if half == 0:
        act.wait_ge(c.s_pe, base + START)
        act.wait_ge(c.s_ss, KD * 5)
        att_table_load(act, c, m, 0)
        att_table_load(act, c, m, 1)
    for j in range(6):
        u = base + j
        stream_high(act, c, u + RING - 1, (u + RING - 1) % RING, (u + RING - 1) // RING)
        if j < 4:
            act.wait_ge(c.s_pe, u + START + 1)
            x = slice(2 * (j % 2), 2 * (j % 2) + 2)
            stacked_high(act, c.ps[:, u % RING], m.q[:, x] if j < 2 else None, m.k_hi[:, x] if j >= 2 else None, m.s_mhi)
    for v in range(2):
        act.wait_ge(m.s_vt, 2 * half + v + 1)
        act.activation(m.v_hi[:, v], c.ps[:, v].rearrange("p (t n) -> p t n", n=P), ACT.Copy).then_inc(m.s_vhi, 1)


def att_in_dve(dve, c, m, half):
    base = BASE["rwkv_in"] + 6 * half
    for j in range(6):
        u = base + j
        dve.wait_ge(c.s_pe, u + START + 1)
        if j < 4:
            x = slice(2 * (j % 2), 2 * (j % 2) + 2)
            before = 12 * half + (2 * j if j < 2 else 4 * j - 4)
            if j < 2:
                stacked_low(dve, c.ps[:, u % RING], m.q[:, x], None, None, m.s_mhi, before, c.s_evac)
            else:
                stacked_low(dve, c.ps[:, u % RING], None, m.k_hi[:, x], m.k_lo[:, x], m.s_mhi, before, c.s_evac)
        else:
            dve.tensor_copy(c.y[:, j - 4], c.ps[:, u % RING]).then_inc(c.s_evac, 1)
    for v in range(2):
        dve.wait_ge(m.s_vhi, 2 * half + v + 1)
        dve.tensor_tensor(m.v_lo[:, v], c.ps[:, v].rearrange("p (t n) -> p t n", n=P), m.v_hi[:, v].bitcast(F32),
                          ALU.subtract).then_inc(m.s_vlo, 1)



CH = 64
NCH = T // CH
PAIRS = 4
LEVELS = (2, 4, 8, 16, 32)
EXP_HALF = float(np.exp(-0.5))
GN_EPS = 64e-5



def rwkv_preparation():
    pe = ["lora_w", "lora_a", "kknorm", "kkb", "bonus"]
    act = ["raw0", "raw1", "raw2", "sigw", "siga", "sq", "root", "eP", "ePi", "ePp", "ePe"]
    dve = ["dr", "r", "dk", "k", "dv", "v", "ld", "L", "kk0", "lp", "le", "rootmax", "rec", "recx", "kk", "ka", "kfin",
           "A", "R", "b0", "B", "Bp", "K", "Kp", "pend", "rk", "bon"]
    return pe, act, dve


def rwkv_steps():
    heads = range(2)
    pe = []
    pe += [f"prod{s}" for s in heads] + [f"lab{s}" for s in heads]
    pe += ["turnA", "turnB", "turnK", "turnV"]
    for lv in range(len(LEVELS)):
        pe += [f"w{lv}{s}" for s in heads] + [f"de{lv}{s}" for s in heads]
    pe += ["lv", "u", "z", "ru", "yl", "g0", "g1", "h0", "h1"]
    pe += [f"s{ch}" for ch in range(2, NCH)] + ["y0", "y1", "mean", "var", "lora_g", "yrb"]
    act = ["tA", "tB", "tK", "tV", "lv", "u", "z", "yl", "h0", "h1", "ysq", "yroot"]
    dve = []
    for s in heads:
        dve += [f"mm{s}{x}" for x in range(4)] + [f"em{s}", f"dm{s}", f"D{s}", f"E{s}"]
    for lv in range(len(LEVELS)):
        dve += [f"W{lv}{s}" for s in heads]
        dve += [x for s in heads for x in ((f"D{lv}{s}", f"E{lv}{s}") if lv < len(LEVELS) - 1 else (f"E{lv}{s}",))]
    dve += ["ru", "gd", "g0", "g1", "S1"] + [f"S{ch}{s}" for ch in range(2, NCH) for s in heads]
    dve += ["y0", "y1", "yc", "yrec", "yrecx", "yn", "ylnb", "ysum", "out"]
    return pe, act, dve


PREPARATION = dict(zip(("pe", "act", "dve"), rwkv_preparation()))
STEPS = dict(zip(("pe", "act", "dve"), rwkv_steps()))


def rwkv_tensors(c, sb, sem):
    w = Parts()
    w.raw = sb("raw", [P, 3, 1 + T])
    w.lora_in = sb("lora_in", [P, 2, T])
    w.lora_w = sb("lora_w", [P, 2, T])
    w.r, w.k, w.v = (sb("rk" + x, [P, T]) for x in "rkv")
    w.eP = sb("eP", [P, T])
    w.L = sb("L", [P, T])
    w.AR = sb("AR", [P, 2, T])
    w.BK = sb("BK", [P, NCH, 2, CH])
    w.BKp = sb("BKp", [P, 2, T])
    w.tok = sb("tok", [P, 4, TT, P])
    w.M = sb("M", [P, 2, TT, 4, P])
    w.DE = sb("DE", [P, 2, 2, TT, P])
    w.W = sb("W", [P, 2, TT, P])
    w.S = c.dist[:].rearrange("p (c n) -> p c n", n=HD)
    w.y32 = sb("y32", [P, PAIRS, T])
    w.scan_keep = c.dist_local[:].bitcast(BF16).rearrange("p (c n) -> p c n", n=CH)
    w.pend = sb("pend", [P, 2, NCH])
    w.norm = sb("rwkv_norm", [P, 2, TT, 2])
    w.ld = c.ss
    w.kk = c.rstd
    w.a = c.root
    w.tmp, w.tmp2, w.rk = c.y[:, 0], c.y[:, 1], c.y[:, 2]
    w.ePi, w.ePp, w.ePe = w.raw[:, 0, 1:], w.raw[:, 1, 1:], w.raw[:, 2, 1:]
    w.LV, w.U, w.Z = w.W[:, 0], w.DE[:, 0, 0], w.DE[:, 1, 0]
    w.YL, w.RU = w.W[:, 1], w.DE[:, 0, 1]
    w.G, w.H = w.DE[:, 1, 1], w.W[:, 0]
    w.yc, w.ysq = w.tok[:, 0], w.tok[:, 1]
    w.s_ppe, w.s_pact, w.s_pdve = sem("s_ppe"), sem("s_pact"), sem("s_pdve")
    w.s_yl = sem("s_yl")
    w.s_wpe, w.s_wact, w.s_wdve = sem("s_wpe"), sem("s_wact"), sem("s_wdve")
    w.s_wshift, w.s_wlora, w.s_whi, w.s_wlo, w.s_wload = (sem("s_wshift"), sem("s_wlora"), sem("s_whi"), sem("s_wlo"),
                                                          sem("s_wload"))
    return w


def step_counter(sem, steps):
    pos = {name: i for i, name in enumerate(steps)}
    issued = [0]

    def done(name, ins):
        assert steps[issued[0] % len(steps)] == name, (name, steps[issued[0] % len(steps)])
        issued[0] += 1
        ins.then_inc(sem, 1)

    def wait(eng, j, name):
        eng.wait_ge(sem, j * len(steps) + pos[name] + 1)

    return done, wait


def preparation_waits(w):
    return {"pe": step_counter(w.s_ppe, PREPARATION["pe"]), "act": step_counter(w.s_pact, PREPARATION["act"]),
            "dve": step_counter(w.s_pdve, PREPARATION["dve"])}


def rwkv_waits(w):
    return {"pe": step_counter(w.s_wpe, STEPS["pe"]), "act": step_counter(w.s_wact, STEPS["act"]),
            "dve": step_counter(w.s_wdve, STEPS["dve"])}


def rwkv_units_pe(pe, c, base, n):
    for j in range(n):
        u = base + j
        pe.wait_ge(c.s_lo, u + 1)
        pe.wait_ge(c.s_evac, u + START + 1 - RING)
        split_products(pe, c, c.ps[:, u % RING], u % RING, lambda k: c.xn_hi[:, k], lambda k: c.xn_lo[:, k],
                       range(KD)).then_inc(c.s_pe, 1)


def chunk(ap, rows, ch):
    return ap[rows, ch // 2, ch % 2 * CH:ch % 2 * CH + CH]


TURN_BANKS = (6, 7, 4, 5)


def preparation_banks(u, j):
    return (4, 5, 6, 7) if j == 0 else ((u + 3) % RING, u % RING, (u + 1) % RING, (u + 2) % RING)


def level_banks(lv):
    return (4, 6) if lv % 2 == 0 else (6, 4)


def spread(norm):
    return norm[:, 1].rearrange("p b s -> p (b s)").unsqueeze(2).broadcast_to([P, 2 * TT, HD])


def rwkv_pe(pe, c, w, base):
    pre, ways = preparation_waits(w), rwkv_waits(w)
    prepared, done = pre["pe"][0], ways["pe"][0]
    PA = lambda j, name: pre["act"][1](pe, j, name)
    PV = lambda j, name: pre["dve"][1](pe, j, name)
    A = lambda j, name: ways["act"][1](pe, j, name)
    V = lambda j, name: ways["dve"][1](pe, j, name)
    ps = c.ps
    first_unit = lambda j: base + 2 + 3 * j

    def unit_part(j, x, first, end):
        if j >= PAIRS:
            return
        u = first_unit(j) + x
        if first == 0:
            pe.wait_ge(c.s_lo, u + 1)
            pe.wait_ge(c.s_evac, u + START + 1 - RING)
            if j >= 2:
                (PA if x < 2 else PV)(j - 1, ("sigw", "siga", "bon")[x])
        mm = split_products(pe, c, ps[:, u % RING], u % RING, lambda k: c.xn_hi[:, k], lambda k: c.xn_lo[:, k],
                            range(first, end), start=first == 0, stop=end == KU)
        if end == KU:
            mm.then_inc(c.s_pe, 1)

    def prepare(j, part):
        if j >= PAIRS:
            return
        u, cols = first_unit(j), slice(j * P, j * P + P)
        banks = preparation_banks(u, j)
        if part == 0:
            pe.wait_ge(c.s_evac, u + START + 1)
            if j >= 1:
                PV(j - 1, "kk")
            prepared("lora_w", pe.matmul(ps[:, banks[0]], w.lora_w[0:HD, 0, cols], w.lora_in[0:HD, 0],
                                         start=True, stop=True))
            prepared("lora_a", pe.matmul(ps[:, banks[1]], w.lora_w[HD:P, 0, cols], w.lora_in[HD:P, 0],
                                         start=True, stop=True))
        elif part == 1:
            pe.wait_ge(c.s_evac, u + START + 2)
            PA(j, "sq")
            for b in range(TT):
                mm = pe.matmul(ps[:, banks[2], 2 * b:2 * b + 2], w.tmp2[:, b * P:b * P + P], c.ones_head[:, 0:P:HD],
                               start=True, stop=True)
            prepared("kknorm", mm)
        elif part == 2:
            pe.wait_ge(c.s_evac, u + START + 3)
            PV(j, "recx")
            for b in range(TT):
                mm = pe.transpose(ps[:, banks[3], b * P:b * P + P], w.tmp2[:, b * P:b * P + P], c.ident[:])
            prepared("kkb", mm)
        elif part == 3:
            PV(j, "rk")
            prepared("bonus", pe.matmul(ps[:, banks[2]], c.ones_head[:], w.rk, start=True, stop=True))

    rwkv_units_pe(pe, c, base, 2)
    rwkv_units_pe(pe, c, base + 2, 3)
    pe.wait_ge(w.s_wload, 32)
    pe.wait_ge(w.s_wlora, 3)
    for part in range(4):
        prepare(0, part)
        if part < 3:
            unit_part(1, part, 0, KU)
    for j in range(PAIRS):
        AR = w.AR
        cols = slice(j * P, j * P + P)
        PV(j, "Kp" if j else "bon")
        if j >= 1:
            V(j - 1, "out")
        for s in range(2):
            rows = slice(s * HD, s * HD + HD)
            for ch in range(NCH):
                mm = pe.matmul(ps[:, 4 + 2 * s + ch // 4, ch % 4 * P:ch % 4 * P + P],
                               w.BK[rows, ch].rearrange("p x n -> p (x n)"), AR[rows, :, ch * CH:ch * CH + CH],
                               start=True, stop=True)
            done(f"prod{s}", mm)
        V(j, "mm03")
        for s in range(2):
            rows = slice(s * HD, s * HD + HD)
            for b in range(TT):
                mm = pe.matmul(ps[:, 4 + s, b * P:b * P + P], AR[rows, 0, b * P:b * P + P],
                               w.BK[rows, 2 * b:2 * b + 2, 0], start=True, stop=True)
            done(f"lab{s}", mm)
        sources = (lambda b: AR[:, 0, b * P:b * P + P], lambda b: w.BKp[:, 0, b * P:b * P + P], lambda b: w.BKp[:, 1, b * P:b * P + P],
                   lambda b: w.v[:, b * P:b * P + P])
        for x, name in enumerate(("turnA", "turnB", "turnK", "turnV")):
            V(j, ("mm13", "mm13", "dm0", "dm1")[x])
            for b in range(TT):
                mm = pe.transpose(ps[:, TURN_BANKS[x], b * P:b * P + P], sources[x](b), c.ident[:])
            done(name, mm)
        for lv in range(len(LEVELS)):
            wb, db = level_banks(lv)
            for s in range(2):
                V(j, f"E{s}" if lv == 0 else f"E{lv - 1}{s}")
                if lv == 0:
                    A(j, ("tK", "tV")[s])
                for b in range(TT):
                    mm = pe.matmul(ps[:, wb + s, b * P:b * P + P], w.M[:, s, b, 0], w.DE[:, s, 0, b], start=True, stop=True)
                done(f"w{lv}{s}", mm)
            for s in range(2):
                V(j, f"W{lv}{s}")
                if s == 1:
                    db = wb
                last = lv == len(LEVELS) - 1
                if not last:
                    for b in range(TT):
                        pe.matmul(ps[:, db, b * P:b * P + P], w.DE[:, s, 1, b], w.W[:, s, b], start=True, stop=True)
                for b in range(TT):
                    mm = pe.matmul(ps[:, db + 1, b * P:b * P + P], w.W[:, s, b], w.DE[:, s, 1, b], start=True, stop=True)
                done(f"de{lv}{s}", mm)
            if lv < 3:
                prepare(j + 1, lv)
            else:
                unit_part(j + 2, 0, 4 * (lv - 3), 4 * (lv - 2))
        for s in range(2):
            for b in range(TT):
                at = slice(b * P + s * HD, b * P + s * HD + HD)
                mm = pe.matmul(ps[:, 4, at], w.M[:, s, b, 2], w.tok[:, 3, b, s * HD:s * HD + HD], start=True, stop=True)
        done("lv", mm)
        unit_part(j + 2, 1, 0, 1)
        V(j, f"E{len(LEVELS) - 1}1")
        for bank, name in ((5, "u"), (6, "z")):
            if name == "z":
                A(j, "lv")
            for s in range(2):
                for b in range(TT):
                    at = slice(b * P + s * HD, b * P + s * HD + HD)
                    rhs = w.tok[:, 0, b, s * HD:s * HD + HD] if name == "u" else w.LV[:, b, s * HD:s * HD + HD]
                    mm = pe.matmul(ps[:, bank, at], w.DE[:, s, 1, b], rhs, start=True, stop=True)
            done(name, mm)
        A(j, "u")
        for s in range(2):
            for b in range(TT):
                mm = pe.matmul(ps[s * HD:s * HD + HD, 7, b * P:b * P + P], w.U[:, b, s * HD:s * HD + HD],
                               w.M[:, s, b, 1], start=True, stop=True)
        done("ru", mm)
        A(j, "z")
        for s in range(2):
            for b in range(TT):
                pe.matmul(ps[s * HD:s * HD + HD, 4, b * P:b * P + P], w.Z[:, b, s * HD:s * HD + HD],
                          w.M[:, s, b, 1], start=True, stop=False)
                mm = pe.matmul(ps[s * HD:s * HD + HD, 4, b * P:b * P + P], w.tok[:, 3, b, s * HD:s * HD + HD],
                               w.M[:, s, b, 3], start=False, stop=True)
        done("yl", mm)
        for half in range(2):
            rows = slice(half * HD, half * HD + HD)
            for s in range(2):
                f = slice(s * HD, s * HD + HD)
                for b in range(TT):
                    mm = pe.matmul(ps[f, 5 + half, b * HD:b * HD + HD], w.U[rows, b, f], w.tok[rows, 1, b, f],
                                   start=True, stop=True)
            done(f"g{half}", mm)
        for half in range(2):
            rows = slice(half * HD, half * HD + HD)
            if half == 0:
                V(j, "ru")
            else:
                A(j, "yl")
            for s in range(2):
                f = slice(s * HD, s * HD + HD)
                for b in range(TT):
                    out = ps[f, (7, 4)[half], b * HD:b * HD + HD]
                    pe.matmul(out, w.tok[rows, 1, b, f], w.Z[rows, b, f], start=True, stop=False)
                    mm = pe.matmul(out, w.tok[rows, 2, b, f], w.tok[rows, 3, b, f], start=False, stop=True)
            done(f"h{half}", mm)
        V(j, "g1")
        A(j, "h1")
        for ch in range(2, NCH):
            V(j, "S1" if ch == 2 else f"S{ch - 1}1")
            for s in range(2):
                f = slice(s * HD, s * HD + HD)
                mm = pe.matmul(ps[f, 5 + s, (ch % 2) * HD:(ch % 2) * HD + HD], chunk(w.G, f, ch - 1), w.S[f, ch - 1],
                               start=True, stop=True)
            done(f"s{ch}", mm)
            unit_part(j + 2, 1, ch - 1, ch)
        unit_part(j + 2, 1, NCH - 1, KU)
        V(j, f"S{NCH - 1}1")
        prepare(j + 1, 3)
        for s in range(2):
            f = slice(s * HD, s * HD + HD)
            for ch in range(1, NCH):
                mm = pe.matmul(ps[f, (7, 4)[s], ch * CH:ch * CH + CH], w.S[f, ch], chunk(w.RU, f, ch),
                               start=True, stop=True)
            done(f"y{s}", mm)
        V(j, "y1")
        done("mean", pe.matmul(ps[:, 5], c.ones_head[:], w.YL, start=True, stop=True))
        unit_part(j + 2, 2, 0, 2)
        A(j, "ysq")
        for b in range(TT):
            mm = pe.matmul(ps[:, 6, 2 * b:2 * b + 2], w.ysq[:, b], c.ones_head[:, 0:P:HD], start=True, stop=True)
        done("var", mm)
        done("lora_g", pe.matmul(ps[:, 4], w.lora_w[:, 1, cols], w.lora_in[:, 1], start=True, stop=True))
        V(j, "yrecx")
        for b in range(TT):
            mm = pe.transpose(ps[:, 7, b * P:b * P + P], w.ysq[:, b], c.ident[:])
        done("yrb", mm)
        unit_part(j + 2, 2, 2, KU)


def rwkv_act(act, c, w, base):
    pre, ways = preparation_waits(w), rwkv_waits(w)
    prepared, done = pre["act"][0], ways["act"][0]
    PE_ = lambda j, name: pre["pe"][1](act, j, name)
    PV = lambda j, name: pre["dve"][1](act, j, name)
    E = lambda j, name: ways["pe"][1](act, j, name)
    V = lambda j, name: ways["dve"][1](act, j, name)
    ps = c.ps

    def high(u):
        stream_high(act, c, u + RING - 1, (u + RING - 1) % RING, (u + RING - 1) // RING)

    def prepare(j):
        u0 = base + 2 + 3 * j
        banks = preparation_banks(u0, j)
        if j >= 1:
            PV(j - 1, "Kp")
        for x in range(3):
            high(u0 + x)
            act.wait_ge(c.s_pe, u0 + x + START + 1)
            prepared(f"raw{x}", act.activation(w.raw[:, x, 1:], ps[:, (u0 + x) % RING], ACT.Copy))
        PE_(j, "lora_w")
        prepared("sigw", act.activation(w.ld[:], ps[:, banks[0]], ACT.Sigmoid, bias=c.column("l0_w0_2", j)))
        PE_(j, "lora_a")
        prepared("siga", act.activation(w.a[:], ps[:, banks[1]], ACT.Sigmoid, bias=c.column("l0_a0_2", j)))
        PV(j, "kk0")
        prepared("sq", act.activation(w.tmp2, w.kk[:], ACT.Square))
        PE_(j, "kknorm")
        prepared("root", act.activation(w.norm[:, 0], ps[:, banks[2], 0:2 * TT].rearrange("p (b s) -> p b s", s=2),
                                        ACT.Sqrt))
        PV(j, "L")
        prepared("eP", act.activation(w.eP[:], w.L[:], ACT.Exp))
        PV(j, "v")
        prepared("ePi", act.activation(w.ePi, w.L[:], ACT.Exp, scale=-1.0))
        PV(j, "lp")
        prepared("ePp", act.activation(w.ePp, w.ePp, ACT.Exp))
        PV(j, "le")
        prepared("ePe", act.activation(w.ePe, w.ePe, ACT.Exp))

    act.wait_ge(c.s_pe, base + START + 1)
    act.dma_start(w.lora_w[:, 0], c.lora[0:P]).then_inc(w.s_wload, 16)
    act.dma_start(w.lora_w[:, 1], c.lora[P:2 * P]).then_inc(w.s_wload, 16)
    act.wait_ge(w.s_wshift, 1)
    for x in range(2):
        high(base + x)
        act.wait_ge(c.s_pe, base + x + START + 1)
        act.activation(w.raw[:, x, 1:], ps[:, (base + x) % RING], ACT.Copy).then_inc(w.s_whi, 1)
    act.wait_ge(w.s_wshift, 6)
    act.activation(w.lora_in[0:HD, 0], c.y[0:HD, 0], ACT.Tanh).then_inc(w.s_wlora, 1)
    act.activation(w.lora_in[HD:P, 0], c.y[HD:P, 0], ACT.Copy).then_inc(w.s_wlora, 1)
    act.activation(w.lora_in[:, 1], c.y[:, 1], ACT.Sigmoid).then_inc(w.s_wlora, 1)
    act.wait_ge(w.s_wlora, 3)
    prepare(0)
    for j in range(PAIRS):
        for x, name in enumerate(("A", "B", "K", "V")):
            E(j, "turn" + name)
            done("t" + name, act.activation(w.tok[:, x], ps[:, TURN_BANKS[x]].rearrange("p (b n) -> p b n", n=P),
                                              ACT.Copy))
        if j + 1 < PAIRS:
            prepare(j + 1)
        E(j, "lv")
        done("lv", act.activation(w.LV, ps[:, 4].rearrange("p (b n) -> p b n", n=P), ACT.Copy))
        E(j, "u")
        done("u", act.activation(w.U, ps[:, 5].rearrange("p (b n) -> p b n", n=P), ACT.Copy))
        E(j, "z")
        done("z", act.activation(w.Z, ps[:, 6].rearrange("p (b n) -> p b n", n=P), ACT.Copy))
        E(j, "yl")
        done("yl", act.activation(w.YL, ps[:, 4].rearrange("p (b n) -> p b n", n=P), ACT.Copy))
        for half in range(2):
            E(j, f"h{half}")
            done(f"h{half}", act.activation(w.H[:, :, half * HD:half * HD + HD],
                                            ps[:, (7, 4)[half], 0:TT * HD].rearrange("p (b n) -> p b n", n=HD), ACT.Copy))
        V(j, "yc")
        done("ysq", act.activation(w.ysq, w.yc, ACT.Square))
        E(j, "var")
        done("yroot", act.activation(w.norm[:, 0], ps[:, 6, 0:2 * TT].rearrange("p (b s) -> p b s", s=2), ACT.Sqrt,
                                     bias=c.gn_eps[:, 0:1], scale=1.0 / HD))
    V(PAIRS - 1, "out")
    act.wait_ge(c.s_pe, base + 14 + START)
    for k in range(KD):
        src = w.y32[:, k] if k < 4 else c.o32[:, k - 4]
        act.activation(c.xn_hi[:, k], src, ACT.Copy).then_inc(w.s_whi, 1)


def rwkv_dve(dve, c, w, base):
    pre, ways = preparation_waits(w), rwkv_waits(w)
    prepared, done = pre["dve"][0], ways["dve"][0]
    PE_ = lambda j, name: pre["pe"][1](dve, j, name)
    PA = lambda j, name: pre["act"][1](dve, j, name)
    mine = lambda j, name: pre["dve"][1](dve, j, name)
    own = lambda j, name: ways["dve"][1](dve, j, name)
    E = lambda j, name: ways["pe"][1](dve, j, name)
    A = lambda j, name: ways["act"][1](dve, j, name)
    ps = c.ps
    blocks = lambda ap: ap.rearrange("p (b n) -> p b n", n=P)
    chunks = lambda ap: ap.rearrange("p (c n) -> p c n", n=CH)
    over = lambda mask: mask.unsqueeze(1).broadcast_to([P, TT, P])

    def prepare(j, part):
        if j >= PAIRS:
            return
        banks = preparation_banks(base + 2 + 3 * j, j)
        if part == 0:
            for x, (name, dst) in enumerate((("r", w.r), ("k", w.k), ("v", w.v))):
                PA(j, f"raw{x}")
                dve.nop().then_inc(c.s_evac, 1)
                prepared("d" + name, dve.tensor_tensor(dst[:], w.raw[:, x, 0:T], w.raw[:, x, 1:], ALU.subtract))
                mine(j, "d" + name)
                prepared(name, dve.scalar_tensor_tensor(out=dst[:], in0=dst[:], scalar=c.column("l0_shift_mu_2", 4 * x + j),
                                                        in1=w.raw[:, x, 1:], op0=ALU.mult, op1=ALU.add))
        elif part == 1:
            PA(j, "sigw")
            prepared("ld", dve.tensor_scalar(w.ld[:], w.ld[:], -EXP_HALF, None, ALU.mult))
            mine(j, "ld")
            prepared("L", dve.tensor_tensor_scan(w.L[:], w.scan_keep.rearrange("p c n -> p (c n)"), w.ld[:], 0.0,
                                                 ALU.mult, ALU.add))
            prepared("kk0", dve.tensor_scalar(w.kk[:], w.k[:], c.column("l0_k_k_2", j), None, ALU.mult))
            mine(j, "L")
            prepared("lp", dve.tensor_tensor(w.ePp, w.L[:], w.ld[:], ALU.subtract))
            lw = w.L[:].rearrange("p (c n) -> p c n", n=CH)
            prepared("le", dve.tensor_tensor(w.ePe.rearrange("p (c n) -> p c n", n=CH),
                                             lw[:, :, CH - 1:CH].broadcast_to([P, NCH, CH]), lw, ALU.subtract))
        elif part == 2:
            PA(j, "root")
            prepared("rootmax", dve.tensor_scalar(w.norm[:, 0], w.norm[:, 0], 1e-12, None, ALU.max))
            mine(j, "rootmax")
            prepared("rec", dve.reciprocal(w.norm[:, 1], w.norm[:, 0]))
            mine(j, "rec")
            prepared("recx", dve.tensor_copy(w.tmp2.rearrange("p (x n) -> p x n", n=HD), spread(w.norm)))
        elif part == 3:
            PE_(j, "kkb")
            prepared("kk", dve.tensor_tensor(w.kk[:], w.kk[:], ps[:, banks[3]], ALU.mult))
            PA(j, "siga")
            prepared("ka", dve.tensor_scalar(w.tmp, w.a[:], c.column("l0_k_a_2", j), c.omka[:, j:j + 1], ALU.mult, ALU.add))
            mine(j, "ka")
            prepared("kfin", dve.tensor_tensor(w.k[:], w.k[:], w.tmp, ALU.mult))
        elif part == 4:
            PA(j, "ePe")
            mine(j, "kfin")
            prepared("A", dve.scalar_tensor_tensor(out=w.AR[:, 0], in0=w.kk[:], scalar=-1.0, in1=w.ePp,
                                                   op0=ALU.mult, op1=ALU.mult))
            prepared("R", dve.tensor_tensor(w.AR[:, 1], w.r[:], w.eP[:], ALU.mult))
            prepared("b0", dve.tensor_tensor(w.tmp, w.kk[:], w.a[:], ALU.mult))
            mine(j, "b0")
            prepared("B", dve.tensor_tensor(w.BK[:, :, 0], chunks(w.tmp), chunks(w.ePi), ALU.mult))
            prepared("Bp", dve.tensor_tensor(w.BKp[:, 0], w.tmp, w.ePe, ALU.mult))
        elif part == 5:
            prepared("K", dve.tensor_tensor(w.BK[:, :, 1], chunks(w.k[:]), chunks(w.ePi), ALU.mult))
            prepared("Kp", dve.tensor_tensor(w.BKp[:, 1], w.k[:], w.ePe, ALU.mult))
            prepared("pend", dve.tensor_copy(w.pend[:, j % 2], w.eP[:, CH - 1:T:CH]))
            prepared("rk", dve.scalar_tensor_tensor(out=w.rk, in0=w.r[:], scalar=c.column("l0_r_k_2", j), in1=w.k[:],
                                                    op0=ALU.mult, op1=ALU.mult))
        elif part == 6:
            PE_(j, "bonus")
            prepared("bon", dve.tensor_tensor(w.y32[:, j], w.v[:], ps[:, banks[2]], ALU.mult))

    dve.wait_ge(c.s_pe, base + START + 1)
    for x in range(3):
        dve.memset(w.raw[:, x, 0:1], 0.0).then_inc(w.s_wlo, 1)
    dve.memset(w.scan_keep, 1.0).then_inc(w.s_wlo, 1)
    dve.memset(w.M[:], 0.0).then_inc(w.s_wlo, 1)
    dve.wait_ge(w.s_wlo, 5)
    dve.memset(w.scan_keep[:, :, 0:1], 0.0).then_inc(w.s_wshift, 1)
    dve.tensor_scalar(c.omka[:], c.par[:, COL["l0_k_a_2"]:COL["l0_k_a_2"] + 4], -1.0, 1.0, ALU.mult,
                      ALU.add).then_inc(w.s_wshift, 1)
    for x in range(2):
        dve.wait_ge(w.s_whi, x + 1)
        dve.tensor_tensor(c.y[:, x], w.raw[:, x, 0:T], w.raw[:, x, 1:], ALU.subtract).then_inc(w.s_wshift, 1)
        dve.wait_ge(w.s_wshift, 3 + 2 * x)
        dve.scalar_tensor_tensor(out=c.y[:, x], in0=c.y[:, x], scalar=c.column("l0_shift_mu_2", 12 + x),
                                 in1=w.raw[:, x, 1:], op0=ALU.mult, op1=ALU.add).then_inc(w.s_wshift, 1)
        dve.nop().then_inc(c.s_evac, 1)
    dve.wait_ge(w.s_wlora, 3)
    for part in range(7):
        prepare(0, part)
    for j in range(PAIRS):
        R = blocks(w.AR[:, 1])
        if j >= 1:
            own(j - 1, "out")
        for s in range(2):
            D, Et = w.DE[:, s, 0], w.DE[:, s, 1]
            E(j, f"prod{s}")
            products = ps[:, 4 + 2 * s:6 + 2 * s].rearrange("p q (b r x n) -> p (q b) r x n", b=2, r=2, x=2)
            for x in range(4):
                part, odd = x // 2, x % 2
                rows, at = slice(part * HD, part * HD + HD), slice(odd * HD, odd * HD + HD)
                mask = c.mask4[rows, 0:2, part * HD:part * HD + HD].unsqueeze(1).broadcast_to([HD, TT, 2, HD])
                done(f"mm{s}{x}", dve.tensor_tensor(w.M[at, s, :, 2 * part:2 * part + 2, at], products[rows, :, odd], mask,
                                                    ALU.mult))
            own(j, f"mm{s}1")
            done(f"em{s}", dve.tensor_tensor(Et, w.M[:, s, :, 0], over(c.level[:, 6]), ALU.mult))
            E(j, f"lab{s}")
            done(f"dm{s}", dve.tensor_tensor(D, blocks(ps[:, 4 + s]), over(c.level[:, 0]), ALU.mult))
            own(j, f"dm{s}")
            done(f"D{s}", dve.tensor_tensor(D, D, over(c.ident[:]), ALU.add))
            done(f"E{s}", dve.tensor_tensor(Et, Et, over(c.ident[:]), ALU.add))
        E(j, "turnV")
        for lv in range(len(LEVELS)):
            wb, db = level_banks(lv)
            for s in range(2):
                E(j, f"w{lv}{s}")
                done(f"W{lv}{s}", dve.tensor_tensor(w.W[:, s], blocks(ps[:, wb + s]), over(c.level[:, lv + 1]), ALU.mult))
            if lv < 4:
                prepare(j + 1, lv)
            for s in range(2):
                E(j, f"de{lv}{s}")
                if s == 1:
                    db = wb
                if lv < len(LEVELS) - 1:
                    done(f"D{lv}{s}", dve.tensor_tensor(w.DE[:, s, 0], w.DE[:, s, 0], blocks(ps[:, db]), ALU.add))
                done(f"E{lv}{s}", dve.tensor_tensor(w.DE[:, s, 1], w.DE[:, s, 1], blocks(ps[:, db + 1]), ALU.add))
        E(j, "ru")
        done("ru", dve.tensor_tensor(w.RU, blocks(ps[:, 7]), R, ALU.add))
        A(j, "tB")
        A(j, "tK")
        done("gd", dve.tensor_tensor(w.G.rearrange("p b (h n) -> p b h n", h=2),
                                     c.ident_head[:].unsqueeze(1).unsqueeze(1).broadcast_to([P, TT, 2, HD]),
                                     w.pend[:, j % 2].rearrange("p (b h) -> p b h", h=2).unsqueeze(3)
                                     .broadcast_to([P, TT, 2, HD]), ALU.mult))
        own(j, "gd")
        for half in range(2):
            E(j, f"g{half}")
            g = w.G[:, :, half * HD:half * HD + HD]
            done(f"g{half}", dve.tensor_tensor(g, g, ps[:, 5 + half, 0:TT * HD].rearrange("p (b n) -> p b n", n=HD), ALU.add))
        own(j, "ru")
        prepare(j + 1, 4)
        A(j, "h1")
        done("S1", dve.tensor_copy(w.S[:, 1], chunk(w.H, slice(0, P), 0)))
        for ch in range(2, NCH):
            E(j, f"s{ch}")
            for s in range(2):
                f = slice(s * HD, s * HD + HD)
                done(f"S{ch}{s}", dve.tensor_tensor(w.S[f, ch], chunk(w.H, f, ch - 1),
                                                    ps[f, 5 + s, (ch % 2) * HD:(ch % 2) * HD + HD], ALU.add))
            if ch == 3:
                prepare(j + 1, 5)
        for s in range(2):
            f = slice(s * HD, s * HD + HD)
            E(j, f"y{s}")
            y = blocks(ps[f, (7, 4)[s]])
            dve.tensor_tensor(w.YL[f, 0, CH:], w.YL[f, 0, CH:], y[:, 0, CH:], ALU.add).then_inc(w.s_yl, 1)
            done(f"y{s}", dve.tensor_tensor(w.YL[f, 1:], w.YL[f, 1:], y[:, 1:], ALU.add))
        prepare(j + 1, 6)
        dve.wait_ge(w.s_yl, 2 * j + 2)
        own(j, "y1")
        E(j, "mean")
        done("yc", dve.scalar_tensor_tensor(out=w.yc, in0=blocks(ps[:, 5]), scalar=-1.0 / HD, in1=w.YL, op0=ALU.mult,
                                            op1=ALU.add))
        A(j, "yroot")
        done("yrec", dve.reciprocal(w.norm[:, 1], w.norm[:, 0]))
        own(j, "yrec")
        done("yrecx", dve.tensor_copy(w.ysq.rearrange("p b (s n) -> p (b s) n", s=2), spread(w.norm)))
        E(j, "yrb")
        done("yn", dve.tensor_tensor(w.yc, w.yc, blocks(ps[:, 7]), ALU.mult))
        own(j, "yn")
        done("ylnb", dve.tensor_scalar(w.yc, w.yc, c.column("l0_lnx_w_2", j), c.column("l0_lnx_b_2", j), ALU.mult, ALU.add))
        own(j, "ylnb")
        mine(j, "bon")
        done("ysum", dve.tensor_tensor(blocks(w.y32[:, j]), blocks(w.y32[:, j]), w.yc, ALU.add))
        E(j, "lora_g")
        own(j, "ysum")
        done("out", dve.tensor_tensor(w.y32[:, j], w.y32[:, j], ps[:, 4], ALU.mult))
    for k in range(KD):
        src = w.y32[:, k] if k < 4 else c.o32[:, k - 4]
        dve.wait_ge(w.s_whi, 2 + k + 1)
        dve.tensor_tensor(c.xn_lo[:, k], src, c.xn_hi[:, k].bitcast(F32), ALU.subtract).then_inc(c.s_xn, 1)


CONSTANT_PARTS = 12


def rwkv_constants(pool, c, part):
    def select(ap, pattern, base, mult, op=ALU.is_ge, fill=0.0):
        pool.wait_ge(c.s_zeroed, c.zeroed)
        pool.affine_select(out=ap, in_=ap, compare_op=op, fill=fill, base=base, pattern=pattern,
                           channel_multiplier=mult).then_inc(c.s_zeroed, 1)
        c.zeroed += 1

    if part == 0:
        for ap, value in ((c.level, 1.0), (c.mask4, 1.0), (c.ones_head, 1.0), (c.ident_head, 0.0), (c.gn_eps, GN_EPS),
                          (c.ln_eps, LN_EPS)):
            pool.memset(ap[:], value).then_inc(c.s_zeroed, 1)
            c.zeroed += 1
    elif part <= 6:
        x = part - 1
        m = ((1,) + LEVELS)[x]
        n = P // (2 * m)
        ap = c.level[:, x].rearrange("p (q h r) -> p q h r", h=2, r=m)
        select(ap, [[-2 * m, n], [0, 2], [0, m]], -m, 1)
        select(ap, [[2 * m, n], [0, 2], [0, m]], 2 * m - 1, -1)
        select(ap, [[0, n], [-1, 2], [0, m]], 0, 0)
    elif part == 7:
        ap = c.level[:, 6].rearrange("p (q h) -> p q h", h=2)
        select(ap, [[-2, P // 2], [0, 2]], 0, 1, op=ALU.is_equal)
        select(ap, [[0, P // 2], [1, 2]], -1, 0)
    elif part <= 9:
        for x in range(2 * (part - 8), 2 * (part - 8) + 2):
            ap = c.mask4[:, x].rearrange("p (c n) -> p c n", n=CH)
            select(ap, [[CH, 2], [1, CH]], -1 if x % 2 == 0 else 0, -1)
            select(ap, [[-CH, 2], [0, CH]], 0, 1)
    elif part == 10:
        ap = c.ones_head[:].rearrange("p (h n) -> p h n", n=HD)
        select(ap, [[-HD, 2], [0, HD]], 0, 1)
        select(ap, [[HD, 2], [0, HD]], HD - 1, -1)
    elif part == 11:
        for h in range(2):
            select(c.ident_head[:], [[-1, HD]], -HD * h, 1, op=ALU.not_equal, fill=1.0)
        pool.wait_ge(c.s_zeroed, c.zeroed)
        pool.nop().then_inc(c.s_const2, 1)



def mlp_up_act(act, c, base, nf):
    with act.Fori(0, nf // RING) as i:
        for s in range(RING):
            u, slot = base + s, (base + s) % RING
            stream_high_ahead(act, c, i, base, s)
            act.wait_ge(c.s_pe, i * RING + (u + START + 1))
            act.wait_ge(c.s_evac, i * RING + (u + START - 1))
            act.activation(c.gate[:, s % 2], c.ps[:, slot], ACT.Relu).then_inc(c.s_act, 1)


def mlp_up_dve(dve, c, base, nf, hid_base, act_base):
    dve.wait_ge(c.s_pe, base + START)
    with dve.Fori(0, nf // RING) as i:
        for s in range(RING):
            u = base + s
            dve.wait_ge(c.s_pe, i * RING + (u + START + 1))
            dve.wait_ge(c.s_act, i * RING + (act_base + s + 1))
            dve.wait_ge(c.s_hid, i * RING + (hid_base + START + s - 1))
            dve.tensor_tensor(c.h[:, s % 2], c.gate[:, s % 2], c.ps[:, u % RING], ALU.mult).then_inc(c.s_evac, 1)
            dve.wait_ge(c.s_evac, i * RING + (u + START + 1))
            dve.tensor_copy(c.hid_hi[:, i * RING + s], c.h[:, s % 2]).then_inc(c.s_hhi, 1)
            dve.wait_ge(c.s_hhi, i * RING + (hid_base + s + 1))
            dve.tensor_tensor(c.hid_lo[:, i * RING + s], c.h[:, s % 2], c.hid_hi[:, i * RING + s].bitcast(F32),
                              ALU.subtract).then_inc(c.s_hid, 1)



TAPS = 31
TAP_UNITS = (1, 1, 1, 1, 1, 2, 2, 3)


def conv_units():
    order = []
    for n in range(KD + 1):
        order += [("value", n), ("gate", n)] if n < KD else []
        order += [("taps", n - 1)] * TAP_UNITS[n - 1] if n >= 1 else []
    return order


CONV_UNITS = conv_units()


def tap_part(j):
    return j - CONV_UNITS.index(CONV_UNITS[j])


def conv_tensors(c, sb, sem):
    v = Parts()
    v.u = sb("cu", [P, 2, TAPS - 1 + T])
    v.u_hi = sb("cu_hi", [P, 2, TAPS - 1 + T], F32R)
    v.u_lo = sb("cu_lo", [P, 2, TAPS - 1 + T], F32R)
    v.gate = sb("cgate", [P, 2, T])
    v.acc = sb("cacc", [P, 2, T])
    v.out = sb("cout", [P, KD, T])
    v.sum = sb("csum", [P, T])
    v.mean = sb("cmean", [P, TT])
    v.square = sb("csquare", [P, TT])
    v.taps = sb("ctaps", [P, KD, TAPS])
    v.s_vgate, v.s_vu, v.s_vtap, v.s_vout = sem("s_vgate"), sem("s_vu"), sem("s_vtap"), sem("s_vout")
    v.s_vuhi, v.s_vulo, v.s_vpart = sem("s_vuhi"), sem("s_vulo"), sem("s_vpart")
    v.s_vsq, v.s_vsum, v.s_vstat, v.s_vroot = sem("s_vsq"), sem("s_vsum"), sem("s_vstat"), sem("s_vroot")
    v.s_vn, v.s_vsilu, v.s_vload, v.s_vmean = sem("s_vn"), sem("s_vsilu"), sem("s_vload"), sem("s_vmean")
    return v


def conv_pe(pe, c, v, base, xn_ready):
    first_two_units(pe, c, base, lambda k: c.xn_hi[:, k], lambda k: c.xn_lo[:, k],
                    lambda k: pe.wait_ge(c.s_xn, xn_ready + k + 1))
    for j, (kind, n) in enumerate(CONV_UNITS):
        if j < 2:
            continue
        u = base + j
        pe.wait_ge(c.s_lo, u + 1)
        part = tap_part(j) if kind == "taps" else 0
        if part == 0:
            pe.wait_ge(c.s_evac, u + START + 1 - RING)
        if kind == "taps":
            pe.wait_ge(v.s_vulo, n + 1)
            split_products(pe, c, c.ps[:, (u - part) % RING], u % RING, lambda t: v.u_hi[:, n % 2, t:t + T],
                           lambda t: v.u_lo[:, n % 2, t:t + T], range(KU), k0=part * KU, start=part == 0,
                           stop=part == TAP_UNITS[n] - 1).then_inc(c.s_pe, 1)
        else:
            split_products(pe, c, c.ps[:, u % RING], u % RING, lambda k: c.xn_hi[:, k], lambda k: c.xn_lo[:, k],
                           range(KD)).then_inc(c.s_pe, 1)
    pe.wait_ge(v.s_vsum, 2 * KD - 1)
    for t in range(TT):
        pe.matmul(c.ps[:, 5, t:t + 1], v.sum[:, t * P:t * P + P], c.ones[:, 0:1], start=True, stop=True)
    pe.wait_ge(v.s_vsum, 2 * KD)
    for t in range(TT):
        mm = pe.matmul(c.ps[:, 5, TT + t:TT + t + 1], c.ss[:, t * P:t * P + P], c.ones[:, 0:1], start=True, stop=True)
    mm.then_inc(v.s_vstat, 1)
    pe.wait_ge(v.s_vmean, 5)
    token_values_pe(pe, c, 6, c.rstd_t)
    token_values_pe(pe, c, 7, v.mean).then_inc(v.s_vstat, 1)


def conv_act(act, c, v, base):
    act.wait_ge(c.s_pe, base + START)
    act.wait_ge(c.s_ss, KD * 7)
    act.dma_start(v.taps[:], c.dw).then_inc(v.s_vload, 16)

    def square(n):
        act.wait_ge(v.s_vout, n + 1)
        if n >= 2:
            act.wait_ge(v.s_vsum, 2 * (n - 1))
        act.activation(c.sq[:, n % 2], v.out[:, n], ACT.Square).then_inc(v.s_vsq, 1)

    for j, (kind, n) in enumerate(CONV_UNITS):
        u = base + j
        stream_high(act, c, u + RING - 1, (u + RING - 1) % RING, (u + RING - 1) // RING)
        if kind == "gate":
            act.wait_ge(c.s_pe, u + START + 1)
            if n >= 2:
                act.wait_ge(v.s_vu, n - 1)
            act.activation(v.gate[:, n % 2], c.ps[:, u % RING], ACT.Sigmoid,
                           bias=c.column("l1_pw1_b_2", KD + n)).then_inc(v.s_vgate, 1)
            act.wait_ge(v.s_vu, n + 1)
            if n >= 2:
                act.wait_ge(c.s_pe, base + CONV_UNITS.index(("taps", n - 2)) + TAP_UNITS[n - 2] + START)
            act.activation(v.u_hi[:, n % 2], v.u[:, n % 2], ACT.Copy).then_inc(v.s_vuhi, 1)
        if kind == "value" and n >= 3:
            square(n - 3)
        if (kind, n) == ("taps", KD - 1) and tap_part(j) == 0:
            square(KD - 3)
    for n in range(KD - 2, KD):
        square(n)
    act.wait_ge(v.s_vmean, 3)
    act.activation(c.root_t[:], c.rstd_t[:], ACT.Sqrt, bias=c.ln_eps[:, 0:1]).then_inc(v.s_vroot, 1)
    for k in range(KD):
        act.wait_ge(v.s_vn, k + 1)
        act.activation(v.out[:, k], v.out[:, k], ACT.Silu, bias=c.column("l1_ln_b_2", k),
                       scale=c.column("l1_ln_w_2", k)).then_inc(v.s_vsilu, 1)
        act.wait_ge(v.s_vsilu, k + 1)
        act.activation(c.xn_hi[:, k], v.out[:, k], ACT.Copy).then_inc(c.s_xhi, 1)


def conv_pool(pool, c, v, base):
    def sums(n):
        pool.wait_ge(v.s_vout, n + 1)
        if n == 0:
            pool.tensor_copy(v.sum[:], v.out[:, 0]).then_inc(v.s_vsum, 1)
            pool.wait_ge(v.s_vsq, 1)
            pool.tensor_copy(c.ss[:], c.sq[:, 0]).then_inc(v.s_vsum, 1)
        else:
            pool.wait_ge(v.s_vsum, 2 * n)
            pool.tensor_tensor(v.sum[:], v.sum[:], v.out[:, n], ALU.add).then_inc(v.s_vsum, 1)
            pool.wait_ge(v.s_vsq, n + 1)
            pool.tensor_tensor(c.ss[:], c.ss[:], c.sq[:, n % 2], ALU.add).then_inc(v.s_vsum, 1)

    for j, (kind, n) in enumerate(CONV_UNITS):
        stream_low(pool, c, base + j + RING - 1, base + j + RING)
        if kind == "gate":
            pool.wait_ge(v.s_vuhi, n + 1)
            pool.tensor_tensor(v.u_lo[:, n % 2], v.u[:, n % 2], v.u_hi[:, n % 2].bitcast(F32),
                               ALU.subtract).then_inc(v.s_vulo, 1)
        if kind == "value" and n >= 3:
            sums(n - 3)


def conv_square(dve, c, v, n):
    dve.wait_ge(v.s_vsq, n + 1)
    dve.wait_ge(v.s_vsum, 2 * n + 1)
    dve.tensor_tensor(c.ss[:], c.ss[:], c.sq[:, n % 2], ALU.add).then_inc(v.s_vsum, 1)


def conv_dve(dve, c, v, base, xhi_base):
    dve.wait_ge(c.s_pe, base + START)
    for b in range(2):
        dve.memset(v.u[:, b, 0:TAPS - 1], 0.0).then_inc(v.s_vload, 16)
    dve.wait_ge(v.s_vload, 48)
    taps_of = [TAPS - KU * x for x in TAP_UNITS]
    taps_before = [sum(taps_of[:n]) for n in range(KD + 1)]
    for j, (kind, n) in enumerate(CONV_UNITS):
        u = base + j
        if kind == "gate":
            dve.wait_ge(c.s_pe, u + START + 1)
            dve.wait_ge(v.s_vgate, n + 1)
            if n >= 2:
                dve.wait_ge(v.s_vulo, n - 1)
                dve.wait_ge(v.s_vtap, taps_before[n - 1])
            dve.scalar_tensor_tensor(out=v.u[:, n % 2, TAPS - 1:], in0=c.ps[:, (u - 1) % RING],
                                     scalar=c.column("l1_pw1_b_2", n), in1=v.gate[:, n % 2], op0=ALU.add,
                                     op1=ALU.mult).then_inc(v.s_vu, 1)
            dve.wait_ge(v.s_vu, n + 1)
            dve.nop().then_inc(c.s_evac, 2)
        elif kind == "taps" and tap_part(j) == TAP_UNITS[n] - 1:
            before, per, first = taps_before[n], taps_of[n], KU * TAP_UNITS[n]
            if n >= 1:
                dve.wait_ge(v.s_vout, n)
            for x in range(per):
                t, acc = first + x, v.acc[:, x % 2]
                src, w = v.u[:, n % 2, t:t + T], v.taps[:, n, t:t + 1]
                if x >= 2:
                    dve.wait_ge(v.s_vtap, before + x - 1)
                    dve.scalar_tensor_tensor(out=acc, in0=src, scalar=w, in1=acc, op0=ALU.mult,
                                             op1=ALU.add).then_inc(v.s_vtap, 1)
                elif x == 0:
                    dve.tensor_scalar(acc, src, w, c.column("l1_dw_b_2", n), ALU.mult, ALU.add).then_inc(v.s_vtap, 1)
                else:
                    dve.tensor_scalar(acc, src, w, None, ALU.mult).then_inc(v.s_vtap, 1)
            dve.wait_ge(c.s_pe, u + START + 1)
            dve.wait_ge(v.s_vtap, before + per - 1)
            last = (per - 2) % 2
            dve.tensor_tensor(v.acc[:, last], v.acc[:, last], c.ps[:, (u + 1 - TAP_UNITS[n]) % RING],
                              ALU.add).then_inc(v.s_vpart, 1)
            dve.wait_ge(v.s_vtap, before + per)
            dve.wait_ge(v.s_vpart, n + 1)
            dve.tensor_tensor(v.out[:, n], v.acc[:, 0], v.acc[:, 1], ALU.add).then_inc(v.s_vout, 1)
            dve.wait_ge(v.s_vout, n + 1)
            dve.nop().then_inc(c.s_evac, TAP_UNITS[n])
            if n >= KD - 3:
                if n > KD - 3:
                    conv_square(dve, c, v, n - 1)
                dve.wait_ge(v.s_vsum, 2 * n)
                dve.tensor_tensor(v.sum[:], v.sum[:], v.out[:, n], ALU.add).then_inc(v.s_vsum, 1)
    conv_square(dve, c, v, KD - 1)
    dve.wait_ge(v.s_vstat, 1)
    dve.tensor_scalar(v.mean[:], c.ps[:, 5, 0:TT], 1.0 / D, None, ALU.mult).then_inc(v.s_vmean, 1)
    dve.wait_ge(v.s_vmean, 1)
    dve.tensor_tensor(v.square[:], v.mean[:], v.mean[:], ALU.mult).then_inc(v.s_vmean, 1)
    dve.wait_ge(v.s_vmean, 2)
    dve.scalar_tensor_tensor(out=c.rstd_t[:], in0=c.ps[:, 5, TT:2 * TT], scalar=1.0 / D, in1=v.square[:], op0=ALU.mult,
                             op1=ALU.subtract).then_inc(v.s_vmean, 1)
    dve.wait_ge(v.s_vroot, 1)
    dve.reciprocal(c.rstd_t[:], c.root_t[:]).then_inc(v.s_vmean, 1)
    dve.wait_ge(v.s_vmean, 4)
    dve.scalar_tensor_tensor(out=v.mean[:], in0=v.mean[:], scalar=-1.0, in1=c.rstd_t[:], op0=ALU.mult,
                             op1=ALU.mult).then_inc(v.s_vmean, 1)
    dve.wait_ge(v.s_vstat, 2)

    def low(k):
        dve.wait_ge(c.s_xhi, xhi_base + k + 1)
        dve.tensor_tensor(c.xn_lo[:, k], v.out[:, k], c.xn_hi[:, k].bitcast(F32), ALU.subtract).then_inc(c.s_xn, 1)

    for k in range(KD):
        dve.tensor_tensor(v.out[:, k], v.out[:, k], c.ps[:, 6], ALU.mult).then_inc(v.s_vmean, 1)
        dve.wait_ge(v.s_vmean, 6 + k)
        dve.tensor_tensor(v.out[:, k], v.out[:, k], c.ps[:, 7], ALU.add).then_inc(v.s_vn, 1)
        if k >= 1:
            low(k - 1)
    low(KD - 1)



def renorm_act(act, c, i):
    norm_act_root(act, c, i)
    for k in range(KD):
        act.wait_ge(c.s_y, KD * i + k + 1)
        act.wait_ge(c.s_ss, KD * (i + 1) + k - 1)
        act.activation(c.sq[:, k % 2], c.x[:, k], ACT.Square).then_inc(c.s_sq, 1)


def renorm_dve(dve, c, i, gain):
    norm_dve_scale(dve, c, i)
    dve.memset(c.ss[:], 0.0).then_inc(c.s_zero, 1)
    dve.wait_ge(c.s_zero, i + 1)
    for k in range(KD):
        dve.scalar_tensor_tensor(out=c.x[:, k], in0=c.x[:, k], scalar=c.column(gain, k), in1=c.ps[:, 5],
                                 op0=ALU.mult, op1=ALU.mult).then_inc(c.s_y, 1)
    for k in range(KD):
        dve.wait_ge(c.s_sq, KD * (i + 1) + k + 1)
        dve.wait_ge(c.s_ss, KD * (i + 1) + k)
        dve.tensor_tensor(c.ss[:], c.ss[:], c.sq[:, k % 2], ALU.add).then_inc(c.s_ss, 1)



def output_dve(dve, c, i, gain):
    norm_dve_scale(dve, c, i)
    for k in range(KD):
        dve.scalar_tensor_tensor(out=c.x[:, k], in0=c.x[:, k], scalar=c.par[:, COL[gain] + k:COL[gain] + k + 1],
                                 in1=c.ps[:, 5], op0=ALU.mult, op1=ALU.mult).then_inc(c.s_y, 1)
    for t in range(TT):
        for half in range(2):
            dve.wait_ge(c.s_tout, 2 * t + half + 1)
            dve.tensor_copy(c.stage[:, t, half * 512:half * 512 + 512], c.ps[:, 2 * (t % 2) + half]).then_inc(c.s_out, 1)


def output_pe(pe, c, i):
    for t in range(TT):
        for k in range(KD):
            if t == 0:
                pe.wait_ge(c.s_y, KD * i + k + 1)
            if t >= 2 and k % 4 == 0:
                pe.wait_ge(c.s_out, 2 * (t - 2) + k // 4 + 1)
            mm = pe.transpose(c.ps[:, 2 * (t % 2) + k // 4, k % 4 * P:k % 4 * P + P], c.x[:, k, t * P:t * P + P],
                              c.ident[:])
            if k % 4 == 3:
                mm.then_inc(c.s_tout, 1)


def output_sp(sp, c):
    for t in range(TT):
        sp.wait_ge(c.s_out, 2 * t + 2)
        sp.dma_start(c.out[t], c.stage[:, t]).then_inc(c.s_stored, 16)
    sp.wait_ge(c.s_stored, 16 * TT)


def constants_pool(pool, c):
    pool.memset(c.ident[:], 0.0).then_inc(c.s_zeroed, 1)
    c.zeroed += 1
    pool.wait_ge(c.s_zeroed, 1)
    pool.affine_select(out=c.ident[:], in_=c.ident[:], compare_op=ALU.not_equal, fill=1.0, base=0,
                       pattern=[[-1, P]], channel_multiplier=1).then_inc(c.s_const, 1)
    pool.memset(c.eps[:], EPS).then_inc(c.s_zeroed, 1)
    c.zeroed += 1
    pool.memset(c.ones[:], 1.0).then_inc(c.s_const, 1)


def program(nc, x, weights, params, lora, table, dw, out):
    ctx = ExitStack()
    with ctx:
        def sb(name, shape, dt=F32, scope=ctx):
            return scope.enter_context(nc.sbuf_tensor("sb_" + name, shape, dt))

        def sem(name):
            return ctx.enter_context(nc.semaphore(name))

        c = Parts()
        c.weights, c.lora, c.table, c.dw = weights, lora, table, dw
        c.out = out.rearrange("a (t p) d -> (a t) p d", p=P)
        c.ps = ctx.enter_context(nc.psum_tensor("ps", [P, 8, 512], F32))
        c.x = sb("x", [P, KD, T])
        c.xn_hi = sb("xn_hi", [P, KD, T], F32R)
        c.xn_lo = sb("xn_lo", [P, KD, T], F32R)
        c.w_raw = sb("w_raw", [P, RING, KU, P])
        c.w_hi = sb("w_hi", [P, RING, KU, P], F32R)
        c.w_lo = sb("w_lo", [P, RING, KU, P], F32R)
        c.ident = sb("ident", [P, P])
        c.ones = sb("ones", [P, P])
        c.eps = sb("eps", [P, 1])
        c.par = sb("par", [P, NCOL])
        c.sinks = c.par[:, SINKS:CMP_W2]
        c.dist = sb("dist", [P, T])
        c.dist_local = sb("dist_local", [P, 2 * P])
        c.dist_cmp = sb("dist_cmp", [P, TT, 32])
        c.sees_block = sb("sees_block", [P, 1])
        c.level = sb("level", [P, 7, P], BF16)
        c.mask4 = sb("mask4", [P, 4, P], BF16)
        c.ones_head = sb("ones_head", [P, P])
        c.ident_head = sb("ident_head", [P, HD])
        c.gn_eps = sb("gn_eps", [P, 1])
        c.ln_eps = sb("ln_eps", [P, 1])
        c.omka = sb("omka", [P, 4])
        c.zeroed = 0
        c.ss = sb("ss", [P, T])
        c.rstd = sb("rstd", [P, T])
        c.root = sb("root", [P, T])
        c.sum_t = sb("sum_t", [P, TT])
        c.root_t = sb("root_t", [P, TT])
        c.rstd_t = sb("rstd_t", [P, TT])
        c.y = sb("y", [P, 3, T])
        c.sq = c.y
        with ExitStack() as region:
            c.stage = sb("stage", [P, TT, D], scope=region)
        with ExitStack() as region:
            c.hid_hi = sb("hid_hi", [P, F1A, T], F32R, region)
            c.hid_lo = sb("hid_lo", [P, F1A, T], F32R, region)
            c.gate = sb("gate", [P, 2, T], scope=region)
            c.h = sb("h", [P, 2, T], scope=region)
        with ExitStack() as region:
            with ExitStack() as sub:
                blk = sb("blk", [P, 2, 16, HD], scope=sub)
            m = mixer_tensors(c, lambda name, shape, dt=F32: sb(name, shape, dt, region), sem)
            m.blk = blk
            with ExitStack() as inner:
                m.blk_hi = sb("blk_hi", [P, 2, 16, HD], F32R, inner)
                m.blk_lo = sb("blk_lo", [P, 2, 16, HD], F32R, inner)
                m.sig = sb("sig", [P, T], scope=inner)
            m.chid = c.ss[:, 0:4 * HD].rearrange("p (q n) -> p q n", n=HD)
            flat = lambda ap: ap[:, 0:5].rearrange("p (a k) n -> p a (k n)", a=1)[:, 0].rearrange("p (a n) -> p a n", a=2)
            a = attention_buffers(c, lambda name, shape, dt=F32: sb(name, shape, dt, region), sem, "a_",
                                  m.q[:, 0:16:2], m.q[:, 1:16:2], pt=(flat(c.xn_hi), flat(c.xn_lo)))
        m.w2 = c.par[:, CMP_W2:NCOL].rearrange("p (a t n) -> p a t n", a=2, t=2)
        c.column = lambda name, j: c.par[:, COL[name] + j:COL[name] + j + 1]
        with ExitStack() as region:
            rsb = lambda name, shape, dt=F32: sb(name, shape, dt, region)
            c.o32 = rsb("o32", [P, 4, T])
            with ExitStack() as inner:
                isb = lambda name, shape, dt=F32: sb(name, shape, dt, inner)
                t = att_tensors(c, isb, sem)
                ta = attention_buffers(c, isb, sem, "t0_", o32=c.o32)
                tb = attention_view(ta, c.o32[:, 2:4], sem, "t1_")
            w = rwkv_tensors(c, rsb, sem)
        with ExitStack() as region:
            v = conv_tensors(c, lambda name, shape, dt=F32: sb(name, shape, dt, region), sem)
        c.s_raw = [sem(f"s_raw{i}") for i in range(RING)]
        c.s_hi = sem("s_hi")
        c.s_lo = sem("s_lo")
        c.s_pe = sem("s_pe")
        c.s_evac = sem("s_evac")
        c.s_const = sem("s_const")
        c.s_zeroed = sem("s_zeroed")
        c.s_load = [sem(f"s_load{t}") for t in range(TT)]
        c.s_tin = sem("s_tin")
        c.s_x = sem("s_x")
        c.s_sq = sem("s_sq")
        c.s_ss = sem("s_ss")
        c.s_zero = sem("s_zero")
        c.s_msum = sem("s_msum")
        c.s_root = sem("s_root")
        c.s_rstd = sem("s_rstd")
        c.s_spread = sem("s_spread")
        c.s_sum_t = sem("s_sum_t")
        c.s_y = sem("s_y")
        c.s_xhi = sem("s_xhi")
        c.s_xn = sem("s_xn")
        c.s_act = sem("s_act")
        c.s_hhi = sem("s_hhi")
        c.s_hid = sem("s_hid")
        c.s_tout = sem("s_tout")
        c.s_out = sem("s_out")
        c.s_stored = sem("s_stored")
        c.s_par = sem("s_par")
        c.s_const2 = sem("s_const2")
        c.s_xb = sem("s_xb")
        block = ctx.enter_context(nc.Block())
        B = BASE

        @block.sync
        def _(sp):
            for t in range(TT):
                sp.dma_start(c.stage[:, t], x[0, t * P:t * P + P]).then_inc(c.s_load[t], 16)
            sp.dma_start(c.par[:], params).then_inc(c.s_par, 16)
            stream_load(sp, c)
            output_sp(sp, c)

        passes = mixer_passes(c, a, m)

        @block.gpsimd
        def _(pool):
            constants_pool(pool, c)
            mixer_constants(pool, c)
            split = min(UNITS, B.get("mix_out", 0) + RING - 1)
            stream_low(pool, c, 0, split)
            for part in range(CONSTANT_PARTS):
                rwkv_constants(pool, c, part)
            conv = B["pw1"]
            stream_low(pool, c, split, conv + RING - 1)
            conv_pool(pool, c, v, conv)
            stream_low(pool, c, conv + len(CONV_UNITS) + RING - 1, UNITS)

        last = 8

        @block.scalar
        def _(act):
            input_act(act, c)
            for u in range(RING - 1):
                act.wait_ge(c.s_raw[u], 16)
                act.activation(c.w_hi[:, u], c.w_raw[:, u], ACT.Copy).then_inc(c.s_hi, 1)

            def ffn(name, f, i, nxt):
                norm_act_root(act, c, i)
                norm_act_high(act, c, i)
                glu_up_act(act, c, B[name + "_upA"], F1A, f)
                down_act(act, c, B[name + "_downA"], F1A)
                glu_up_act(act, c, B[name + "_upB"], F1 - F1A, f + F1A)
                down_act(act, c, B[name + "_downB"], F1 - F1A, KD * nxt)

            def mlp(name, i, nxt):
                norm_act_root(act, c, i)
                norm_act_high(act, c, i)
                mlp_up_act(act, c, B[name + "_upA"], F1A)
                down_act(act, c, B[name + "_downA"], F1A)
                mlp_up_act(act, c, B[name + "_upB"], F1A)
                down_act(act, c, B[name + "_downB"], F1A, KD * nxt)

            ffn("ffn1", 0, 0, 1)
            norm_act_root(act, c, 1)
            norm_act_high(act, c, 1)
            mixer_in_act(act, c, m, B["mix_in"])
            attention_act(act, c, a, passes)
            down_act(act, c, B["mix_out"], KD, 2 * KD)
            ffn("ffn2", F1, 2, 3)
            renorm_act(act, c, 3)
            norm_act_root(act, c, 4)
            norm_act_high(act, c, 4)
            for half, x in ((0, ta), (1, tb)):
                att_in_act(act, c, t, half)
                attention_act(act, c, x, att_passes(c, x, t, half))
            rwkv_act(act, c, w, B["rwkv_in"] + 12)
            down_act(act, c, B["rwkv_out"], KD, 5 * KD)
            mlp("mlp0", 5, 6)
            norm_act_root(act, c, 6)
            norm_act_high(act, c, 6)
            conv_act(act, c, v, B["pw1"])
            down_act(act, c, B["pw2"], KD, 7 * KD)
            mlp("mlp1", 7, 8)
            norm_act_root(act, c, last)

        @block.tensor
        def _(pe):
            def hid_ready(base):
                return lambda k: pe.wait_ge(c.s_hid, base + START + k + 1)

            def ffn(name, f, i, xn):
                norm_pe(pe, c, i)
                up_pe(pe, c, B[name + "_upA"], 2 * F1A, xn, True)
                down_pe(pe, c, B[name + "_downA"], F1A, c.hid_hi, c.hid_lo, hid_ready(f))
                up_pe(pe, c, B[name + "_upB"], 2 * (F1 - F1A), xn, False)
                down_pe(pe, c, B[name + "_downB"], F1 - F1A, c.hid_hi, c.hid_lo, hid_ready(f + F1A))

            def mlp(name, f, i, xn):
                norm_pe(pe, c, i)
                up_pe(pe, c, B[name + "_upA"], F1A, xn, True)
                down_pe(pe, c, B[name + "_downA"], F1A, c.hid_hi, c.hid_lo, hid_ready(f))
                up_pe(pe, c, B[name + "_upB"], F1A, xn, False)
                down_pe(pe, c, B[name + "_downB"], F1A, c.hid_hi, c.hid_lo, hid_ready(f + F1A))

            input_pe(pe, c)
            ffn("ffn1", 0, 0, 0)
            norm_pe(pe, c, 1)
            mixer_in_pe(pe, c, m, B["mix_in"], KD)
            attention_pe(pe, c, a, passes)
            down_pe(pe, c, B["mix_out"], KD, a.o_hi, a.o_lo, lambda k: pe.wait_ge(a.s_olow, 2 * k + 2), True)
            ffn("ffn2", F1, 2, 2 * KD)
            norm_pe(pe, c, 3)
            norm_pe(pe, c, 4)
            for half, x in ((0, ta), (1, tb)):
                att_in_pe(pe, c, t, half, 3 * KD)
                attention_pe(pe, c, x, att_passes(c, x, t, half))
            pe.wait_ge(c.s_const2, 1)
            rwkv_pe(pe, c, w, B["rwkv_in"] + 12)
            down_pe(pe, c, B["rwkv_out"], KD, c.xn_hi, c.xn_lo, lambda k: pe.wait_ge(c.s_xn, 4 * KD + k + 1), True)
            mlp("mlp0", 2 * F1, 5, 5 * KD)
            norm_pe(pe, c, 6)
            conv_pe(pe, c, v, B["pw1"], 6 * KD)
            down_pe(pe, c, B["pw2"], KD, c.xn_hi, c.xn_lo, lambda k: pe.wait_ge(c.s_xn, 7 * KD + k + 1), True)
            mlp("mlp1", 2 * F1 + F2, 7, 8 * KD)
            norm_pe(pe, c, last)
            output_pe(pe, c, last)

        @block.vector
        def _(dve):
            def ffn(name, f, i, gain, xhi, nxt):
                norm_dve(dve, c, i, gain, xhi, xhi)
                glu_up_dve(dve, c, B[name + "_upA"], F1A, f, f, B[name + "_upA"])
                down_dve(dve, c, B[name + "_downA"], F1A, 0.5)
                glu_up_dve(dve, c, B[name + "_upB"], F1 - F1A, f + F1A, f + F1A, B[name + "_upB"])
                down_dve(dve, c, B[name + "_downB"], F1 - F1A, 0.5, KD * nxt)

            def mlp(name, f, i, gain, xhi, xn, nxt):
                norm_dve(dve, c, i, gain, xhi, xn)
                mlp_up_dve(dve, c, B[name + "_upA"], F1A, f, f)
                down_dve(dve, c, B[name + "_downA"], F1A, 1.0)
                mlp_up_dve(dve, c, B[name + "_upB"], F1A, f + F1A, f + F1A)
                down_dve(dve, c, B[name + "_downB"], F1A, 1.0, KD * nxt)

            input_dve(dve, c)
            dve.wait_ge(c.s_par, 16)
            ffn("ffn1", 0, 0, "ffn1_norm", 0, 1)
            norm_dve(dve, c, 1, "mix_norm", KD, KD)
            mixer_in_dve(dve, c, m, B["mix_in"])
            attention_dve(dve, c, a, passes)
            down_dve(dve, c, B["mix_out"], KD, 1.0, 2 * KD)
            ffn("ffn2", F1, 2, "ffn2_norm", 2 * KD, 3)
            renorm_dve(dve, c, 3, "final_norm")
            norm_dve(dve, c, 4, "l0_norm_mix_2", 3 * KD, 3 * KD)
            for half, x in ((0, ta), (1, tb)):
                att_in_dve(dve, c, t, half)
                attention_dve(dve, c, x, att_passes(c, x, t, half))
            dve.wait_ge(c.s_const2, 1)
            rwkv_dve(dve, c, w, B["rwkv_in"] + 12)
            down_dve(dve, c, B["rwkv_out"], KD, 1.0, 5 * KD)
            mlp("mlp0", 2 * F1, 5, "l0_norm_ffn_2", 4 * KD, 5 * KD, 6)
            norm_dve(dve, c, 6, "l1_norm_mix_2", 5 * KD, 6 * KD)
            conv_dve(dve, c, v, B["pw1"], 6 * KD)
            down_dve(dve, c, B["pw2"], KD, 1.0, 7 * KD, bias="l1_pw2_b_2")
            mlp("mlp1", 2 * F1 + F2, 7, "l1_norm_ffn_2", 7 * KD, 8 * KD, 8)
            output_dve(dve, c, last, "final_norm_2")



def diagonal(values):
    m = np.zeros((P, P), np.float32)
    m[np.arange(P), np.arange(P)] = values
    return m


def weight_units(a):
    units = np.zeros((UNITS, P, KU, P), np.float32)
    at = [0]

    def put(block):
        rows, cols = block.shape
        kt = rows // P
        units[at[0], :, 0:kt, 0:cols] = block.reshape(kt, P, cols).transpose(1, 0, 2)
        at[0] += 1

    def ffn(up, gated, down):
        tiles = down.shape[0] // P
        for lo in range(0, tiles, F1A):
            hi = min(tiles, lo + F1A)
            for f in range(lo, hi):
                put(up[:, f * P:f * P + P])
                if gated:
                    put(up[:, (tiles + f) * P:(tiles + f) * P + P])
            for n in range(KD):
                for k in range(lo, hi, KU):
                    put(down[k * P:min(k + KU, hi) * P, n * P:n * P + P])

    ffn(a["ffn1_w_in"][0], True, a["ffn1_w_out"][0])
    w = a["w_mix_in"][0]
    pair = lambda off, j: np.concatenate([w[:, off + HD * h:off + HD * h + HD] for h in (j, j + 4)], 1)
    kv = lambda i: w[:, 512 + i * P:512 + i * P + P]
    tiles = {"kc": kv(0), "vc": kv(1), "ks": kv(2), "kw": kv(4), "kb": w[:, 1816:1816 + P],
             "vs": kv(3), "vw": kv(5), "vb": w[:, 1944:1944 + P], "gate": w[:, 1280:1304]}
    for j in range(4):
        tiles[f"qa{j}"], tiles[f"qb{j}"] = pair(0, j), pair(1304, j)
    for unit in MIX_UNITS:
        if unit in tiles:
            put(tiles[unit])
        else:
            q, half = unit
            hidden = a["cmp_k_w1" if q < 2 else "cmp_v_w1"][0]
            put(hidden[half * D:half * D + D, q % 2 * P:q % 2 * P + P])
    rows = np.concatenate([np.arange(HD) + off + HD * h for off in (0, 512) for j in range(4) for h in (j, j + 4)])
    for n in range(KD):
        put(a["w_mix_out"][0][rows, n * P:n * P + P])
    ffn(a["ffn2_w_in"][0], True, a["ffn2_w_out"][0])
    w = a["l0_w_in_2"]
    tile = lambda t: put(w[:, t * P:t * P + P])
    for half in range(2):
        for off in (14, 18, 22):
            tile(off + 2 * half), tile(off + 2 * half + 1)
    tile(12), tile(13)
    for j in range(PAIRS):
        tile(j), tile(4 + j), tile(8 + j)
    for n in range(KD):
        put(a["l0_w_out_2"][:, n * P:n * P + P])
    ffn(a["l0_ffn_up_2"], False, a["l0_ffn_down_2"])
    for j, (kind, n) in enumerate(CONV_UNITS):
        if kind == "taps":
            first = KU * tap_part(j)
            put(np.concatenate([diagonal(a["l1_dw_2"][t, n * P:n * P + P]) for t in range(first, first + KU)], 0))
        else:
            off = n * P + (D if kind == "gate" else 0)
            put(a["l1_pw1_2"][:, off:off + P])
    for n in range(KD):
        put(a["l1_pw2_2"][:, n * P:n * P + P])
    ffn(a["l1_ffn_up_2"], False, a["l1_ffn_down_2"])
    assert at[0] == UNITS
    return units.reshape(UNITS, P, KU, P)


def parameter_columns(a):
    columns = [a[name].reshape(n, P).T for name, n in VECTORS]
    columns.append(np.broadcast_to(a["swa_sinks"].reshape(1, 8), (P, 8)))
    columns += [a[name][0].reshape(2, P, HD).transpose(1, 0, 2).reshape(P, 2 * HD) for name in ("cmp_k_w2", "cmp_v_w2")]
    return np.concatenate(columns, 1)


def bias_rows(table):
    distance = T - P + np.arange(P)[:, None] - np.arange(T)[None, :]
    return np.ascontiguousarray(table[:, np.minimum(distance, MAX_REL) + MAX_REL])


def kernel(**inputs):
    import concourse.bacc as bacc
    from concourse.bass_utils import run_bass_kernel_spmd

    a = {name: np.ascontiguousarray(v) for name, v in inputs.items()}
    arrays = {"x": a["x"], "weights": weight_units(a), "params": np.ascontiguousarray(parameter_columns(a)),
              "lora": np.concatenate([a["l0_w2_2"], a["l0_a2_2"], a["l0_g2_2"]], 0),
              "table": bias_rows(a["l0_rel_bias_2"]),
              "dw": np.ascontiguousarray(a["l1_dw_2"].reshape(TAPS, KD, P).transpose(2, 1, 0))}
    nc = bacc.Bacc("TRN2", target_bir_lowering=False, num_devices=1)
    args = [nc.dram_tensor(n, v.shape, mybir.dt.from_np(v.dtype), kind="ExternalInput").ap() for n, v in arrays.items()]
    out = nc.dram_tensor("out", (1, T, D), F32, kind="ExternalOutput").ap()
    program(nc, *args, out)
    r = run_bass_kernel_spmd(nc, [arrays], core_ids=[0])
    return r.results[0]["out"]
```
